# Optimizing a Trainium2 kernel written in Bass

```python
import math
import jax, jax.numpy as jnp
from jax import lax
import numpy as np

D_MODEL = 1024
BATCH = 1
SEQ = 512
DEPTH = 1
DEC_BATCH = 8
DEC_SEQ = 16
PAST_LEN = 256

CHUNK = 64
Q_BLOCK = 128
ROPE_THETA = 10000.0
EPS = 1e-6
RET_HEADS = 4
RET_DK = D_MODEL // RET_HEADS
RET_DV = 2 * RET_DK
RET_W_QK = RET_HEADS * RET_DK
RET_W_V = RET_HEADS * RET_DV
DIFF_HEADS = 8
DIFF_DH = D_MODEL // (2 * DIFF_HEADS)
DIFF_DV = 2 * DIFF_DH
DIFF_W_QK = DIFF_HEADS * 2 * DIFF_DH
DIFF_W_V = DIFF_HEADS * DIFF_DV
N_BRANCHES = 2
IN_COLS = 2 * RET_W_QK + 2 * RET_W_V + 2 * DIFF_W_QK + DIFF_W_V + N_BRANCHES * D_MODEL
N_GROUPS = 4
EXPERTS_PER_GROUP = 4
N_EXPERTS = N_GROUPS * EXPERTS_PER_GROUP
TOP_K = 2
D_EXPERT = 512

kernel_name = 'hybrid_retention_diffattn_hmoe_stream_step'

def rms_norm(x, g=None):
    xf = x.astype(jnp.float32)
    y = xf * lax.rsqrt(jnp.mean(xf * xf, axis=-1, keepdims=True) + EPS)
    if g is not None:
        y = y * g.astype(jnp.float32)
    return y.astype(x.dtype)

def rope(x, pos):
    d = x.shape[-1]
    inv = ROPE_THETA ** (-jnp.arange(0, d, 2, dtype=jnp.float32) / d)
    ang = pos.astype(jnp.float32)[:, None] * inv[None, :]
    cos = jnp.cos(ang)[:, None, :]
    sin = jnp.sin(ang)[:, None, :]
    x1, x2 = jnp.split(x.astype(jnp.float32), 2, axis=-1)
    return jnp.concatenate([x1 * cos - x2 * sin, x1 * sin + x2 * cos], axis=-1).astype(x.dtype)

def retention_log_gamma():
    return jnp.log1p(-jnp.exp2(-5.0 - jnp.arange(RET_HEADS, dtype=jnp.float32)))

def retention_block(q, k, v, s, log_gamma):
    L = q.shape[1]
    idx = jnp.arange(L, dtype=jnp.float32)
    rel = idx[:, None] - idx[None, :]
    decay = jnp.where(rel >= 0, jnp.exp(jnp.maximum(rel, 0.0)[None] * log_gamma[:, None, None]), 0.0)
    scores = jnp.einsum('blhd,bmhd->bhlm', q, k) * decay[None]
    intra = jnp.einsum('bhlm,bmhv->blhv', scores, v)
    q_decay = jnp.exp((idx + 1.0)[:, None] * log_gamma[None, :])
    cross = jnp.einsum('blhd,bhdv->blhv', q, s) * q_decay[None, :, :, None]
    k_decay = jnp.exp((L - 1.0 - idx)[:, None] * log_gamma[None, :])
    s_new = s * jnp.exp(L * log_gamma)[None, :, None, None] + jnp.einsum(
        'blhd,blhv->bhdv', k * k_decay[None, :, :, None], v)
    return intra + cross, s_new

def retention(q, k, v, s0, log_gamma):
    B, L = q.shape[0], q.shape[1]
    if L <= CHUNK:
        return retention_block(q, k, v, s0, log_gamma)
    nc = L // CHUNK

    def to_chunks(t):
        return t.reshape(B, nc, CHUNK, *t.shape[2:]).swapaxes(0, 1)

    def step(s, qkv):
        o, s_next = retention_block(qkv[0], qkv[1], qkv[2], s, log_gamma)
        return s_next, o

    s_fin, o = lax.scan(step, s0, (to_chunks(q), to_chunks(k), to_chunks(v)))
    return o.swapaxes(0, 1).reshape(B, L, *o.shape[3:]), s_fin

def diff_attend(q, k, v, q_pos, k_pos, lam):
    s = jnp.einsum('bqhcd,bkhcd->bhcqk', q, k).astype(jnp.float32) * (DIFF_DH ** -0.5)
    visible = (k_pos // CHUNK)[None, :] <= (q_pos // CHUNK)[:, None]
    s = jnp.where(visible, s, -1e30)
    p = jax.nn.softmax(s, axis=-1)
    a = p[:, :, 0] - lam * p[:, :, 1]
    return jnp.einsum('bhqk,bkhv->bqhv', a.astype(v.dtype), v)

def diff_attention(q, k, v, q_pos, k_pos, lam):
    B, L = q.shape[0], q.shape[1]
    if L <= Q_BLOCK:
        return diff_attend(q, k, v, q_pos, k_pos, lam)
    nb = L // Q_BLOCK
    qb = q.reshape(B, nb, Q_BLOCK, *q.shape[2:]).swapaxes(0, 1)
    pb = q_pos.reshape(nb, Q_BLOCK)
    ob = lax.map(lambda a: diff_attend(a[0], k, v, a[1], k_pos, lam), (qb, pb))
    return ob.swapaxes(0, 1).reshape(B, L, *ob.shape[3:])

def hierarchical_moe(h, w_group, b_group, w_expert_router, b_expert, w1, w3, w2):
    B, L, D = h.shape
    hf = h.reshape(B * L, D)
    g_logits = (hf @ w_group).astype(jnp.float32) + b_group.astype(jnp.float32)
    g_idx = jnp.argmax(g_logits, axis=-1)
    g_prob = jnp.take_along_axis(jax.nn.softmax(g_logits, axis=-1), g_idx[:, None], axis=-1)
    e_logits = ((hf @ w_expert_router).astype(jnp.float32) + b_expert.astype(jnp.float32)).reshape(
        -1, N_GROUPS, EXPERTS_PER_GROUP)
    e_in_group = jnp.take_along_axis(e_logits, g_idx[:, None, None], axis=1)[:, 0]
    top_v, top_i = lax.top_k(e_in_group, TOP_K)
    weights = jax.nn.softmax(top_v, axis=-1) * g_prob
    expert_id = g_idx[:, None] * EXPERTS_PER_GROUP + top_i
    combine = jnp.sum(jax.nn.one_hot(expert_id, N_EXPERTS, dtype=jnp.float32) * weights[..., None], axis=1)
    y = jnp.zeros_like(hf)
    for e in range(N_EXPERTS):
        ff = (jax.nn.silu(hf @ w1[e]) * (hf @ w3[e])) @ w2[e]
        y = y + combine[:, e:e + 1].astype(hf.dtype) * ff
    return y.reshape(B, L, D)

def layer(x, c, pos, ret_state, k_past, v_past, lw, li):
    B, L, _ = x.shape
    mod = jax.nn.silu(c) @ lw['w_ada'] + lw['b_ada']
    sh1, sc1, gt1, sh2, sc2, gt2 = jnp.split(mod[:, None, :], 6, axis=-1)
    h = rms_norm(x, lw['norm1_g']) * (1.0 + sc1) + sh1
    proj = h @ lw['w_in']
    sizes = [RET_W_QK, RET_W_QK, RET_W_V, RET_W_V, DIFF_W_QK, DIFF_W_QK, DIFF_W_V]
    split_at = [int(i) for i in np.cumsum(sizes)]
    rq, rk, rv, rg, dq, dk, dv, gates = jnp.split(proj, split_at, axis=-1)

    rq = rope(rq.reshape(B, L, RET_HEADS, RET_DK), pos).astype(jnp.float32)
    rk = rope(rk.reshape(B, L, RET_HEADS, RET_DK), pos).astype(jnp.float32) * (RET_DK ** -0.5)
    rv = rv.reshape(B, L, RET_HEADS, RET_DV).astype(jnp.float32)
    ret_o, ret_state_new = retention(rq, rk, rv, ret_state.astype(jnp.float32), retention_log_gamma())
    ret_o = rms_norm(ret_o).reshape(B, L, RET_W_V).astype(x.dtype) * jax.nn.silu(rg)

    dq = rope(rms_norm(dq.reshape(B, L, 2 * DIFF_HEADS, DIFF_DH), lw['diff_qnorm_g']), pos)
    dk = rope(rms_norm(dk.reshape(B, L, 2 * DIFF_HEADS, DIFF_DH), lw['diff_knorm_g']), pos)
    k_rows = dk.reshape(B, L, DIFF_HEADS, 2 * DIFF_DH)
    v_rows = dv.reshape(B, L, DIFF_HEADS, DIFF_DV)
    if k_past is None:
        k_all, v_all, k_pos = k_rows, v_rows, pos
    else:
        k_all = jnp.concatenate([k_past.astype(k_rows.dtype), k_rows], axis=1)
        v_all = jnp.concatenate([v_past.astype(v_rows.dtype), v_rows], axis=1)
        k_pos = jnp.arange(k_all.shape[1], dtype=jnp.int32)
    lam_init = 0.8 - 0.6 * math.exp(-0.3 * li)
    lam = (jnp.exp(jnp.sum(lw['diff_lambda_q1'] * lw['diff_lambda_k1']))
           - jnp.exp(jnp.sum(lw['diff_lambda_q2'] * lw['diff_lambda_k2'])) + lam_init).astype(jnp.float32)
    diff_o = diff_attention(dq.reshape(B, L, DIFF_HEADS, 2, DIFF_DH),
                            k_all.reshape(B, -1, DIFF_HEADS, 2, DIFF_DH), v_all, pos, k_pos, lam)
    diff_o = (rms_norm(diff_o, lw['diff_subln_g']) * (1.0 - lam_init)).reshape(B, L, DIFF_W_V)

    gate_ret, gate_diff = jnp.split(jax.nn.sigmoid(gates), 2, axis=-1)
    merged = gate_ret * (ret_o @ lw['w_br_ret']) + gate_diff * (diff_o @ lw['w_br_diff'])
    x = x + gt1 * (merged @ lw['w_out'])

    h2 = rms_norm(x, lw['norm2_g']) * (1.0 + sc2) + sh2
    x = x + gt2 * hierarchical_moe(h2, lw['w_group'], lw['b_group'], lw['w_expert_router'],
                                   lw['b_expert'], lw['w1'], lw['w3'], lw['w2'])
    return x, ret_state_new, k_rows, v_rows

def setup_inputs(seed: int = 0) -> dict:
    key = jax.random.key(seed)
    ks = jax.random.split(key, 32)
    f32 = jnp.float32
    D = D_MODEL

    def nrm(k, shape, scale):
        return jax.random.normal(k, shape, f32) * scale

    return {
        'x_prompt': nrm(ks[0], (BATCH, SEQ, D), 1.0),
        'x_sample': nrm(ks[1], (DEC_BATCH, DEC_SEQ, D), 1.0),
        'c_prompt': nrm(ks[2], (BATCH, D), 1.0),
        'c_sample': nrm(ks[3], (DEC_BATCH, D), 1.0),
        'cache_diff_k': nrm(ks[4], (DEPTH, DEC_BATCH, PAST_LEN, DIFF_HEADS, 2 * DIFF_DH), 1.0),
        'cache_diff_v': nrm(ks[5], (DEPTH, DEC_BATCH, PAST_LEN, DIFF_HEADS, DIFF_DV), 1.0),
        'state_ret': nrm(ks[6], (DEPTH, DEC_BATCH, RET_HEADS, RET_DK, RET_DV), 0.5),
        'w_ada': nrm(ks[7], (DEPTH, D, 6 * D), 0.5 * D ** -0.5),
        'b_ada': nrm(ks[8], (DEPTH, 6 * D), 0.01),
        'norm1_g': 1.0 + nrm(ks[9], (DEPTH, D), 0.01),
        'w_in': nrm(ks[10], (DEPTH, D, IN_COLS), D ** -0.5),
        'diff_qnorm_g': 1.0 + nrm(ks[11], (DEPTH, DIFF_DH), 0.01),
        'diff_knorm_g': 1.0 + nrm(ks[12], (DEPTH, DIFF_DH), 0.01),
        'diff_lambda_q1': nrm(ks[13], (DEPTH, DIFF_DH), 0.1),
        'diff_lambda_k1': nrm(ks[14], (DEPTH, DIFF_DH), 0.1),
        'diff_lambda_q2': nrm(ks[15], (DEPTH, DIFF_DH), 0.1),
        'diff_lambda_k2': nrm(ks[16], (DEPTH, DIFF_DH), 0.1),
        'diff_subln_g': 1.0 + nrm(ks[17], (DEPTH, DIFF_DV), 0.01),
        'w_br_ret': nrm(ks[18], (DEPTH, RET_W_V, D), RET_W_V ** -0.5),
        'w_br_diff': nrm(ks[19], (DEPTH, DIFF_W_V, D), DIFF_W_V ** -0.5),
        'w_out': nrm(ks[20], (DEPTH, D, D), D ** -0.5),
        'norm2_g': 1.0 + nrm(ks[21], (DEPTH, D), 0.01),
        'w_group': nrm(ks[22], (DEPTH, D, N_GROUPS), D ** -0.5),
        'b_group': nrm(ks[23], (DEPTH, N_GROUPS), 0.01),
        'w_expert_router': nrm(ks[24], (DEPTH, D, N_EXPERTS), D ** -0.5),
        'b_expert': nrm(ks[25], (DEPTH, N_EXPERTS), 0.01),
        'w1': nrm(ks[26], (DEPTH, N_EXPERTS, D, D_EXPERT), D ** -0.5),
        'w3': nrm(ks[27], (DEPTH, N_EXPERTS, D, D_EXPERT), D ** -0.5),
        'w2': nrm(ks[28], (DEPTH, N_EXPERTS, D_EXPERT, D), D_EXPERT ** -0.5),
    }

def reference(x_prompt, x_sample, c_prompt, c_sample, cache_diff_k, cache_diff_v, state_ret,
              w_ada, b_ada, norm1_g, w_in, diff_qnorm_g, diff_knorm_g, diff_lambda_q1, diff_lambda_k1,
              diff_lambda_q2, diff_lambda_k2, diff_subln_g, w_br_ret, w_br_diff, w_out, norm2_g,
              w_group, b_group, w_expert_router, b_expert, w1, w3, w2):
    B, S, _ = x_prompt.shape
    Ls = x_sample.shape[1]
    past = cache_diff_k.shape[2]
    pos_p = jnp.arange(S, dtype=jnp.int32)
    pos_s = past + jnp.arange(Ls, dtype=jnp.int32)
    xp, xs = x_prompt, x_sample
    kp_l, vp_l, sp_l, ks_l, vs_l, ss_l = [], [], [], [], [], []
    for li in range(DEPTH):
        lw = {
            'w_ada': w_ada[li], 'b_ada': b_ada[li], 'norm1_g': norm1_g[li], 'w_in': w_in[li],
            'diff_qnorm_g': diff_qnorm_g[li], 'diff_knorm_g': diff_knorm_g[li],
            'diff_lambda_q1': diff_lambda_q1[li], 'diff_lambda_k1': diff_lambda_k1[li],
            'diff_lambda_q2': diff_lambda_q2[li], 'diff_lambda_k2': diff_lambda_k2[li],
            'diff_subln_g': diff_subln_g[li], 'w_br_ret': w_br_ret[li], 'w_br_diff': w_br_diff[li],
            'w_out': w_out[li], 'norm2_g': norm2_g[li], 'w_group': w_group[li], 'b_group': b_group[li],
            'w_expert_router': w_expert_router[li], 'b_expert': b_expert[li],
            'w1': w1[li], 'w3': w3[li], 'w2': w2[li],
        }
        s0 = jnp.zeros((B, RET_HEADS, RET_DK, RET_DV), jnp.float32)
        xp, sp, kp, vp = layer(xp, c_prompt, pos_p, s0, None, None, lw, li)
        xs, ss, kss, vss = layer(xs, c_sample, pos_s, state_ret[li], cache_diff_k[li], cache_diff_v[li], lw, li)
        kp_l.append(kp)
        vp_l.append(vp)
        sp_l.append(sp)
        ks_l.append(kss)
        vs_l.append(vss)
        ss_l.append(ss)
    return (xp, xs, jnp.stack(kp_l), jnp.stack(vp_l), jnp.stack(sp_l).astype(x_prompt.dtype),
            jnp.stack(ks_l), jnp.stack(vs_l), jnp.stack(ss_l).astype(state_ret.dtype))


_drawn_inputs = setup_inputs


def setup_inputs(seed=0):
    import zlib

    import numpy as np

    out = dict(_drawn_inputs(seed))
    spreads = {}
    factors = {'norm1_g': 5.377,
     'diff_qnorm_g': 8.0,
     'diff_knorm_g': 6.245,
     'diff_lambda_q1': 5.72,
     'diff_lambda_k1': 6.853,
     'diff_lambda_q2': 5.674,
     'diff_lambda_k2': 6.598,
     'diff_subln_g': 8.0,
     'norm2_g': 5.564,
     'b_group': 8.0,
     'b_expert': 8.0}
    for name, (base, spread) in spreads.items():
        noise = np.random.default_rng([zlib.crc32(name.encode()), seed]).standard_normal(out[name].shape)
        drawn = base * np.exp(spread * noise) if base else spread * noise
        out[name] = __import__('jax').numpy.asarray(drawn.astype(out[name].dtype))
    for name, factor in factors.items():
        out[name] = (out[name] * factor).astype(out[name].dtype)
    return out
```

```python
import math
from contextlib import ExitStack

import numpy as np

import concourse.bass as bass
from concourse import mybir

F32 = mybir.dt.float32
F32R = mybir.dt.float32r
I32 = mybir.dt.int32
U32 = mybir.dt.uint32
ALU = mybir.AluOpType
ACT = mybir.ActivationFunctionType
AX = mybir.AxisListType.X

P = 128
D_MODEL = 1024
SEQ = 512
DEC_B = 8
DEC_L = 16
PAST = 256
CHUNK = 64
EPS = 1e-6
NT = (SEQ + DEC_B * DEC_L) // P
NP_T = SEQ // P
KT = D_MODEL // P
RH, RDK, RDV = 4, 256, 512
DH, DDH, DDV = 8, 64, 128
LAM_INIT = 0.8 - 0.6 * math.exp(0.0)
N_EXP = 16
D_EXP = 512
CAP = P
IN_COLS = 11264
COL_RQ, COL_RK, COL_RV, COL_RG = 0, 1024, 2048, 4096
COL_DQ, COL_DK, COL_DV, COL_GATE = 6144, 7168, 8192, 9216
W = 512
NEG = -1e30

T_DEC, T_SMP, T_KDEC, T_KMASK, T_QDEC = 0, 512, 640, 644, 652
T_RET = 780


class Map:

    def __init__(self, nc, start, end):
        self.nc, self.at, self.end = nc, start, end

    def __call__(self, name, shape, dt, at=None):
        size = int(np.prod(shape[1:])) * 4
        off = self.at if at is None else at
        t = self.nc.alloc_sbuf_tensor_at(name, shape, dt, offset=off)
        if at is None:
            self.at += (size + 31) // 32 * 32
            assert self.at <= self.end, (name, self.at, self.end)
        return t


class Links:

    def __init__(self, eng, sem, base=0):
        self.eng, self.sem, self.base, self.n = eng, sem, base, 0

    def __call__(self, ins):
        self.n += 1
        ins.then_inc(self.sem, 1)

    def sync(self):
        self.eng.wait_ge(self.sem, self.base + self.n)


def mm3(pe, out, s_hi, s_lo, m_hi, m_lo, start, stop):
    pe.matmul(out, s_hi, m_hi, start=start, stop=False)
    pe.matmul(out, s_hi, m_lo, start=False, stop=False)
    return pe.matmul(out, s_lo, m_hi, start=False, stop=stop)


class Weights:

    def __init__(self, nc, ctx, sb):
        self.raw = sb("w_raw", [P, 4, 2, W], F32)
        self.hi = sb("w_hi", [P, 4, 2, W], F32R)
        self.lo = sb("w_lo", [P, 4, 2, W], F32R)
        four = lambda name: [ctx.enter_context(nc.semaphore(f"{name}{p}")) for p in range(4)]
        self.loaded, self.hi_done, self.lo_done, self.used = map(four, ("w_loaded", "w_hi_done", "w_lo_done", "w_used"))

    def load(self, sp, n, pairs):
        for p, src in enumerate(pairs):
            sp.wait_ge(self.lo_done[p], n)
            sp.dma_start(self.raw[:, p], src).then_inc(self.loaded[p], 16)

    def split_hi(self, act, n, p, free):
        act.wait_ge(self.loaded[p], n * 16 + 16)
        act.wait_ge(*free)
        act.activation(self.hi[:, p], self.raw[:, p], ACT.Copy).then_inc(self.hi_done[p], 1)

    def split_lo(self, eng, n, p):
        eng.wait_ge(self.hi_done[p], n + 1)
        eng.tensor_tensor(self.lo[:, p], self.raw[:, p], self.hi[:, p].bitcast(F32), ALU.subtract) \
           .then_inc(self.lo_done[p], 1)


def rows_of(w, c0):
    return [w[p * 256:(p + 1) * 256, bass.ds(c0, W)].rearrange("(k r) n -> r k n", k=2) for p in range(4)]


def halves_of(w, r0):
    return [w[bass.ds(r0 + q * 256, 256), j * W:(j + 1) * W].rearrange("(k r) n -> r k n", k=2)
            for j in range(2) for q in range(2)]


def project(pe, wts, n, banks, stat_hi, stat_lo, bank_free, group, done, tiles=NT, between=None):
    for p in range(4):
        if p == 3 and between:
            between()
        pe.wait_ge(wts.lo_done[p], n + 1)
        for kk in range(2):
            k = 2 * p + kk
            for t in range(tiles):
                if k == 0:
                    pe.wait_ge(bank_free[t], group)
                s = slice(t * P, (t + 1) * P)
                last = mm3(pe, banks[t][:], stat_hi[:, k, s], stat_lo[:, k, s], wts.hi[:, p, kk], wts.lo[:, p, kk],
                           k == 0, k == KT - 1)
                if k == KT - 1:
                    last.then_inc(done, 1)
        if p < 3:
            last.then_inc(wts.used[p], 1)


def bc(ap, shape):
    return ap.broadcast_to(shape)


def rsqrt_steps(dve, links, out, var, std, tmp):
    links(dve.reciprocal(out, std))
    links.sync()
    links(dve.tensor_tensor(tmp, out, out, ALU.mult))
    links.sync()
    links(dve.tensor_tensor(tmp, tmp, var, ALU.mult))
    links.sync()
    links(dve.tensor_scalar(tmp, tmp, -0.5, 1.5, ALU.mult, ALU.add))
    links.sync()
    links(dve.tensor_tensor(out, out, tmp, ALU.mult))
    links.sync()


def phase_a(nc, io, K):
    wts = K.wts
    NCH = 12
    KEEP = 4
    with ExitStack() as ctx:
        sb = Map(nc, K.phase_base, K.sbuf_end)
        sem = lambda name: K.semaphore("a_" + name)
        x = sb("a_x", [P, NT, D_MODEL], F32)
        sq = sb("a_sq", [P, D_MODEL], F32)
        c9 = sb("a_c9", [9, D_MODEL], F32)
        c9s = sb("a_c9s", [9, D_MODEL], F32)
        cS = sb("a_cS", [P, KT, P], F32R)
        mod = sb("a_mod", [19, 6 * D_MODEL], F32)
        sel = sb("a_sel", [19, 2, P], F32)
        g = sb("a_g", [P, 2, D_MODEL], F32)
        m1 = sb("a_m1", [P, 2, 2, D_MODEL], F32)
        m2 = sb("a_m2", [P, 2, 4, D_MODEL], F32)
        st = sb("a_st", [P, 5, 8], F32)
        ps = [ctx.enter_context(nc.psum_tensor(f"a_ps{i}", [P, W], F32)) for i in range(8)]
        s_x, s_c, s_small = sem("x_in"), sem("c_in"), sem("small_in")
        silu_done, zero_done, cT_done, cT_hi, cT_split = map(sem, ("silu_done", "zero_done", "cT_done", "cT_hi", "cT_split"))
        mod_done, mod_copied, sel_done, sel_taken = map(sem, ("mod_done", "mod_copied", "sel_done", "sel_taken"))
        sumsq, var_done, std_done, h_done, hT_done, hi_done, lo_done = map(
            sem, ("sumsq", "var_done", "std_done", "h_done", "hT_done", "hT_hi_done", "hT_lo_done"))
        link, m_out = sem("dve_link"), sem("mods_out")
        block = ctx.enter_context(nc.Block())

        def kind(t):
            return 0 if t < NP_T else 1

        @block.sync
        def _(sp):
            sp.dma_start(c9[0:1], io["c_prompt"]).then_inc(s_c, 16)
            sp.dma_start(c9[1:9], io["c_sample"]).then_inc(s_c, 16)
            sp.dma_start(K.ident[:], io["ident"]).then_inc(s_small, 16)
            sp.dma_start(sel[:], io["sel"]).then_inc(s_small, 16)
            sp.dma_start(K.g16[:], io["g16"]).then_inc(s_small, 16)
            sp.dma_start(mod[18:19], io["b_ada"]).then_inc(s_small, 16)
            for i, name in enumerate(("norm1_g", "norm2_g")):
                sp.dma_start(g[:, i], io[name].broadcast_to([P, D_MODEL])) \
                  .then_inc(s_small, 16)
            for n in range(NCH):
                wts.load(sp, n, rows_of(io["w_ada"][0], n * W))
                if n == 1:
                    sp.dma_start(x[:, 0:NP_T], io["x_prompt"][0].rearrange("(t p) d -> p t d", p=P)).then_inc(s_x, 16)
                    sp.dma_start(x[:, NP_T], io["x_sample"].rearrange("b l d -> (b l) d")).then_inc(s_x, 16)
            sp.wait_ge(sel_taken, NCH * 2)
            sp.dma_start(io["mods"].rearrange("k m p d -> p k m d"), m2[:]).then_inc(m_out, 16)
            sp.wait_ge(m_out, 16)

        @block.gpsimd
        def _(pool):
            for n in range(NCH):
                for p in (1, 3):
                    wts.split_lo(pool, n, p)

        def copy_hT(q):
            act = nc.scalar
            act.wait_ge(hT_done, q + 1)
            t, half = q // 2, q % 2
            act.activation(K.hT_hi[:, 4 * half:4 * half + 4, t * P:(t + 1) * P],
                           ps[6 + q % 2][:].rearrange("p (k c) -> p k c", c=P), ACT.Copy).then_inc(hi_done, 1)

        @block.scalar
        def _(act):
            act.wait_ge(s_c, 32)
            act.activation(c9s[:], c9[:], ACT.Silu).then_inc(silu_done, 1)
            act.wait_ge(cT_done, 1)
            act.wait_ge(zero_done, 1)
            act.activation(cS[:, :, 0:9], ps[7][:, 0:72].rearrange("p (k c) -> p k c", c=9), ACT.Copy).then_inc(cT_hi, 1)

            def take_mod(n):
                act.wait_ge(mod_done, n + 1)
                act.activation(mod[0:18, n * W:(n + 1) * W], ps[n % 2][0:18], ACT.Copy).then_inc(mod_copied, 1)

            for n in range(NCH):
                wts.split_hi(act, n, 0, (wts.used[0], n))
                wts.split_hi(act, n, 1, (wts.used[1], n))
                if n:
                    take_mod(n - 1)
                wts.split_hi(act, n, 2, (wts.used[2], n))
                wts.split_hi(act, n, 3, (mod_done, n))
                if n == 3:
                    act.wait_ge(s_x, 32)
                    for t in range(NT):
                        if t:
                            act.wait_ge(sumsq, t)
                        act.activation(sq[:], x[:, t], ACT.Square, accum_out=st[:, 0, t:t + 1]).then_inc(sumsq, 1)
                if n == 4:
                    act.wait_ge(var_done, 1)
                    act.activation(st[:, 2, 0:NT], st[:, 1, 0:NT], ACT.Sqrt).then_inc(std_done, 1)
                if n >= 8:
                    for q in range(2 * (n - 8), 2 * (n - 8) + 2):
                        copy_hT(q)
            take_mod(NCH - 1)
            for q in (8, 9):
                copy_hT(q)

        @block.vector
        def _(dve):
            links = Links(dve, link)
            dve.memset(cS[:].bitcast(F32), 0.0).then_inc(zero_done, 1)

            def take_sel(n):
                seg, half = n // 2, n % 2
                cols = slice(half * W, (half + 1) * W)
                for kd in range(2):
                    dve.wait_ge(sel_done, 2 * n + kd + 1)
                    dst = m1[:, kd, seg, cols] if seg < 2 else m2[:, kd, seg - 2, cols]
                    src = ps[2 + (n % 2) * 2 + kd][:]
                    if seg in (1, 4):
                        ins = dve.scalar_tensor_tensor(dst, src, 1.0, g[:, 0 if seg == 1 else 1, cols], ALU.add, ALU.mult)
                    else:
                        ins = dve.tensor_copy(dst, src)
                    ins.then_inc(sel_taken, 1)

            def split_hT(q):
                dve.wait_ge(hi_done, q + 1)
                t, half = q // 2, q % 2
                s = (slice(None), slice(4 * half, 4 * half + 4), slice(t * P, (t + 1) * P))
                dve.tensor_tensor(K.hT_lo[s], ps[6 + q % 2][:].rearrange("p (k c) -> p k c", c=P),
                                  K.hT_hi[s].bitcast(F32), ALU.subtract).then_inc(lo_done, 1)

            def norm(t):
                if t == 0:
                    dve.wait_ge(std_done, 1)
                    rsqrt_steps(dve, links, st[:, 3, 0:NT], st[:, 1, 0:NT], st[:, 2, 0:NT], st[:, 4, 0:NT])
                    dve.wait_ge(sel_taken, 2 * KEEP)
                links(dve.scalar_tensor_tensor(x[:, t], x[:, t], st[:, 3, t:t + 1], m1[:, kind(t), 1], ALU.mult, ALU.mult))
                links.sync()
                dve.tensor_tensor(x[:, t], x[:, t], m1[:, kind(t), 0], ALU.add).then_inc(h_done, 1)

            for n in range(NCH):
                if n == 0:
                    dve.wait_ge(cT_hi, 1)
                    dve.tensor_tensor(cS[:, :, 9:18], ps[7][:, 0:72].rearrange("p (k c) -> p k c", c=9),
                                      cS[:, :, 0:9].bitcast(F32), ALU.subtract).then_inc(cT_split, 1)
                    dve.wait_ge(s_small, 6 * 16)
                wts.split_lo(dve, n, 0)
                wts.split_lo(dve, n, 2)
                if n:
                    take_sel(n - 1)
                if n == 3:
                    dve.wait_ge(sumsq, NT)
                    dve.tensor_scalar(st[:, 1, 0:NT], st[:, 0, 0:NT], 1.0 / D_MODEL, EPS, ALU.mult, ALU.add).then_inc(var_done, 1)
                if 5 <= n < 5 + NT:
                    norm(n - 5)
                if n >= 8:
                    for q in range(2 * (n - 8), 2 * (n - 8) + 2):
                        split_hT(q)
            take_sel(NCH - 1)
            for q in (8, 9):
                split_hT(q)

        @block.tensor
        def _(pe):
            pe.wait_ge(s_small, 6 * 16)
            pe.wait_ge(silu_done, 1)
            for k in range(KT):
                last = pe.transpose(ps[7][:, 9 * k:9 * k + 9], c9s[:, k * P:(k + 1) * P], K.ident[0:9, 0:9])
            last.then_inc(cT_done, 1)
            pe.wait_ge(cT_split, 1)
            def spread(m):
                pe.wait_ge(mod_copied, m + 1)
                if m >= 2:
                    pe.wait_ge(sel_taken, 2 * (m - 1))
                for kd in range(2):
                    pe.matmul(ps[2 + (m % 2) * 2 + kd][:], sel[:, kd], mod[:, m * W:(m + 1) * W],
                              start=True, stop=True).then_inc(sel_done, 1)

            for n in range(NCH + 1):
                if n < NCH:
                    for p in range(4):
                        if n and p == 2:
                            spread(n - 1)
                        pe.wait_ge(wts.lo_done[p], n + 1)
                        if p == 0 and n >= 2:
                            pe.wait_ge(mod_copied, n - 1)
                        for kk in range(2):
                            k = 2 * p + kk
                            pe.matmul(ps[n % 2][:], cS[:, k, :], wts.hi[:, p, kk], start=(k == 0), stop=False)
                            last = pe.matmul(ps[n % 2][:], cS[:, k, :], wts.lo[:, p, kk], start=False, stop=(k == KT - 1))
                        if p < 3:
                            last.then_inc(wts.used[p], 1)
                    last.then_inc(mod_done, 1)
                else:
                    spread(NCH - 1)
                if 7 <= n < 7 + NT:
                    t = n - 7
                    pe.wait_ge(h_done, t + 1)
                    for half in range(2):
                        q = 2 * t + half
                        if q >= 2:
                            pe.wait_ge(lo_done, q - 1)
                        for j in range(4):
                            k = 4 * half + j
                            last = pe.transpose(ps[6 + q % 2][:, j * P:(j + 1) * P], x[:, t, k * P:(k + 1) * P], K.ident[:])
                        last.then_inc(hT_done, 1)


def phase_r(nc, io, K):
    wts = K.wts
    N0 = 12
    G = 6
    J = 33
    J_T, J_SC, J_ST, J_UP, J_OT = 0, 5, 10, 12, 28
    UN = 2 * DEC_B
    SLOTS = 4
    NLINK = 20
    scoff = [0, 512, 896, 1152, 1280]
    with ExitStack() as ctx:
        sb = Map(nc, K.phase_base, K.sbuf_end)
        sem = lambda name: K.semaphore("r_" + name)
        K.acc_ret = sb("acc_ret", [P, NT, D_MODEL], F32)
        K.after_acc_ret = sb.at
        rope = sb("r_rope", [P, NT, 2, P], F32)
        tab = sb("r_tab", [P, T_RET], F32)
        qk = sb("r_qk", [P, NT, 2, RDK], F32)
        tmp = sb("r_tmp", [P, 2, W], F32)
        qkT = sb("r_qkT", [P, 4, NT * P], F32)
        v = sb("r_v", [P, NT, RDV], F32)
        gate = sb("r_gate", [P, NT, RDV], F32)
        scT = sb("r_scT", [P, 1280 + P], F32)
        oT_hi = sb("r_oT_hi", [P, 4, NT * P], F32R)
        oT_lo = sb("r_oT_lo", [P, 4, NT * P], F32R)
        qz = sb("r_qz", [P, DEC_B, P], F32)
        kz = sb("r_kz", [P, DEC_B, P], F32)
        S = sb("r_S", [P, SLOTS, RDV], F32)
        S_p = sb("r_S_p", [P, RDV], F32)
        S_sq = sb("r_squares", [P, RDV], F32)
        st = sb("r_st", [P, 5, 8], F32)
        pj = [ctx.enter_context(nc.psum_tensor(f"r_pj{i}", [P, W], F32)) for i in range(NT)]
        sm = [ctx.enter_context(nc.psum_tensor(f"r_sm{i}", [P, W], F32)) for i in range(3)]
        many = lambda name, n: [sem(f"{name}{i}") for i in range(n)]
        tab_in, rope_in, S_in, S_out, Sp_out = sem("tab_in"), sem("rope_in"), many("S_in", SLOTS), many("S_out", SLOTS), sem("Sp_out")
        xg_zero, acc_zero = sem("xg_zero"), sem("acc_zero")
        pj_done, pj_free, sm_done, sm_free = sem("pj_done"), many("pj_free", NT), sem("sm_done"), many("sm_free", 3)
        qk_roped, kd_done, z_done, qz_set = map(sem, ("qk_roped", "kd_done", "z_done", "qz_set"))
        sumsq, var_done, std_done, oT_hi_done, link = map(sem, ("sumsq", "var_done", "std_done", "oT_hi_done", "dve_link"))
        k_loaded = many("k_loaded", 4)
        block = ctx.enter_context(nc.Block())
        w_in = io["w_in"][0]

        def sm_bank(n):
            return sm[n % 3]

        def sm_taken(eng, h, job):
            eng.wait_ge(sm_free[job % 3], h * (J // 3) + job // 3 + 1)

        def pj_taken(eng, h, g, t):
            eng.wait_ge(pj_free[t], h * G + g + 1)

        @block.sync
        def _(sp):
            sp.dma_start(rope[:], io["rope_ret"]).then_inc(rope_in, 16)
            with sp.Fori(0, RH) as h:
                sp.wait_ge(sm_done, h * J)
                sp.dma_start(tab[:], io["tab_ret"][bass.ds(h, 1)].rearrange("a p c -> (a p) c")).then_inc(tab_in, 16)
                q_cols, k_cols = (w_in[:, bass.ds(h * RDK + c, RDK)].rearrange("(p k r) n -> p r k n", k=2, r=P)
                                  for c in (COL_RQ, COL_RK))
                for p in range(4):
                    sp.wait_ge(wts.lo_done[p], h * 4 + N0)
                    sp.dma_start(wts.raw[:, p, :, 0:RDK], q_cols[p]).then_inc(wts.loaded[p], 16)
                    sp.dma_start(wts.raw[:, p, :, RDK:W], k_cols[p]).then_inc(k_loaded[p], 16)
                wts.load(sp, h * 4 + N0 + 1, rows_of(w_in, h * RDV + COL_RV))
                wts.load(sp, h * 4 + N0 + 2, rows_of(w_in, h * RDV + COL_RG))
                wts.load(sp, h * 4 + N0 + 3, halves_of(io["w_br_ret"][0], h * RDV))
                for u in range(UN):
                    d, b = u // DEC_B, u % DEC_B
                    sp.wait_ge(S_out[u % SLOTS], h * (UN // SLOTS * 16) + 16 * (u // SLOTS))
                    sp.dma_start(S[:, u % SLOTS], io["state_ret"][0, b, bass.ds(h, 1), d * P:(d + 1) * P, :]
                                 .rearrange("a p c -> (a p) c")).then_inc(S_in[u % SLOTS], 16)

        @block.gpsimd
        def _(pool):
            pool.memset(qz[:], 0.0).then_inc(qz_set, 1)
            pool.wait_ge(qz_set, 1)
            with pool.Fori(0, RH) as h:
                for c in range(3):
                    for p in range(4):
                        wts.split_lo(pool, h * 4 + N0 + c, p)
                pool.wait_ge(tab_in, h * 16 + 16)
                pool.wait_ge(sm_done, h * J + J_T + NT)
                for t in range(NP_T):
                    pool.tensor_tensor(qk[:, t, 1], qk[:, t, 1], bc(tab[:, T_KDEC + t:T_KDEC + t + 1], [P, RDK]), ALU.mult) \
                        .then_inc(kd_done, 1)
                sm_taken(pool, h, J_T + NP_T)
                for d in range(2):
                    pool.wait_ge(sm_done, h * J + (J_UP + DEC_B) * d)
                    diag = qz[:].rearrange("p b c -> p (b c)")[:, 0:DEC_B * P]
                    diag = bass.AP(tensor=diag.tensor, offset=diag.offset, ap=[list(diag.ap[0]), [P + DEC_L, DEC_B], [1, DEC_L]])
                    pool.tensor_tensor(diag, qkT[:, d, NP_T * P:NT * P].rearrange("p (b l) -> p b l", l=DEC_L),
                                       tab[:, T_QDEC:T_QDEC + P].rearrange("p (b l) -> p b l", l=DEC_L), ALU.mult).then_inc(z_done, 1)
                    last = pool.tensor_tensor(kz[:], bc(qk[:, NP_T, 1, d * P:(d + 1) * P].unsqueeze(1), [P, DEC_B, P]),
                                              bc(tab[:, T_KMASK:T_KMASK + DEC_B].unsqueeze(2), [P, DEC_B, P]), ALU.mult)
                    last.then_inc(z_done, 1)
                for p in range(4):
                    wts.split_lo(pool, h * 4 + N0 + 3, p)

        @block.scalar
        def _(act):
            act.wait_ge(acc_zero, 1)
            for e in range(N_EXP + 1):
                act.dma_start(io["xg"][e * CAP:(e + 1) * CAP, :], K.acc_ret[:, 0]).then_inc(xg_zero, 16)
            with act.Fori(0, RH) as h:
                n = lambda c: h * 4 + N0 + c

                def hi(c, p):
                    if c == 0:
                        act.wait_ge(k_loaded[p], h * 16 + 16)
                    if p in (0, 2):
                        free = (wts.used[p], n(c))
                    elif p == 1 and c > 0:
                        free = (wts.used[1], h * 3 + N0 + c)
                    else:
                        free = (pj_done, h * (G * NT) + c * NT)
                    wts.split_hi(act, n(c), p, free)

                def take(g, dst, func):
                    for t in range(NT):
                        act.wait_ge(pj_done, h * (G * NT) + g * NT + t + 1)
                        act.activation(dst(t), pj[t][:], func).then_inc(pj_free[t], 1)

                def sums(ts):
                    for t in ts:
                        act.wait_ge(pj_done, h * (G * NT) + 3 * NT + t + 1)
                        act.wait_ge(sumsq, h * NT + t)
                        act.activation(S_sq[:], pj[t][:], ACT.Square, accum_out=st[:, 0, t:t + 1]).then_inc(sumsq, 1)

                def roots(a, b, i):
                    act.wait_ge(var_done, h * 2 + i + 1)
                    act.activation(st[:, 2, a:b], st[:, 1, a:b], ACT.Sqrt).then_inc(std_done, 1)

                for p in range(4):
                    hi(0, p)
                for p in range(3):
                    hi(1, p)
                take(0, lambda t: qk[:, t].rearrange("p a c -> p (a c)"), ACT.Copy)
                hi(1, 3)
                for p in range(3):
                    hi(2, p)
                take(1, lambda t: v[:, t], ACT.Copy)
                hi(2, 3)
                for p in range(3):
                    hi(3, p)
                take(2, lambda t: gate[:, t], ACT.Silu)
                hi(3, 3)
                sums(range(NP_T))
                roots(0, NP_T, 0)
                for d in range(2):
                    act.wait_ge(sm_done, h * J + J_ST + d + 1)
                    act.wait_ge(Sp_out, h * 32 + 16 * d)
                    act.activation(S_p[:], sm_bank(J_ST + d)[:], ACT.Copy).then_inc(sm_free[(J_ST + d) % 3], 1)
                    sm_taken(act, h, J_ST + d)
                    act.dma_start(io["o_state_p"][0, 0, bass.ds(h, 1), d * P:(d + 1) * P, :].rearrange("a p c -> (a p) c"),
                                  S_p[:]).then_inc(Sp_out, 16)
                for u in range(UN):
                    d, b = u // DEC_B, u % DEC_B
                    sm_taken(act, h, J_UP + u)
                    act.dma_start(io["o_state_s"][0, b, bass.ds(h, 1), d * P:(d + 1) * P, :].rearrange("a p c -> (a p) c"),
                                  S[:, u % SLOTS]).then_inc(S_out[u % SLOTS], 16)
                sums([NP_T])
                roots(NP_T, NT, 1)
                for t in range(NT):
                    act.wait_ge(sm_done, h * J + J_OT + t + 1)
                    act.activation(oT_hi[:, :, t * P:(t + 1) * P], sm_bank(J_OT + t)[:].rearrange("p (k c) -> p k c", c=P),
                                   ACT.Copy).then_inc(oT_hi_done, 1)
            act.wait_ge(Sp_out, RH * 32)
            for s in range(SLOTS):
                act.wait_ge(S_out[s], RH * (UN // SLOTS) * 16)

        @block.vector
        def _(dve):
            dve.memset(K.acc_ret[:], 0.0).then_inc(acc_zero, 1)
            dve.wait_ge(rope_in, 16)
            with dve.Fori(0, RH) as h:
                links = Links(dve, link, h * NLINK)
                for t in range(NT):
                    pj_taken(dve, h, 0, t)
                    x = qk[:, t].rearrange("p a (e c) -> p (a e) c", e=2)
                    cos = bc(rope[:, t, 0].unsqueeze(1), [P, 4, P])
                    sin = bc(rope[:, t, 1].unsqueeze(1), [P, 4, P])
                    t1 = tmp[:, 0].rearrange("p (a e c) -> p a e c", a=2, e=2)
                    t2 = tmp[:, 1].rearrange("p (a e c) -> p a e c", a=2, e=2)
                    xx = qk[:, t].rearrange("p a (e c) -> p a e c", e=2)
                    dve.wait_ge(qk_roped, h * NT + t)
                    links(dve.tensor_tensor(tmp[:, 0].rearrange("p (a c) -> p a c", a=4), x, cos, ALU.mult))
                    links(dve.tensor_tensor(tmp[:, 1].rearrange("p (a c) -> p a c", a=4), x, sin, ALU.mult))
                    links.sync()
                    dve.tensor_tensor(xx[:, :, 0], t1[:, :, 0], t2[:, :, 1], ALU.subtract)
                    dve.tensor_tensor(xx[:, :, 1], t1[:, :, 1], t2[:, :, 0], ALU.add).then_inc(qk_roped, 1)
                for t in range(NT):
                    dve.wait_ge(sm_done, h * J + J_T + t + 1)
                    dve.tensor_copy(qkT[:, :, t * P:(t + 1) * P], sm_bank(J_T + t)[:].rearrange("p (k c) -> p k c", c=P)) \
                       .then_inc(sm_free[(J_T + t) % 3], 1)
                dve.wait_ge(tab_in, h * 16 + 16)
                for j in range(NT):
                    n = scoff[j + 1] - scoff[j] if j < NP_T else P
                    c0 = T_DEC if j < NP_T else T_SMP
                    dve.wait_ge(sm_done, h * J + J_SC + j + 1)
                    dve.tensor_tensor(scT[:, scoff[j]:scoff[j] + n], sm_bank(J_SC + j)[:, 0:n], tab[:, c0:c0 + n], ALU.mult) \
                       .then_inc(sm_free[(J_SC + j) % 3], 1)

                def variance(a, b):
                    dve.wait_ge(sumsq, h * NT + b)
                    dve.tensor_scalar(st[:, 1, a:b], st[:, 0, a:b], 1.0 / RDV, EPS, ALU.mult, ALU.add).then_inc(var_done, 1)

                def gated(ts, i):
                    dve.wait_ge(std_done, h * 2 + i + 1)
                    a, b = ts[0], ts[-1] + 1
                    rsqrt_steps(dve, links, st[:, 3, a:b], st[:, 1, a:b], st[:, 2, a:b], st[:, 4, a:b])
                    for t in ts:
                        pj_taken(dve, h, 2, t)
                        dve.scalar_tensor_tensor(gate[:, t], pj[t][:], st[:, 3, t:t + 1], gate[:, t], ALU.mult, ALU.mult) \
                           .then_inc(pj_free[t], 1)

                variance(0, NP_T)
                gated(list(range(NP_T)), 0)
                for u in range(UN):
                    dve.wait_ge(sm_done, h * J + J_UP + u + 1)
                    dve.scalar_tensor_tensor(S[:, u % SLOTS], S[:, u % SLOTS], K.g16[:, bass.ds(h, 1)], sm_bank(J_UP + u)[:],
                                             ALU.mult, ALU.add).then_inc(sm_free[(J_UP + u) % 3], 1)
                variance(NP_T, NT)
                gated([NP_T], 1)
                for t in range(NT):
                    dve.wait_ge(oT_hi_done, h * NT + t + 1)
                    s = (slice(None), slice(None), slice(t * P, (t + 1) * P))
                    dve.tensor_tensor(oT_lo[s], sm_bank(J_OT + t)[:].rearrange("p (k c) -> p k c", c=P),
                                      oT_hi[s].bitcast(F32), ALU.subtract).then_inc(sm_free[(J_OT + t) % 3], 1)
                dve.wait_ge(acc_zero, 1)
                dve.wait_ge(xg_zero, 16 * (N_EXP + 1))
                for j in range(2):
                    for t in range(NT):
                        dve.wait_ge(pj_done, h * (G * NT) + (4 + j) * NT + t + 1)
                        a = K.acc_ret[:, t, j * W:(j + 1) * W]
                        dve.tensor_tensor(a, a, pj[t][:], ALU.add).then_inc(pj_free[t], 1)
                assert links.n == NLINK, links.n

        @block.tensor
        def _(pe):
            with pe.Fori(0, RH) as h:
                n = lambda c: h * 4 + N0 + c
                group = lambda g: h * G + g

                def small(job):
                    pe.wait_ge(sm_free[job % 3], h * (J // 3) + job // 3)
                    return sm_bank(job)

                hT = (K.hT_hi, K.hT_lo)
                project(pe, wts, n(0), pj, *hT, pj_free, group(0), pj_done)
                project(pe, wts, n(1), pj, *hT, pj_free, group(1), pj_done)
                for t in range(NT):
                    pe.wait_ge(qk_roped, h * NT + t + 1)
                    out = small(J_T + t)
                    for a in range(4):
                        last = pe.transpose(out[:, a * P:(a + 1) * P], qk[:, t, a // 2, (a % 2) * P:(a % 2 + 1) * P], K.ident[:])
                    last.then_inc(sm_done, 1)
                project(pe, wts, n(2), pj, *hT, pj_free, group(2), pj_done)
                for t in (2, 3, 4):
                    sm_taken(pe, h, J_T + t)
                for j in range(NT):
                    out = small(J_SC + j)
                    ke = slice(j * P, (j + 1) * P)
                    qs = slice(j * P, SEQ) if j < NP_T else ke
                    w = qs.stop - qs.start
                    for d in range(2):
                        last = pe.matmul(out[:, 0:w], qkT[:, 2 + d, ke], qkT[:, d, qs], start=(d == 0), stop=(d == 1))
                    last.then_inc(sm_done, 1)
                for i in range(NP_T):
                    pe.wait_ge(pj_free[i], group(3))
                    for j in range(i + 1):
                        pj_taken(pe, h, 1, j)
                        sm_taken(pe, h, J_SC + j)
                        c = scoff[j] + (i - j) * P
                        last = pe.matmul(pj[i][:], scT[:, c:c + P], v[:, j], start=(j == 0), stop=(j == i))
                    last.then_inc(pj_done, 1)
                pe.wait_ge(kd_done, h * NP_T + NP_T)
                for d in range(2):
                    out = small(J_ST + d)
                    for t in range(NP_T):
                        last = pe.matmul(out[:], qk[:, t, 1, d * P:(d + 1) * P], v[:, t], start=(t == 0), stop=(t == NP_T - 1))
                    last.then_inc(sm_done, 1)
                pe.wait_ge(pj_free[NP_T], group(3))
                pj_taken(pe, h, 1, NP_T)
                sm_taken(pe, h, J_SC + NP_T)
                pe.matmul(pj[NP_T][:], scT[:, scoff[4]:scoff[4] + P], v[:, NP_T], start=True, stop=False)
                for u in range(UN):
                    d, b = u // DEC_B, u % DEC_B
                    if b == 0:
                        pe.wait_ge(z_done, h * 4 + 2 * d + 2)
                    pe.wait_ge(S_in[u % SLOTS], h * (UN // SLOTS * 16) + 16 * (u // SLOTS) + 16)
                    o = pe.matmul(pj[NP_T][:], qz[:, b], S[:, u % SLOTS], start=False, stop=(u == UN - 1))
                    if u == UN - 1:
                        o.then_inc(pj_done, 1)
                    out = small(J_UP + u)
                    last = pe.matmul(out[:], kz[:, b], v[:, NP_T], start=True, stop=True)
                    last.then_inc(sm_done, 1)
                for t in range(NT):
                    pj_taken(pe, h, 3, t)
                    out = small(J_OT + t)
                    for a in range(4):
                        last = pe.transpose(out[:, a * P:(a + 1) * P], gate[:, t, a * P:(a + 1) * P], K.ident[:])
                    last.then_inc(sm_done, 1)
                branch(pe, wts, n(3), pj, oT_hi, oT_lo, lambda t: sm_taken(pe, h, J_OT + t), pj_free, group(4), pj_done)


def branch(pe, wts, n, banks, hi, lo, stands, bank_free, group, done):
    for j in range(2):
        for p in (2 * j, 2 * j + 1):
            pe.wait_ge(wts.lo_done[p], n + 1)
            for kk in range(2):
                k = 2 * (p % 2) + kk
                for t in range(NT):
                    if k == 0:
                        pe.wait_ge(bank_free[t], group + j)
                        stands(t)
                    s = slice(t * P, (t + 1) * P)
                    last = mm3(pe, banks[t][:], hi[:, k, s], lo[:, k, s], wts.hi[:, p, kk], wts.lo[:, p, kk], k == 0, k == 3)
                    if k == 3:
                        last.then_inc(done, 1)
            if k == 1:
                last.then_inc(wts.used[p], 1)


def phase_d(nc, io, K):
    wts = K.wts
    N0, USED1 = 28, 24
    G = 5
    HH = 4
    U = NP_T * HH
    NJ = 2 * NT
    SCALE = DDH ** -0.5
    KEYS = PAST + P
    NLINK = 2 * (5 + 3 * NT) + 4 * U + 3 * DEC_B + 2 * (5 + NT)
    with ExitStack() as ctx:
        sem = lambda name: K.semaphore("d_" + name)
        many = lambda name, n: [sem(f"{name}{i}") for i in range(n)]
        sb = Map(nc, K.phase_base, K.after_acc_ret)
        kc = sb("d_kc", [P, 2, 2, W], F32)
        vc = sb("d_vc", [P, 2, 2, W], F32)
        kcT = sb("d_kcT", [P, HH, PAST], F32)
        sb = Map(nc, K.after_acc_ret, K.sbuf_end)
        K.acc_diff = sb("acc_diff", [P, NT, D_MODEL], F32)
        K.after_accs = sb.at
        at_T = sb.at
        qT = sb("d_qT", [P, HH, NT * P], F32)
        kT = sb("d_kT", [P, HH, NT * P], F32)
        oT_hi = sb("d_oT_hi", [P, HH, NT * P], F32R, at=at_T)
        oT_lo = sb("d_oT_lo", [P, HH, NT * P], F32R, at=at_T + HH * NT * P * 4)
        stage = sb("d_stage", [P, NT, W], F32)
        v = sb("d_v", [P, NT, W], F32)
        at_tmp = sb.at
        tmp = sb("d_tmp", [P, 2, W], F32)
        qB = sb("d_qB", [P, 2, HH, P], F32, at=at_tmp)
        Pr = sb("d_P", [P, 4, W], F32)
        AT = sb("d_AT", [P, 2, HH, P], F32)
        Ps = sb("d_Ps", [P, 2, KEYS], F32)
        ATs = sb("d_ATs", [P, 2, 12, DEC_L], F32)
        oTs = sb("d_oTs", [P, W], F32)
        rope = sb("d_rope", [P, NT, 2, 32], F32)
        tabs = sb("d_tabs", [P, 2, NT, 2, DDH], F32)
        gains = sb("d_gains", [P, 2, DDH], F32)
        gsub = sb("d_gsub", [P, DDV], F32)
        lv = sb("d_lv", [P, 4, DDH], F32)
        lam = sb("d_lam", [P, 8], F32)
        mp = sb("d_mask_p", [P, P + CHUNK], F32)
        ms = sb("d_mask_s", [P, P + DEC_B * P], F32)
        st = sb("d_st", [P, 5, NT * 8], F32)
        sm = sb("d_sm", [P, 2, 8], F32)
        sms = sb("d_sms", [P, 2, 8], F32)
        B = [ctx.enter_context(nc.psum_tensor(f"d_B{i}", [P, W], F32)) for i in range(8)]
        pj = B[0:NT]
        const_in, spilled, kc_in, vc_in = sem("const_in"), sem("acc_ret_spilled"), many("kc_in", 2), many("vc_in", 2)
        krow_out, vrow_out, go = sem("krow_out"), sem("vrow_out"), sem("sync_goes_on")
        pj_done, pj_free = sem("pj_done"), many("pj_free", NT)
        squared, reduced, var_done, std_done, roped = map(sem, ("squared", "reduced", "var_done", "std_done", "roped"))
        qkT_done, qkT_taken = map(sem, ("qkT_done", "qkT_taken"))
        s_done, nmax_done, exp_done, A_done, at_done, at_taken, pv_done, o_taken = map(
            sem, ("s_done", "nmax_done", "exp_done", "A_done", "at_done", "at_taken", "pv_done", "o_taken"))
        kcT_done, kcT_taken, qB_zero, qB_done, ss_done, snmax_done, sexp_done, sA_done, sat_done, sat_taken, spv_done = map(
            sem, ("kcT_done", "kcT_taken", "qB_zero", "qB_done", "ss_done", "snmax_done", "sexp_done", "sA_done",
                  "sat_done", "sat_taken", "spv_done"))
        oTs_done, o4_done, osq, dn_done, ot_done, ot_hi, ot_lo, link, lam_exp, lam_sum, acc_zero = map(
            sem, ("oTs_done", "o4_done", "o_squared", "dn_done", "ot_done", "ot_hi", "ot_lo", "dve_link", "lam_exp", "lam_sum", "acc_zero"))
        block = ctx.enter_context(nc.Block())
        w_in = io["w_in"][0]

        def slot_wait(eng, s, i, per, u):
            eng.wait_ge(s, i * per + max(u - 1, 0))

        @block.sync
        def _(sp):
            sp.dma_start(io["acc_ret_d"], K.acc_ret[:]).then_inc(spilled, 16)
            sp.dma_start(rope[:], io["rope_diff"]).then_inc(const_in, 16)
            sp.dma_start(gains[:, 0], io["diff_qnorm_g"].broadcast_to([P, DDH])).then_inc(const_in, 16)
            sp.dma_start(gains[:, 1], io["diff_knorm_g"].broadcast_to([P, DDH])).then_inc(const_in, 16)
            sp.dma_start(gsub[:], io["diff_subln_g"].broadcast_to([P, DDV])).then_inc(const_in, 16)
            for j, name in enumerate(("q1", "k1", "q2", "k2")):
                sp.dma_start(lv[:, j], io["diff_lambda_" + name].broadcast_to([P, DDH])).then_inc(const_in, 16)
            sp.dma_start(mp[:], io["mask_p"]).then_inc(const_in, 16)
            sp.dma_start(ms[:], io["mask_s"]).then_inc(const_in, 16)
            sp.dma_start(lam[:, 5:6], io["csign"]).then_inc(const_in, 16)
            with sp.Fori(0, 2) as i:
                n = lambda c: i * 4 + N0 + c
                wts.load(sp, n(0), rows_of(w_in, i * W + COL_DQ))
                wts.load(sp, n(1), rows_of(w_in, i * W + COL_DK))
                wts.load(sp, n(2), rows_of(w_in, i * W + COL_DV))
                wts.load(sp, n(3), halves_of(io["w_br_diff"][0], i * W))
                for b in range(DEC_B):
                    s = b % 2
                    cache = lambda ap: ap[0, b].rearrange("l h d -> l (h d)")[:, bass.ds(i * W, W)].rearrange("(k p) c -> p k c", p=P)
                    sp.wait_ge(kcT_done, (i * DEC_B + max(b - 1, 0)) * 2)
                    if b == 0:
                        sp.sem_inc(go, 1)
                        sp.wait_ge(spilled, 16)
                    sp.dma_start(kc[:, s], cache(io["cache_diff_k"])).then_inc(kc_in[s], 16)
                    slot_wait(sp, spv_done, i, DEC_B, b)
                    sp.dma_start(vc[:, s], cache(io["cache_diff_v"])).then_inc(vc_in[s], 16)

        @block.gpsimd
        def _(pool):
            with pool.Fori(0, 2) as i:
                for c in range(3):
                    for p in range(4):
                        wts.split_lo(pool, i * 4 + N0 + c, p)
                for p in range(4):
                    wts.split_lo(pool, i * 4 + N0 + 3, p)

        @block.scalar
        def _(act):
            act.wait_ge(lam_sum, 1)
            act.activation(lam[:, 2:4], lam[:, 0:2], ACT.Exp).then_inc(lam_exp, 1)
            with act.Fori(0, 2) as i:
                n = lambda c: i * 4 + N0 + c

                def hi(c, p):
                    if p in (0, 2):
                        free = (wts.used[p], n(c))
                    elif p == 1 and c > 0:
                        free = (wts.used[1], i * 3 + USED1 + c)
                    else:
                        free = (pj_done, i * (G * NT) + c * NT)
                    wts.split_hi(act, n(c), p, free)

                def take(g, dst, squares):
                    for t in range(NT):
                        act.wait_ge(pj_done, i * (G * NT) + g * NT + t + 1)
                        if squares:
                            act.wait_ge(reduced, i * NJ + max(g * NT + t - 3, 0))
                            act.activation(Pr[:, (g * NT + t) % 4], pj[t][:], ACT.Square).then_inc(squared, 1)
                        act.activation(dst[:, t], pj[t][:], ACT.Copy).then_inc(pj_free[t], 1)

                def root(k):
                    act.wait_ge(var_done, i * 4 + k + 1)
                    w = slice(0, NT * 8) if k < 2 else slice(0, NP_T * HH) if k == 2 else slice(NP_T * HH, NT * HH)
                    act.activation(st[:, 2, w], st[:, 1, w], ACT.Sqrt).then_inc(std_done, 1)

                def take_T(a):
                    for t in range(NT):
                        job = a * NT + t
                        act.wait_ge(qkT_done, i * NJ + job + 1)
                        act.activation((qT, kT)[a][:, :, t * P:(t + 1) * P],
                                       B[5 + job % 3][:].rearrange("p (h c) -> p h c", c=P), ACT.Copy).then_inc(qkT_taken, 1)

                def send_rows(name, rows, out):
                    flat = lambda ap: ap.rearrange("l h d -> l (h d)")[:, bass.ds(i * W, W)]
                    act.dma_start(flat(io[f"o_{name}_p"][0, 0]).rearrange("(t p) c -> p t c", p=P), rows[:, 0:NP_T]).then_inc(out, 16)
                    act.dma_start(flat(io[f"o_{name}_s"][0].rearrange("b l h d -> (b l) h d")), rows[:, NP_T]).then_inc(out, 16)

                for p in range(4):
                    hi(0, p)
                for p in range(3):
                    hi(1, p)
                take(0, stage, True)
                hi(1, 3)
                root(0)
                hi(2, 0)
                hi(2, 1)
                take_T(0)
                hi(2, 2)
                take(1, stage, True)
                hi(2, 3)
                root(1)
                hi(3, 0)
                hi(3, 1)
                take_T(1)
                send_rows("k", stage, krow_out)
                hi(3, 2)
                act.wait_ge(vrow_out, i * 32)
                take(2, v, False)
                for t in range(NT):
                    act.wait_ge(pj_free[t], i * G + 3)
                send_rows("v", v, vrow_out)
                hi(3, 3)

                def exps(u):
                    s = u % 2
                    act.wait_ge(nmax_done, i * U + u + 1)
                    slot_wait(act, at_done, i, U, u)
                    nk = (u // HH + 1) * P
                    for m in range(2):
                        last = act.activation(Pr[:, 2 * s + m, 0:nk], B[2 * s + m][:, 0:nk], ACT.Exp, scale=SCALE,
                                              bias=sm[:, s, 2 + m:3 + m], accum_out=sm[:, s, 4 + m:5 + m])
                    last.then_inc(exp_done, 1)

                def copy_AT(u):
                    s, blocks = u % 2, u // HH + 1
                    act.wait_ge(at_done, i * U + u + 1)
                    slot_wait(act, pv_done, i, U, u)
                    act.activation(AT[:, s, 0:blocks].rearrange("p b c -> p (b c)"), B[4 + s][:, 0:blocks * P], ACT.Copy).then_inc(at_taken, 1)

                def take_o(t):
                    act.wait_ge(pv_done, i * U + HH * (t + 1))
                    act.wait_ge(krow_out, i * 32 + 32)
                    act.activation(stage[:, t], B[6 + t % 2][:], ACT.Copy).then_inc(o_taken, 1)

                for u in range(U + 3):
                    if u < U:
                        exps(u)
                    if 2 <= u < U + 2:
                        copy_AT(u - 2)
                    if u >= HH + 2 and (u - 3) % HH == HH - 1:
                        take_o((u - 3) // HH)

                def sq_o(t):
                    act.wait_ge(o_taken, i * NT + t + 1)
                    act.wait_ge(osq, i * NT + t)
                    act.wait_ge(A_done, i * U + U)
                    act.activation(Pr[:, t % 4], stage[:, t], ACT.Square).then_inc(osq, 1)

                for b in range(DEC_B):
                    s = b % 2
                    for k in range(2):
                        act.wait_ge(kcT_done, (i * DEC_B + b) * 2 + k + 1)
                        act.wait_ge(ss_done, i * DEC_B + b)
                        act.activation(kcT[:, :, k * P:(k + 1) * P], B[k][:].rearrange("p (h c) -> p h c", c=P), ACT.Copy) \
                           .then_inc(kcT_taken, 1)
                    act.wait_ge(snmax_done, i * DEC_B + b + 1)
                    slot_wait(act, sat_done, i, DEC_B, b)
                    act.activation(Ps[:, s], B[2 + s][:, 0:KEYS], ACT.Exp, scale=SCALE, bias=sms[:, s, 1:2],
                                   accum_out=sms[:, s, 2:3]).then_inc(sexp_done, 1)
                    if b == 2:
                        for t in range(NP_T):
                            sq_o(t)
                    if b == 3:
                        root(2)
                act.wait_ge(o4_done, i + 1)
                act.activation(stage[:, NP_T], B[7][:], ACT.Copy).then_inc(o_taken, 1)
                sq_o(NP_T)
                root(3)
                for t in range(NT):
                    act.wait_ge(ot_done, i * NT + t + 1)
                    act.activation(oT_hi[:, :, t * P:(t + 1) * P], B[5 + t % 3][:].rearrange("p (h c) -> p h c", c=P),
                                   ACT.Copy).then_inc(ot_hi, 1)
            act.wait_ge(krow_out, 64)
            act.wait_ge(vrow_out, 64)

        @block.vector
        def _(dve):
            dve.memset(K.acc_diff[:], 0.0).then_inc(acc_zero, 1)
            dve.wait_ge(const_in, 11 * 16)
            first = Links(dve, link)
            for a in range(2):
                for m in range(2):
                    for e in range(2):
                        h32 = slice(e * 32, (e + 1) * 32)
                        first(dve.tensor_tensor(tabs[:, a, :, m, h32], rope[:, :, m],
                                                bc(gains[:, a, h32].unsqueeze(1), [P, NT, 32]), ALU.mult))
            first(dve.tensor_scalar(gsub[:], gsub[:], 1.0 - LAM_INIT, None, ALU.mult))
            for a in range(2):
                first(dve.tensor_tensor(lv[:, 2 * a], lv[:, 2 * a], lv[:, 2 * a + 1], ALU.mult))
            first.sync()
            for a in range(2):
                last = dve.tensor_reduce(lam[:, a:a + 1], lv[:, 2 * a], AX, ALU.add)
            last.then_inc(lam_sum, 1)
            dve.wait_ge(lam_exp, 1)
            first(dve.tensor_tensor(lam[:, 4:5], lam[:, 3:4], lam[:, 2:3], ALU.subtract))
            first.sync()
            first(dve.tensor_scalar(lam[:, 4:5], lam[:, 4:5], LAM_INIT, None, ALU.subtract))
            first.sync()
            first(dve.tensor_scalar(lam[:, 7:8], lam[:, 4:5], -1.0, 1.0, ALU.mult, ALU.add))
            first.sync()
            first(dve.tensor_tensor(lam[:, 7:8], lam[:, 7:8], lam[:, 5:6], ALU.mult))
            first.sync()
            first(dve.tensor_tensor(lam[:, 6:7], lam[:, 7:8], lam[:, 4:5], ALU.add))
            first.sync()
            with dve.Fori(0, 2) as i:
                links = Links(dve, link, i * NLINK + first.n)

                def head_norm(a):
                    for t in range(NT):
                        dve.wait_ge(squared, i * NJ + a * NT + t + 1)
                        dve.tensor_reduce(st[:, 0, t * 8:(t + 1) * 8], Pr[:, (a * NT + t) % 4].rearrange("p (g c) -> p g c", c=DDH),
                                          AX, ALU.add).then_inc(reduced, 1)
                    dve.wait_ge(reduced, i * NJ + a * NT + NT)
                    dve.tensor_scalar(st[:, 1], st[:, 0], 1.0 / DDH, EPS, ALU.mult, ALU.add).then_inc(var_done, 1)
                    dve.wait_ge(std_done, i * 4 + a + 1)
                    rsqrt_steps(dve, links, st[:, 3], st[:, 1], st[:, 2], st[:, 4])
                    for t in range(NT):
                        pj_taken(dve, a, t)
                        x = stage[:, t].rearrange("p (g c) -> p g c", c=DDH)
                        xx = stage[:, t].rearrange("p (g e c) -> p g e c", e=2, c=32)
                        t1, t2 = (tmp[:, m].rearrange("p (g e c) -> p g e c", e=2, c=32) for m in range(2))
                        dve.wait_ge(roped, i * NJ + a * NT + t)
                        for m in range(2):
                            links(dve.tensor_tensor(tmp[:, m].rearrange("p (g c) -> p g c", c=DDH), x,
                                                    bc(tabs[:, a, t, m].unsqueeze(1), [P, 8, DDH]), ALU.mult))
                        links.sync()
                        dve.tensor_tensor(xx[:, :, 0], t1[:, :, 0], t2[:, :, 1], ALU.subtract)
                        links(dve.tensor_tensor(xx[:, :, 1], t1[:, :, 1], t2[:, :, 0], ALU.add))
                        links.sync()
                        dve.tensor_tensor(x, x, bc(st[:, 3, t * 8:(t + 1) * 8].unsqueeze(2), [P, 8, DDH]), ALU.mult).then_inc(roped, 1)

                def pj_taken(eng, g, t):
                    eng.wait_ge(pj_free[t], i * G + g + 1)

                def block_q(b):
                    for m in range(2):
                        rows = slice(m * DDH, (m + 1) * DDH)
                        dst = qB[rows, b % 2].rearrange("p h c -> p (h c)")
                        dst = bass.AP(tensor=dst.tensor, offset=dst.offset + m * DEC_L,
                                      ap=[list(dst.ap[0]), [P + 2 * DEC_L, HH], [1, DEC_L]])
                        dve.tensor_copy(dst, qT[rows, :, SEQ + b * DEC_L:SEQ + (b + 1) * DEC_L]).then_inc(qB_done, 1)

                head_norm(0)
                head_norm(1)
                dve.wait_ge(roped, i * NJ + NJ)
                dve.memset(qB[:], 0.0).then_inc(qB_zero, 1)
                dve.wait_ge(qB_zero, i + 1)
                dve.wait_ge(qkT_taken, i * NJ + NT)
                block_q(0)
                block_q(1)

                def maxima(u):
                    s, nk = u % 2, (u // HH + 1) * P
                    dve.wait_ge(s_done, i * U + u + 1)
                    for m in range(2):
                        ins = dve.tensor_reduce(sm[:, s, m:m + 1], B[2 * s + m][:, 0:nk], AX, ALU.max)
                    links(ins)
                    links.sync()
                    dve.tensor_scalar(sm[:, s, 2:4], sm[:, s, 0:2], -SCALE, None, ALU.mult).then_inc(nmax_done, 1)

                def combine(u):
                    s, nk = u % 2, (u // HH + 1) * P
                    dve.wait_ge(exp_done, i * U + u + 1)
                    links(dve.reciprocal(sm[:, s, 6:8], sm[:, s, 4:6]))
                    links.sync()
                    links(dve.tensor_tensor(sm[:, s, 7:8], sm[:, s, 7:8], lam[:, 4:5], ALU.mult))
                    a, b = Pr[:, 2 * s, 0:nk], Pr[:, 2 * s + 1, 0:nk]
                    links(dve.tensor_scalar(a, a, sm[:, s, 6:7], None, ALU.mult))
                    links.sync()
                    dve.scalar_tensor_tensor(a, b, sm[:, s, 7:8], a, ALU.mult, ALU.add).then_inc(A_done, 1)

                for u in range(U + 1):
                    if u < U:
                        maxima(u)
                    if u >= 1:
                        combine(u - 1)

                def sub_roots(ts, k):
                    for t in ts:
                        dve.wait_ge(osq, i * NT + t + 1)
                        links(dve.tensor_reduce(st[:, 0, t * HH:(t + 1) * HH], Pr[:, t % 4].rearrange("p (g c) -> p g c", c=DDV),
                                                AX, ALU.add))
                    links.sync()
                    w = slice(ts[0] * HH, (ts[-1] + 1) * HH)
                    dve.tensor_scalar(st[:, 1, w], st[:, 0, w], 1.0 / DDV, EPS, ALU.mult, ALU.add).then_inc(var_done, 1)

                def sub_norm(ts, k):
                    w = slice(ts[0] * HH, (ts[-1] + 1) * HH)
                    if ts[0] == 0 or ts[0] == NP_T:
                        w = slice(0, NP_T * HH) if ts[0] == 0 else w
                        dve.wait_ge(std_done, i * 4 + k + 1)
                        rsqrt_steps(dve, links, st[:, 3, w], st[:, 1, w], st[:, 2, w], st[:, 4, w])
                    for t in ts:
                        x = stage[:, t].rearrange("p (g c) -> p g c", c=DDV)
                        links(dve.tensor_tensor(x, x, bc(st[:, 3, t * HH:(t + 1) * HH].unsqueeze(2), [P, HH, DDV]), ALU.mult))
                        links.sync()
                        dve.tensor_tensor(x, x, bc(gsub[:].unsqueeze(1), [P, HH, DDV]), ALU.mult).then_inc(dn_done, 1)

                def s_maxima(b):
                    s = b % 2
                    dve.wait_ge(ss_done, i * DEC_B + b + 1)
                    links(dve.tensor_reduce(sms[:, s, 0:1], B[2 + s][:, 0:KEYS], AX, ALU.max))
                    links.sync()
                    dve.tensor_scalar(sms[:, s, 1:2], sms[:, s, 0:1], -SCALE, None, ALU.mult).then_inc(snmax_done, 1)

                def s_scale(b):
                    s = b % 2
                    dve.wait_ge(sexp_done, i * DEC_B + b + 1)
                    links(dve.reciprocal(sms[:, s, 3:4], sms[:, s, 2:3]))
                    links.sync()
                    links(dve.tensor_tensor(sms[:, s, 3:4], sms[:, s, 3:4], lam[:, 6:7], ALU.mult))
                    links.sync()
                    dve.tensor_scalar(Ps[:, s], Ps[:, s], sms[:, s, 3:4], None, ALU.mult).then_inc(sA_done, 1)

                def s_fold(b):
                    s = b % 2
                    dve.wait_ge(sat_done, i * DEC_B + b + 1)
                    slot_wait(dve, spv_done, i, DEC_B, b)
                    dve.tensor_reduce(ATs[:, s], B[4 + s][:, 0:3 * P].rearrange("p (g m l) -> p g l m", m=2, l=DEC_L), AX, ALU.add) \
                       .then_inc(sat_taken, 1)

                for b in range(DEC_B + 1):
                    if b < DEC_B:
                        s_maxima(b)
                        if b + 2 < DEC_B:
                            block_q(b + 2)
                    if b >= 1:
                        s_fold(b - 1)
                    if b < DEC_B:
                        s_scale(b)
                    if b == 3:
                        sub_roots(list(range(NP_T)), 2)
                    if 4 <= b < 4 + NP_T:
                        sub_norm([b - 4], 2)
                dve.wait_ge(spv_done, i * DEC_B + DEC_B)
                dve.tensor_copy(oTs[:], B[6][:]).then_inc(oTs_done, 1)
                sub_roots([NP_T], 3)
                sub_norm([NP_T], 3)
                for t in range(NT):
                    dve.wait_ge(ot_hi, i * NT + t + 1)
                    sl = (slice(None), slice(None), slice(t * P, (t + 1) * P))
                    dve.tensor_tensor(oT_lo[sl], B[5 + t % 3][:].rearrange("p (h c) -> p h c", c=P),
                                      oT_hi[sl].bitcast(F32), ALU.subtract).then_inc(ot_lo, 1)
                dve.wait_ge(acc_zero, 1)
                for j in range(2):
                    for t in range(NT):
                        dve.wait_ge(pj_done, i * (G * NT) + (3 + j) * NT + t + 1)
                        a = K.acc_diff[:, t, j * W:(j + 1) * W]
                        dve.tensor_tensor(a, a, pj[t][:], ALU.add).then_inc(pj_free[t], 1)
                assert links.n == NLINK, (links.n, NLINK)

        @block.tensor
        def _(pe):
            pe.wait_ge(const_in, 11 * 16)
            with pe.Fori(0, 2) as i:
                n = lambda c: i * 4 + N0 + c
                group = lambda g: i * G + g
                hT = (K.hT_hi, K.hT_lo)

                def transpose_rows(a):
                    for t in range(NT):
                        job = a * NT + t
                        pe.wait_ge(roped, i * NJ + job + 1)
                        if job >= 3:
                            pe.wait_ge(qkT_taken, i * NJ + job - 2)
                        for h in range(HH):
                            last = pe.transpose(B[5 + job % 3][:, h * P:(h + 1) * P], stage[:, t, h * P:(h + 1) * P], K.ident[:])
                        last.then_inc(qkT_done, 1)

                project(pe, wts, n(0), pj, *hT, pj_free, group(0), pj_done)
                project(pe, wts, n(1), pj, *hT, pj_free, group(1), pj_done, between=lambda: transpose_rows(0))
                project(pe, wts, n(2), pj, *hT, pj_free, group(2), pj_done, between=lambda: transpose_rows(1))

                def scores(u):
                    s, t, h = u % 2, u // HH, u % HH
                    nk = (t + 1) * P
                    if u < 2:
                        for b in (2 * u, 2 * u + 1):
                            pe.wait_ge(pj_free[b], i * G + 3)
                    else:
                        pe.wait_ge(exp_done, i * U + u - 1)
                    for m in range(2):
                        rows = slice(m * DDH, (m + 1) * DDH)
                        pe.matmul(B[2 * s + m][:, 0:nk], qT[rows, h, t * P:(t + 1) * P], kT[rows, h, 0:nk], start=True, stop=False)
                        last = pe.matmul(B[2 * s + m][:, nk - CHUNK:nk], mp[rows, 0:P], mp[rows, P:P + CHUNK], start=False, stop=True)
                    last.then_inc(s_done, 1)

                def turn(u):
                    s, t = u % 2, u // HH
                    pe.wait_ge(A_done, i * U + u + 1)
                    if u < 2:
                        pe.wait_ge(pj_free[NP_T], i * G + 3)
                    else:
                        pe.wait_ge(at_taken, i * U + u - 1)
                    for j in range(t + 1):
                        last = pe.transpose(B[4 + s][:, j * P:(j + 1) * P], Pr[:, 2 * s, j * P:(j + 1) * P], K.ident[:])
                    last.then_inc(at_done, 1)

                def values(u):
                    s, t, h = u % 2, u // HH, u % HH
                    pe.wait_ge(at_taken, i * U + u + 1)
                    if h == 0 and t >= 2:
                        pe.wait_ge(o_taken, i * NT + t - 1)
                    for j in range(t + 1):
                        last = pe.matmul(B[6 + t % 2][:, h * P:(h + 1) * P], AT[:, s, j], v[:, j, h * P:(h + 1) * P],
                                         start=(j == 0), stop=(j == t))
                    last.then_inc(pv_done, 1)

                pe.wait_ge(qkT_taken, i * NJ + NJ)
                for u in range(U + 3):
                    if u < U:
                        scores(u)
                    if 2 <= u < U + 2:
                        turn(u - 2)
                    if u >= 3:
                        values(u - 3)

                def s_scores(b):
                    s = b % 2
                    pe.wait_ge(kc_in[s], i * (DEC_B // 2 * 16) + (b // 2 + 1) * 16)
                    if b == 0:
                        pe.wait_ge(exp_done, i * U + U)
                    pe.wait_ge(kcT_taken, (i * DEC_B + b) * 2)
                    for k in range(2):
                        for h in range(HH):
                            last = pe.transpose(B[k][:, h * P:(h + 1) * P], kc[:, s, k, h * P:(h + 1) * P], K.ident[:])
                        last.then_inc(kcT_done, 1)
                    pe.wait_ge(qB_done, (i * DEC_B + b) * 2 + 2)
                    pe.wait_ge(kcT_taken, (i * DEC_B + b) * 2 + 2)
                    if b >= 2:
                        pe.wait_ge(sexp_done, i * DEC_B + b - 1)
                    out = B[2 + s]
                    for h in range(HH):
                        pe.matmul(out[:, 0:PAST], qB[:, s, h], kcT[:, h], start=(h == 0), stop=False)
                        pe.matmul(out[:, PAST:KEYS], qB[:, s, h], kT[:, h, SEQ:SEQ + P], start=False, stop=False)
                    pe.matmul(out[:, PAST:KEYS], ms[:, 0:P], ms[:, P + b * P:P + (b + 1) * P], start=False, stop=True).then_inc(ss_done, 1)

                def s_values(b):
                    s = b % 2
                    pe.wait_ge(sA_done, i * DEC_B + b + 1)
                    if b >= 2:
                        pe.wait_ge(sat_taken, i * DEC_B + b - 1)
                    else:
                        pe.wait_ge(at_taken, i * U + U)
                    for j in range(3):
                        last = pe.transpose(B[4 + s][:, j * P:(j + 1) * P], Ps[:, s, j * P:(j + 1) * P], K.ident[:])
                    last.then_inc(sat_done, 1)
                    pe.wait_ge(vc_in[s], i * (DEC_B // 2 * 16) + (b // 2 + 1) * 16)
                    pe.wait_ge(sat_taken, i * DEC_B + b + 1)
                    if b == 0:
                        pe.wait_ge(o_taken, i * NT + NP_T)
                    for h in range(HH):
                        cols = slice(h * P + b * DEC_L, h * P + (b + 1) * DEC_L)
                        for j in range(3):
                            val = vc[:, s, j, h * P:(h + 1) * P] if j < 2 else v[:, NP_T, h * P:(h + 1) * P]
                            last = pe.matmul(B[6][:, cols], val, ATs[:, s, j * HH + h], start=(j == 0), stop=(j == 2))
                    last.then_inc(spv_done, 1)

                for b in range(DEC_B + 1):
                    if b < DEC_B:
                        s_scores(b)
                    if b >= 1:
                        s_values(b - 1)
                pe.wait_ge(oTs_done, i + 1)
                for h in range(HH):
                    last = pe.transpose(B[7][:, h * P:(h + 1) * P], oTs[:, h * P:(h + 1) * P], K.ident[:])
                last.then_inc(o4_done, 1)
                for t in range(NT):
                    pe.wait_ge(dn_done, i * NT + t + 1)
                    if t == 2:
                        pe.wait_ge(o_taken, i * NT + NT)
                    if t >= 3:
                        pe.wait_ge(ot_lo, i * NT + t - 2)
                    for h in range(HH):
                        last = pe.transpose(B[5 + t % 3][:, h * P:(h + 1) * P], stage[:, t, h * P:(h + 1) * P], K.ident[:])
                    last.then_inc(ot_done, 1)
                branch(pe, wts, n(3), pj, oT_hi, oT_lo, lambda t: pe.wait_ge(ot_lo, i * NT + t + 1), pj_free, group(3), pj_done)


def phase_g(nc, io, K):
    wts = K.wts
    N0, USED1 = 36, 30
    NE, NG, EG = N_EXP, 4, 4
    NB_T = 2 * NT
    with ExitStack() as ctx:
        sem = lambda name: K.semaphore("g_" + name)
        many = lambda name, n: [sem(f"{name}{i}") for i in range(n)]
        sb = Map(nc, K.phase_base, K.sbuf_end)
        acc_ret = sb("g_acc_ret", [P, NT, D_MODEL], F32)
        h2T = sb("g_h2T", [P, KT, NT * P], F32, at=K.phase_base)
        K.h2_at = sb.at
        K.h2 = sb("g_h2", [P, NT, D_MODEL], F32)
        K.x1 = sb("g_x1", [P, NT, D_MODEL], F32)
        K.pos = sb("g_pos", [P, 2, NT], F32)
        K.eid = sb("g_eid", [P, 2, NT], F32)
        K.wgt = sb("g_wgt", [P, 2, NT], F32)
        K.rounds = sb("g_rounds", [P, 4], I32)
        K.after_g = sb.at
        sg = sb("g_sg", [P, NT, W], F32)
        mods = sb("g_mods", [P, 2, 3, D_MODEL], F32)
        wr = sb("g_wr", [P, KT, 20], F32)
        br = sb("g_br", [P, 20], F32)
        tri = sb("g_tri", [P, 2 * P], F32)
        rk = sb("g_rk", [P, 24], F32)
        L = sb("g_L", [P, NT, 20], F32)
        s4 = sb("g_s4", [P, 8, NT, 4], F32)
        s1 = sb("g_s1", [P, 8, NT], F32)
        A = sb("g_A", [P, 4, NT, NE], F32)
        st = sb("g_st", [P, 5, 8], F32)
        B = [ctx.enter_context(nc.psum_tensor(f"g_B{i}", [P, W], F32)) for i in range(8)]
        pj = B[0:NT]
        acc_in, x_in, mods_in, small_in = map(sem, ("acc_in", "x_in", "mods_in", "small_in"))
        pj_done, pj_free, ret_gated, merged = sem("pj_done"), many("pj_free", NT), sem("ret_gated"), sem("merged")
        t_done, t_hi, t_taken, scaled, x1_done = map(sem, ("t_done", "t_hi", "t_taken", "scaled", "x1_done"))
        sumsq, var_done, std_done, h2_done, logits_done = map(sem, ("sumsq", "var_done", "std_done", "h2_done", "logits_done"))
        link, shifted, exp_done, assigned, pos_done, sg_free = map(sem, ("dve_link", "shifted", "exp_done", "assigned", "pos_done", "sg_free"))
        block = ctx.enter_context(nc.Block())
        w_in = io["w_in"][0]
        kind = lambda t: 0 if t < NP_T else 1
        half = lambda j: slice(j * W, (j + 1) * W)

        @block.sync
        def _(sp):
            sp.dma_start(acc_ret[:], io["acc_ret_d"]).then_inc(acc_in, 16)
            with sp.Fori(0, 2) as j:
                for c in range(2):
                    wts.load(sp, j * 2 + N0 + c, rows_of(w_in, j * W + COL_GATE + c * D_MODEL))
            sp.dma_start(K.x1[:, 0:NP_T], io["x_prompt"][0].rearrange("(t p) d -> p t d", p=P)).then_inc(x_in, 16)
            sp.dma_start(K.x1[:, NP_T], io["x_sample"].rearrange("b l d -> (b l) d")).then_inc(x_in, 16)
            for kd in range(2):
                sp.dma_start(mods[:, kd], io["mods"][kd, 0:3].rearrange("m p d -> p m d")).then_inc(mods_in, 16)
            for j in range(2):
                wts.load(sp, N0 + 4 + j, rows_of(io["w_out"][0], j * W))
            sp.dma_start(wr[:, :, 0:NG], io["w_group"][0].rearrange("(k p) n -> p k n", p=P)).then_inc(small_in, 16)
            sp.dma_start(wr[:, :, NG:20], io["w_expert_router"][0].rearrange("(k p) n -> p k n", p=P)).then_inc(small_in, 16)
            sp.dma_start(br[:, 0:NG], io["b_group"].broadcast_to([P, NG])).then_inc(small_in, 16)
            sp.dma_start(br[:, NG:20], io["b_expert"].broadcast_to([P, NE])).then_inc(small_in, 16)
            sp.dma_start(tri[:], io["tri"]).then_inc(small_in, 16)
            sp.dma_start(rk[:], io["ranks"].broadcast_to([P, 24])).then_inc(small_in, 16)

        @block.gpsimd
        def _(pool):
            with pool.Fori(0, 2) as j:
                for c in range(2):
                    for p in range(4):
                        wts.split_lo(pool, j * 2 + N0 + c, p)
            for c in range(4, 6):
                for p in range(4):
                    wts.split_lo(pool, N0 + c, p)

        @block.scalar
        def _(act):
            def hi(c, p):
                free = (pj_done, c * NT) if p == 3 else (wts.used[p], c + (USED1 if p == 1 else N0))
                wts.split_hi(act, c + N0, p, free)

            with act.Fori(0, 2) as j:
                for c in range(2):
                    for p in range(4):
                        hi(j * 2 + c, p)
                    for t in range(NT):
                        act.wait_ge(pj_done, (j * 2 + c) * NT + t + 1)
                        act.wait_ge(sg_free, (j * 2 + c) * NT)
                        act.activation(sg[:, t], pj[t][:], ACT.Sigmoid).then_inc(pj_free[t], 1)
            for c in range(4, 6):
                for p in range(4):
                    hi(c, p)
                if c == 4:
                    for q in range(NB_T):
                        act.wait_ge(t_done, q + 1)
                        s = (slice(None), slice(4 * (q % 2), 4 * (q % 2) + 4), slice(q // 2 * P, (q // 2 + 1) * P))
                        act.activation(K.hT_hi[s], B[5 + q % 3][:].rearrange("p (k c) -> p k c", c=P), ACT.Copy).then_inc(t_hi, 1)
            for t in range(NT):
                act.wait_ge(x1_done, 2 * NT)
                act.wait_ge(sumsq, t)
                act.activation(sg[:, 0:2].rearrange("p a c -> p (a c)"), K.x1[:, t], ACT.Square, accum_out=st[:, 0, t:t + 1]).then_inc(sumsq, 1)
            act.wait_ge(var_done, 1)
            act.activation(st[:, 2, 0:NT], st[:, 1, 0:NT], ACT.Sqrt).then_inc(std_done, 1)
            for q in range(NB_T):
                act.wait_ge(t_done, NB_T + q + 1)
                s = (slice(None), slice(4 * (q % 2), 4 * (q % 2) + 4), slice(q // 2 * P, (q // 2 + 1) * P))
                act.activation(h2T[s], B[5 + q % 3][:].rearrange("p (k c) -> p k c", c=P), ACT.Copy).then_inc(t_taken, 1)
            act.wait_ge(shifted, 1)
            act.activation(s4[:, 1], s4[:, 0], ACT.Exp).then_inc(exp_done, 1)
            act.wait_ge(shifted, 2)
            act.activation(s1[:, 5], s1[:, 4], ACT.Exp).then_inc(exp_done, 1)

        @block.vector
        def _(dve):
            links = Links(dve, link)

            def do(ins):
                links(ins)
                links.sync()

            dve.wait_ge(acc_in, 16)
            with dve.Fori(0, 2) as j:
                a_ret, a_diff = (lambda t: acc_ret[:, t, bass.ds(j * W, W)]), (lambda t: K.acc_diff[:, t, bass.ds(j * W, W)])
                for t in range(NT):
                    dve.wait_ge(pj_free[t], j * 2 + 1)
                    dve.tensor_tensor(a_ret(t), a_ret(t), sg[:, t], ALU.mult).then_inc(sg_free, 1)
                for t in range(NT):
                    dve.wait_ge(pj_free[t], j * 2 + 2)
                    dve.tensor_tensor(a_diff(t), a_diff(t), sg[:, t], ALU.mult).then_inc(sg_free, 1)
                for t in range(NT):
                    dve.wait_ge(sg_free, j * (2 * NT) + NT + t + 1)
                    dve.tensor_tensor(a_ret(t), a_ret(t), a_diff(t), ALU.add).then_inc(merged, 1)
            for q in range(NB_T):
                dve.wait_ge(t_hi, q + 1)
                s = (slice(None), slice(4 * (q % 2), 4 * (q % 2) + 4), slice(q // 2 * P, (q // 2 + 1) * P))
                dve.tensor_tensor(K.hT_lo[s], B[5 + q % 3][:].rearrange("p (k c) -> p k c", c=P), K.hT_hi[s].bitcast(F32),
                                  ALU.subtract).then_inc(t_taken, 1)
            dve.wait_ge(x_in, 32)
            dve.wait_ge(mods_in, 32)
            for j in range(2):
                for t in range(NT):
                    dve.wait_ge(pj_done, (4 + j) * NT + t + 1)
                    dve.tensor_tensor(sg[:, t], pj[t][:], mods[:, kind(t), 0, half(j)], ALU.mult).then_inc(pj_free[t], 1)
                for t in range(NT):
                    dve.wait_ge(pj_free[t], 5 + j)
                    dve.tensor_tensor(K.x1[:, t, half(j)], K.x1[:, t, half(j)], sg[:, t], ALU.add).then_inc(x1_done, 1)
                if j == 0:
                    dve.wait_ge(x1_done, NT)
            dve.wait_ge(sumsq, NT)
            dve.tensor_scalar(st[:, 1, 0:NT], st[:, 0, 0:NT], 1.0 / D_MODEL, EPS, ALU.mult, ALU.add).then_inc(var_done, 1)
            dve.wait_ge(std_done, 1)
            rsqrt_steps(dve, links, st[:, 3, 0:NT], st[:, 1, 0:NT], st[:, 2, 0:NT], st[:, 4, 0:NT])
            for t in range(NT):
                links(dve.scalar_tensor_tensor(K.h2[:, t], K.x1[:, t], st[:, 3, t:t + 1], mods[:, kind(t), 2], ALU.mult, ALU.mult))
                links.sync()
                dve.tensor_tensor(K.h2[:, t], K.h2[:, t], mods[:, kind(t), 1], ALU.add).then_inc(h2_done, 1)
            dve.wait_ge(small_in, 6 * 16)
            dve.wait_ge(logits_done, 1)
            do(dve.tensor_tensor(L[:], B[0][:, 0:NT * 20].rearrange("p (t c) -> p t c", c=20), bc(br[:].unsqueeze(1), [P, NT, 20]), ALU.add))
            four = lambda x: bc(x.unsqueeze(2), [P, NT, 4])
            ranks = bc(rk[:, 0:4].unsqueeze(1), [P, NT, 4])

            def first_max(x, top, hot):
                do(dve.tensor_reduce(top, x, AX, ALU.max))
                do(dve.tensor_tensor(hot, x, four(top), ALU.is_equal))
                do(dve.tensor_tensor(hot, hot, ranks, ALU.mult))
                do(dve.tensor_reduce(s1[:, 7], hot, AX, ALU.max))
                do(dve.tensor_tensor(hot, hot, four(s1[:, 7]), ALU.is_equal))

            G4, E4, H1, H2, M4 = s4[:, 2], s4[:, 3], s4[:, 4], s4[:, 5], s4[:, 6]
            first_max(L[:, :, 0:NG], s1[:, 0], G4)
            dve.tensor_tensor(s4[:, 0], L[:, :, 0:NG], four(s1[:, 0]), ALU.subtract).then_inc(shifted, 1)
            Lg = L[:, :, NG:20].rearrange("p t (g c) -> p t g c", c=EG)
            for t in range(NT):
                links(dve.tensor_tensor(A[:, 3, t].rearrange("p (g c) -> p g c", c=EG), Lg[:, t], bc(G4[:, t].unsqueeze(2), [P, NG, EG]), ALU.mult))
            links.sync()
            do(dve.tensor_reduce(E4, A[:, 3].rearrange("p t (g c) -> p t c g", c=EG), AX, ALU.add))
            first_max(E4, s1[:, 1], H1)
            do(dve.tensor_scalar(M4, H1, NEG, None, ALU.mult))
            do(dve.tensor_tensor(M4, M4, E4, ALU.add))
            first_max(M4, s1[:, 2], H2)
            dve.tensor_tensor(s1[:, 4], s1[:, 2], s1[:, 1], ALU.subtract).then_inc(shifted, 1)
            for a, H in ((0, H1), (1, H2)):
                for t in range(NT):
                    links(dve.tensor_tensor(A[:, a, t].rearrange("p (g c) -> p g c", c=EG), bc(G4[:, t].unsqueeze(2), [P, NG, EG]),
                                            bc(H[:, t].unsqueeze(1), [P, NG, EG]), ALU.mult))
            links.sync()
            dve.tensor_tensor(A[:, 2], A[:, 0], A[:, 1], ALU.add).then_inc(assigned, 1)
            dve.wait_ge(exp_done, 2)
            do(dve.tensor_reduce(s1[:, 3], s4[:, 1], AX, ALU.add))
            do(dve.reciprocal(s1[:, 3], s1[:, 3]))
            do(dve.tensor_scalar(s1[:, 6], s1[:, 5], 1.0, None, ALU.add))
            do(dve.reciprocal(s1[:, 6], s1[:, 6]))
            do(dve.tensor_tensor(K.wgt[:, 0], s1[:, 6], s1[:, 3], ALU.mult))
            do(dve.tensor_tensor(K.wgt[:, 1], K.wgt[:, 0], s1[:, 5], ALU.mult))
            for a in range(2):
                nums = bc(rk[:, 4:20].unsqueeze(1), [P, NT, NE])
                do(dve.tensor_tensor(A[:, 3], A[:, a], nums, ALU.mult))
                do(dve.tensor_reduce(K.eid[:, a], A[:, 3], AX, ALU.add))
            dve.wait_ge(pos_done, 1)
            for a in range(2):
                do(dve.tensor_tensor(A[:, 3], A[:, a], B[1][:, 0:NT * NE].rearrange("p (t e) -> p t e", e=NE), ALU.mult))
                do(dve.tensor_reduce(K.pos[:, a], A[:, 3], AX, ALU.add))
            do(dve.tensor_reduce(s1[:, 0, 0:1], B[1][:, NT * NE:(NT + 1) * NE], AX, ALU.max))
            do(dve.tensor_tensor(s4[:, 0, 0], bc(s1[:, 0, 0:1], [P, 4]), rk[:, 20:24], ALU.is_gt))
            do(dve.tensor_reduce(s1[:, 0, 1:2], s4[:, 0, 0], AX, ALU.add))
            do(dve.tensor_scalar(K.rounds[:, 0:1], s1[:, 0, 1:2], 1.0, None, ALU.add))

        @block.tensor
        def _(pe):
            hT = (K.hT_hi, K.hT_lo)
            with pe.Fori(0, 2) as j:
                for c in range(2):
                    project(pe, wts, j * 2 + N0 + c, pj, *hT, pj_free, j * 2 + c, pj_done)

            def turn(src, ready, q0):
                for q in range(NB_T):
                    t = q // 2
                    ready(t)
                    if q0 + q >= 3:
                        pe.wait_ge(t_taken, q0 + q - 2)
                    for a in range(4):
                        k = 4 * (q % 2) + a
                        last = pe.transpose(B[5 + q % 3][:, a * P:(a + 1) * P], src[:, t, k * P:(k + 1) * P], K.ident[:])
                    last.then_inc(t_done, 1)

            turn(acc_ret, lambda t: pe.wait_ge(merged, NT + t + 1), 0)
            pe.wait_ge(t_taken, NB_T)
            for j in range(2):
                project(pe, wts, N0 + 4 + j, pj, *hT, pj_free, 4 + j, pj_done)
            turn(K.h2, lambda t: pe.wait_ge(h2_done, t + 1), NB_T)
            pe.wait_ge(t_taken, 2 * NB_T)
            pe.wait_ge(small_in, 6 * 16)
            for t in range(NT):
                pe.wait_ge(pj_free[0], 6)
                for k in range(KT):
                    last = pe.matmul(B[0][:, t * 20:(t + 1) * 20], h2T[:, k, t * P:(t + 1) * P], wr[:, k], start=(k == 0), stop=(k == KT - 1))
            last.then_inc(logits_done, 1)
            pe.wait_ge(assigned, 1)
            pe.wait_ge(pj_free[1], 6)
            for t in range(NT + 1):
                out = B[1][:, t * NE:(t + 1) * NE]
                for s in range(min(t, NT - 1) + 1):
                    last = pe.matmul(out, tri[:, 0:P] if s == t else tri[:, P:2 * P], A[:, 2, s], start=(s == 0), stop=(s == min(t, NT - 1)))
            last.then_inc(pos_done, 1)


def phase_m(nc, io, K):
    wts = K.wts
    N0, USED1 = 42, 36
    NE = N_EXP
    BIG = 1.0e6
    with ExitStack() as ctx:
        sem = lambda name: K.semaphore("m_" + name)
        sb = Map(nc, K.hT_at, K.phase_base)
        yacc = sb("m_yacc", [P, NT, D_MODEL], F32)
        xT_hi = sb("m_xT_hi", [P, KT, P], F32R)
        xT_lo = sb("m_xT_lo", [P, KT, P], F32R)
        xe = sb("m_xe", [P, D_MODEL], F32)
        yst = sb("m_yst", [P, D_MODEL], F32)
        sb = Map(nc, K.after_g, K.sbuf_end)
        gt2 = sb("m_gt2", [P, 2, D_MODEL], F32)
        gx = sb("m_gx", [P, 2, D_MODEL], F32)
        su = sb("m_su", [P, W], F32)
        aT_hi = sb("m_aT_hi", [P, 4, P], F32R)
        aT_lo = sb("m_aT_lo", [P, 4, P], F32R)
        idf = sb("m_idf", [P, 5, 2, NT], F32)
        idx = sb("m_idx", [P, 2, 2, NT], I32)
        wv = sb("m_wv", [P, 2, NT], F32)
        B = [ctx.enter_context(nc.psum_tensor(f"m_B{i}", [P, W], F32)) for i in range(8)]
        U, V, Y, T, AT = B[0], B[1], B[2:4], B[4:6], B[6]
        gt2_in, xe_in, y_out, out_sem, scat = map(sem, ("gt2_in", "xe_in", "y_out", "rows_out", "scattered"))
        gath = [sem(f"gathered{i}") for i in range(2)]
        idx_done, used, added, go = sem("idx_done"), sem("gathers_used"), sem("added"), sem("pool_goes_on")
        t_done, t_hi, t_lo, u_done, v_done, su_done, a_done, at_done, at_hi, at_lo, y0_done, y1_done, y_taken = map(
            sem, ("t_done", "t_hi", "t_lo", "u_done", "v_done", "su_done", "a_done", "at_done", "at_hi", "at_lo",
                  "y0_done", "y1_done", "y_taken"))
        link, y_zero, fin = sem("dve_link"), sem("y_zero"), sem("fin")
        block = ctx.enter_context(nc.Block())
        kind = lambda t: 0 if t < NP_T else 1
        w1 = io["w1"][0].rearrange("e r n -> (e r) n")
        w3 = io["w3"][0].rearrange("e r n -> (e r) n")
        w2 = io["w2"][0].rearrange("e r n -> (e r) n")
        rounds = lambda eng: eng.value_load(K.rounds[0:1, 0:1], min_val=1, max_val=5)

        def rows_at(w, r0):
            return [w[bass.ds(r0 + p * 256, 256), :].rearrange("(k r) n -> r k n", k=2) for p in range(4)]

        @block.sync
        def _(sp):
            R = rounds(sp)
            for kd in range(2):
                sp.dma_start(gt2[:, kd], io["mods"][kd, 3]).then_inc(gt2_in, 16)
            with sp.Fori(0, R) as r:
                sp.wait_ge(scat, r * (2 * NT * 16) + 2 * NT * 16)
                sp.dma_start(xe[:], io["xg"][0:P, :]).then_inc(xe_in, 16)
                with sp.Fori(0, NE) as e:
                    n = r * (3 * NE) + e * 3 + N0
                    wts.load(sp, n, rows_at(w1, e * D_MODEL))
                    sp.wait_ge(t_done, r * (2 * NE + 2) + e * 2 + 2)
                    sp.dma_start(xe[:], io["xg"][bass.ds(e * P + P, P), :]).then_inc(xe_in, 16)
                    wts.load(sp, n + 1, rows_at(w3, e * D_MODEL))
                    wts.load(sp, n + 2, halves_of(w2, e * D_EXP))
            sp.wait_ge(fin, NT)
            sp.dma_start(io["o_y_p"][0].rearrange("(t p) d -> p t d", p=P), yacc[:, 0:NP_T]).then_inc(out_sem, 16)
            sp.dma_start(io["o_y_s"].rearrange("b l d -> (b l) d"), yacc[:, NP_T]).then_inc(out_sem, 16)
            sp.wait_ge(out_sem, 32)

        @block.gpsimd
        def _(pool):
            R = rounds(pool)
            with pool.Fori(0, R) as r:
                pool.wait_ge(idx_done, r * 4 + 4)
                pool.sem_inc(go, 1)
                for a in range(2):
                    for t in range(NT):
                        pool.indirect_dma_start(
                            out=io["xg"][:, :], out_offset=bass.IndirectOffsetOnAxis(ap=idx[:, 0, a, t:t + 1], axis=0),
                            in_=K.h2[:, t], in_offset=None, bounds_check=NE * CAP - 1, oob_is_err=False).then_inc(scat, 16)
                with pool.Fori(0, NE) as e:
                    n = r * (3 * NE) + e * 3 + N0
                    for c in range(3):
                        for p in (1, 3):
                            wts.split_lo(pool, n + c, p)
                pool.wait_ge(y_out, r * (NE * 16) + NE * 16)
                for a in range(2):
                    for t in range(NT):
                        q = a * NT + t
                        pool.wait_ge(used, r * (2 * NT) + max(q - 1, 0))
                        pool.sem_inc(go, 1)
                        pool.indirect_dma_start(
                            out=gx[:, q % 2], out_offset=None, in_=io["yg"][:, :],
                            in_offset=bass.IndirectOffsetOnAxis(ap=idx[:, 1, a, t:t + 1], axis=0),
                            bounds_check=NE * CAP - 1, oob_is_err=False).then_inc(gath[q % 2], 16)

        @block.scalar
        def _(act):
            R = rounds(act)
            with act.Fori(0, R) as r:
                def take_x(j, first):
                    for k in range(2):
                        v = r * (2 * NE + 2) + j * 2 + k + 1
                        act.wait_ge(t_done, v)
                        act.activation(xT_hi[:, 4 * k:4 * k + 4], T[k][:].rearrange("p (k c) -> p k c", c=P), ACT.Copy).then_inc(t_hi, 1)

                take_x(0, True)
                with act.Fori(0, NE) as e:
                    n = r * (3 * NE) + e * 3 + N0
                    q = r * NE + e

                    def hi(c, p):
                        if p in (0, 2):
                            free = (wts.used[p], n + c)
                        elif p == 1:
                            free = (y0_done, q) if c == 0 else (wts.used[1], q * 2 + USED1 + c)
                        else:
                            free = ((y1_done, q), (u_done, q + 1), (v_done, q + 1))[c]
                        wts.split_hi(act, n + c, p, free)

                    for p in range(4):
                        hi(0, p)
                    for p in range(3):
                        hi(1, p)
                    act.wait_ge(u_done, q + 1)
                    act.wait_ge(a_done, q)
                    act.activation(su[:], U[:], ACT.Silu).then_inc(su_done, 1)
                    hi(1, 3)
                    for p in range(3):
                        hi(2, p)
                    take_x(e + 1, False)
                    act.wait_ge(at_done, q + 1)
                    act.activation(aT_hi[:], AT[:].rearrange("p (k c) -> p k c", c=P), ACT.Copy).then_inc(at_hi, 1)
                    hi(2, 3)
                    for j in range(2):
                        act.wait_ge((y0_done, y1_done)[j], q + 1)
                        act.wait_ge(y_out, q * 16)
                        act.activation(yst[:, j * W:(j + 1) * W], Y[j][:], ACT.Copy).then_inc(y_taken, 1)
                    act.wait_ge(y_taken, q * 2 + 2)
                    act.dma_start(io["yg"][bass.ds(e * P, P), :], yst[:]).then_inc(y_out, 16)

        @block.vector
        def _(dve):
            R = rounds(dve)
            dve.memset(yacc[:], 0.0).then_inc(y_zero, 1)
            with dve.Fori(0, R) as r:
                NL = 7
                links = Links(dve, link, r * NL)

                def do(ins):
                    links(ins)
                    links.sync()

                ok, slot, inside, g = idf[:, 0], idf[:, 1], idf[:, 2], idf[:, 3]
                do(dve.tensor_scalar(ok, K.pos[:], 0.0, None, ALU.is_ge))
                do(dve.tensor_scalar(inside, K.pos[:], float(CAP), None, ALU.is_lt))
                do(dve.tensor_tensor(ok, ok, inside, ALU.mult))
                do(dve.scalar_tensor_tensor(slot, K.eid[:], float(CAP), K.pos[:], ALU.mult, ALU.add))
                do(dve.tensor_tensor(g, slot, ok, ALU.mult))
                do(dve.tensor_scalar(inside, ok, -BIG, BIG, ALU.mult, ALU.add))
                do(dve.tensor_tensor(inside, inside, g, ALU.add))
                dve.tensor_copy(idx[:, 0], inside).then_inc(idx_done, 1)
                dve.tensor_copy(idx[:, 1], g).then_inc(idx_done, 1)
                dve.tensor_tensor(wv[:], K.wgt[:], ok, ALU.mult).then_inc(idx_done, 1)
                dve.tensor_scalar(K.pos[:], K.pos[:], float(CAP), None, ALU.subtract).then_inc(idx_done, 1)

                def take_x(j):
                    for k in range(2):
                        v = r * (2 * NE + 2) + j * 2 + k + 1
                        dve.wait_ge(t_hi, v)
                        s = slice(4 * k, 4 * k + 4)
                        dve.tensor_tensor(xT_lo[:, s], T[k][:].rearrange("p (k c) -> p k c", c=P), xT_hi[:, s].bitcast(F32),
                                          ALU.subtract).then_inc(t_lo, 1)

                take_x(0)
                with dve.Fori(0, NE) as e:
                    n = r * (3 * NE) + e * 3 + N0
                    q = r * NE + e
                    for c in range(3):
                        if c == 2:
                            wts.split_lo(dve, n + c, 0)
                            dve.wait_ge(su_done, q + 1)
                            dve.wait_ge(v_done, q + 1)
                            dve.wait_ge(at_done, q)
                            dve.tensor_tensor(su[:], su[:], V[:], ALU.mult).then_inc(a_done, 1)
                            wts.split_lo(dve, n + c, 2)
                        else:
                            wts.split_lo(dve, n + c, 0)
                            wts.split_lo(dve, n + c, 2)
                    take_x(e + 1)
                    dve.wait_ge(at_hi, q + 1)
                    dve.tensor_tensor(aT_lo[:], AT[:].rearrange("p (k c) -> p k c", c=P), aT_hi[:].bitcast(F32), ALU.subtract) \
                       .then_inc(at_lo, 1)
                dve.wait_ge(y_zero, 1)
                for a in range(2):
                    for t in range(NT):
                        j = a * NT + t
                        dve.wait_ge(gath[j % 2], r * (NT * 16) + (j // 2 + 1) * 16)
                        dve.wait_ge(used, r * (2 * NT) + max(j - NT + 1, 0))
                        dve.scalar_tensor_tensor(yacc[:, t], gx[:, j % 2], wv[:, a, t:t + 1], yacc[:, t], ALU.mult, ALU.add).then_inc(used, 1)
                dve.wait_ge(used, r * (2 * NT) + 2 * NT)
                assert links.n == NL, links.n
            dve.wait_ge(gt2_in, 32)
            for t in range(NT):
                dve.tensor_tensor(yacc[:, t], yacc[:, t], gt2[:, kind(t)], ALU.mult).then_inc(added, 1)
                dve.wait_ge(added, t + 1)
                dve.tensor_tensor(yacc[:, t], yacc[:, t], K.x1[:, t], ALU.add).then_inc(fin, 1)

        @block.tensor
        def _(pe):
            R = rounds(pe)
            with pe.Fori(0, R) as r:
                def turn_x(j, k):
                    pe.wait_ge(xe_in, r * ((NE + 1) * 16) + j * 16 + 16)
                    pe.wait_ge(t_lo, r * (2 * NE + 2) + j * 2)
                    for a in range(4):
                        c = (4 * k + a) * P
                        last = pe.transpose(T[k][:, a * P:(a + 1) * P], xe[:, c:c + P], K.ident[:])
                    last.then_inc(t_done, 1)

                turn_x(0, 0)
                turn_x(0, 1)
                with pe.Fori(0, NE) as e:
                    n = r * (3 * NE) + e * 3 + N0
                    q = r * NE + e
                    pe.wait_ge(t_lo, r * (2 * NE + 2) + e * 2 + 2)
                    for c, (out, done) in enumerate(((U, u_done), (V, v_done))):
                        if c == 0:
                            pe.wait_ge(su_done, q)
                        else:
                            pe.wait_ge(a_done, q)
                        for p in range(4):
                            pe.wait_ge(wts.lo_done[p], n + c + 1)
                            for kk in range(2):
                                k = 2 * p + kk
                                last = mm3(pe, out[:], xT_hi[:, k], xT_lo[:, k], wts.hi[:, p, kk], wts.lo[:, p, kk], k == 0, k == KT - 1)
                            if p < 3:
                                last.then_inc(wts.used[p], 1)
                        last.then_inc(done, 1)
                    turn_x(e + 1, 0)
                    pe.wait_ge(a_done, q + 1)
                    pe.wait_ge(at_lo, q)
                    for a in range(4):
                        last = pe.transpose(AT[:, a * P:(a + 1) * P], su[:, a * P:(a + 1) * P], K.ident[:])
                    last.then_inc(at_done, 1)
                    turn_x(e + 1, 1)
                    pe.wait_ge(at_lo, q + 1)
                    pe.wait_ge(y_taken, q * 2)
                    for j in range(2):
                        for p in (2 * j, 2 * j + 1):
                            pe.wait_ge(wts.lo_done[p], n + 3)
                            for kk in range(2):
                                k = 2 * (p % 2) + kk
                                last = mm3(pe, Y[j][:], aT_hi[:, k], aT_lo[:, k], wts.hi[:, p, kk], wts.lo[:, p, kk], k == 0, k == 3)
                            if p % 2 == 0:
                                last.then_inc(wts.used[p], 1)
                        last.then_inc((y0_done, y1_done)[j], 1)


def constants():
    f = np.float32
    out = {"ident": np.eye(P, dtype=f)}
    sel = np.zeros((19, 2, P), f)
    for t in range(P):
        sel[0, 0, t] = sel[9, 0, t] = sel[18, 0, t] = 1
        b = t // DEC_L
        sel[1 + b, 1, t] = sel[10 + b, 1, t] = sel[18, 1, t] = 1
    out["sel"] = sel
    pos = np.concatenate([np.arange(SEQ), np.tile(PAST + np.arange(DEC_L), DEC_B)]).astype(f)
    for name, d in (("rope_ret", RDK), ("rope_diff", DDH)):
        inv = (f(10000.0) ** (-np.arange(0, d, 2, dtype=f) / f(d))).astype(f)
        ang = (pos[:, None] * inv[None, :]).astype(f)
        tab = np.stack([np.cos(ang), np.sin(ang)], 1).astype(f)
        out[name] = np.ascontiguousarray(tab.reshape(NT, P, 2, d // 2).transpose(1, 0, 2, 3))
    tab = np.zeros((RH, P, T_RET), np.float64)
    m = np.arange(P)
    for h in range(RH):
        lg = np.log1p(-np.exp2(-5.0 - h))
        c = np.arange(SEQ)
        rel = c[None, :] - m[:, None]
        tab[h, :, T_DEC:T_DEC + SEQ] = np.where(rel >= 0, np.exp(np.maximum(rel, 0) * lg), 0) / 16
        rel = m[None, :] - m[:, None]
        same = (m[None, :] // DEC_L) == (m[:, None] // DEC_L)
        tab[h, :, T_SMP:T_SMP + P] = np.where(same & (rel >= 0), np.exp(np.maximum(rel, 0) * lg), 0) / 16
        for t in range(NP_T):
            tab[h, :, T_KDEC + t] = np.exp((SEQ - 1 - t * P - m) * lg) / 16
        for b in range(DEC_B):
            tab[h, :, T_KMASK + b] = np.where(m // DEC_L == b, np.exp((DEC_L - 1 - m % DEC_L) * lg), 0) / 16
        tab[h, :, T_QDEC:T_QDEC + P] = np.exp((m % DEC_L + 1) * lg)[None, :]
    out["tab_ret"] = tab.astype(f)
    out["g16"] = np.tile(np.exp(DEC_L * np.log1p(-np.exp2(-5.0 - np.arange(RH)))).astype(f), (P, 1))
    ind = np.zeros((P, P), f)
    ind[0, 0:CHUNK] = ind[CHUNK, 0:CHUNK] = 1
    neg = np.zeros((P, CHUNK), f)
    neg[0] = neg[CHUNK] = NEG
    out["mask_p"] = np.concatenate([ind, neg], 1)
    one = np.zeros((P, P + DEC_B * P), f)
    one[0, 0:P] = 1
    for b in range(DEC_B):
        one[0, P + b * P:P + (b + 1) * P] = np.where(m // DEC_L == b, 0, NEG)
    out["mask_s"] = one
    out["csign"] = np.where((m // DEC_L) % 2 == 0, 1, 0).astype(f)[:, None]
    tri = (m[:, None] < m[None, :]).astype(f)
    out["ranks"] = np.concatenate([[4, 3, 2, 1], np.arange(N_EXP), CAP * np.arange(1, 5)]).astype(f)[None]
    out["tri"] = np.concatenate([tri, np.ones((P, P), f)], 1)
    return out


def setup(nc):
    K = type("K", (), {})()
    K.sbuf_end = nc.sbuf_usable_end if not callable(nc.sbuf_usable_end) else nc.sbuf_usable_end()
    base = nc.sbuf_base if not callable(nc.sbuf_base) else nc.sbuf_base()
    sb = Map(nc, (base + 31) // 32 * 32, K.sbuf_end)
    return K, sb


def program(nc, io, stop=None):
    with ExitStack() as ctx:
        K, sb = setup(nc)

        def semaphore(name):
            K.taken.append(nc.alloc_semaphore(name))
            return K.taken[-1]

        K.semaphore = semaphore
        K.ident = sb("ident", [P, P], F32)
        K.g16 = sb("g16", [P, RH], F32)
        K.wts = Weights(nc, ctx, sb)
        K.hT_at = sb.at
        K.hT_hi = sb("hT_hi", [P, KT, NT * P], F32R)
        K.hT_lo = sb("hT_lo", [P, KT, NT * P], F32R)
        K.phase_base = sb.at
        K.phase_base = sb.at
        for name, phase in (("A", phase_a), ("R", phase_r), ("D", phase_d), ("G", phase_g), ("M", phase_m)):
            K.taken = []
            phase(nc, io, K)
            if stop == name:
                break
            if name != "M":
                nc.clear_and_free_semaphores(K.taken)
                nc.all_engine_barrier()
        return K


INPUTS = ["x_prompt", "x_sample", "c_prompt", "c_sample", "cache_diff_k", "cache_diff_v", "state_ret", "w_ada", "b_ada",
          "norm1_g", "w_in", "diff_qnorm_g", "diff_knorm_g", "diff_lambda_q1", "diff_lambda_k1", "diff_lambda_q2",
          "diff_lambda_k2", "diff_subln_g", "w_br_ret", "w_br_diff", "w_out", "norm2_g", "w_group", "b_group",
          "w_expert_router", "b_expert", "w1", "w3", "w2"]
OUTPUTS = {"o_y_p": (1, SEQ, D_MODEL), "o_y_s": (DEC_B, DEC_L, D_MODEL), "o_k_p": (1, 1, SEQ, DH, 2 * DDH),
           "o_v_p": (1, 1, SEQ, DH, DDV), "o_state_p": (1, 1, RH, RDK, RDV), "o_k_s": (1, DEC_B, DEC_L, DH, 2 * DDH),
           "o_v_s": (1, DEC_B, DEC_L, DH, DDV), "o_state_s": (1, DEC_B, RH, RDK, RDV)}
SCRATCH = {"mods": (2, 4, P, D_MODEL), "acc_ret_d": (P, NT, D_MODEL), "xg": ((N_EXP + 1) * CAP, D_MODEL),
           "yg": (N_EXP * CAP, D_MODEL)}


def kernel(**inputs):
    import concourse.bacc as bacc
    from concourse.bass_utils import run_bass_kernel_spmd

    nc = bacc.Bacc("TRN2", target_bir_lowering=False, num_devices=1)
    arrays = {name: np.ascontiguousarray(inputs[name]) for name in INPUTS}
    arrays.update(constants())
    io = {name: nc.dram_tensor(name, a.shape, mybir.dt.from_np(a.dtype), kind="ExternalInput").ap() for name, a in arrays.items()}
    io.update({name: nc.dram_tensor(name, shape, F32, kind="ExternalOutput").ap() for name, shape in OUTPUTS.items()})
    io.update({name: nc.dram_tensor(name, shape, F32).ap() for name, shape in SCRATCH.items()})
    program(nc, io)
    got = run_bass_kernel_spmd(nc, [arrays], core_ids=[0]).results[0]
    return tuple(got[name] for name in OUTPUTS)
```

```python
import math
from contextlib import ExitStack
from typing import NamedTuple

import numpy as np

import concourse.bass as bass
from concourse import mybir

F32 = mybir.dt.float32
F32R = mybir.dt.float32r
I32 = mybir.dt.int32
U32 = mybir.dt.uint32
ALU = mybir.AluOpType
ACT = mybir.ActivationFunctionType
AX = mybir.AxisListType.X

P = 128
D_MODEL = 1024
SEQ = 512
DEC_B = 8
DEC_L = 16
PAST = 256
CHUNK = 64
EPS = 1e-6
NT = (SEQ + DEC_B * DEC_L) // P
NP_T = SEQ // P
KT = D_MODEL // P
RH, RDK, RDV = 4, 256, 512
DH, DDH, DDV = 8, 64, 128
LAM_INIT = 0.8 - 0.6 * math.exp(0.0)
N_EXP = 16
D_EXP = 512
CAP = P
IN_COLS = 11264
COL_RQ, COL_RK, COL_RV, COL_RG = 0, 1024, 2048, 4096
COL_DQ, COL_DK, COL_DV, COL_GATE = 6144, 7168, 8192, 9216
W = 512
NEG = -1e30

T_DEC, T_SMP, T_KDEC, T_KMASK, T_QDEC = 0, 512, 640, 644, 652
T_RET = 780


class Map:

    def __init__(self, nc, start, end):
        self.nc, self.at, self.end = nc, start, end

    def __call__(self, name, shape, dt, at=None):
        size = int(np.prod(shape[1:])) * 4
        off = self.at if at is None else at
        t = self.nc.alloc_sbuf_tensor_at(name, shape, dt, offset=off)
        if at is None:
            self.at += (size + 31) // 32 * 32
            assert self.at <= self.end, (name, self.at, self.end)
        return t


class Links:

    def __init__(self, eng, sem, base=0):
        self.eng, self.sem, self.base, self.n = eng, sem, base, 0

    def __call__(self, ins):
        self.n += 1
        ins.then_inc(self.sem, 1)

    def sync(self):
        self.eng.wait_ge(self.sem, self.base + self.n)


def mm3(pe, out, s_hi, s_lo, m_hi, m_lo, start, stop):
    pe.matmul(out, s_hi, m_hi, start=start, stop=False)
    pe.matmul(out, s_hi, m_lo, start=False, stop=False)
    return pe.matmul(out, s_lo, m_hi, start=False, stop=stop)


class Chunk(NamedTuple):

    n: int
    raw: object
    loaded: list
    loads: int
    back: int


class Weights:

    def __init__(self, nc, ctx, sb):
        self.raw = sb("w_raw", [P, 4, 2, W], F32)
        self.hi = sb("w_hi", [P, 4, 2, W], F32R)
        self.lo = sb("w_lo", [P, 4, 2, W], F32R)
        four = lambda name: [ctx.enter_context(nc.semaphore(f"{name}{p}")) for p in range(4)]
        self.loaded, self.hi_done, self.lo_done, self.used = map(four, ("w_loaded", "w_hi_done", "w_lo_done", "w_used"))

    def chunk(self, n):
        return n if isinstance(n, Chunk) else Chunk(n, self.raw, self.loaded, n, 1)

    def load(self, sp, n, pairs):
        c = self.chunk(n)
        for p, src in enumerate(pairs):
            sp.wait_ge(self.lo_done[p], c.n + 1 - c.back)
            sp.dma_start(c.raw[:, p], src).then_inc(c.loaded[p], 16)

    def split_hi(self, act, n, p, free):
        c = self.chunk(n)
        act.wait_ge(c.loaded[p], c.loads * 16 + 16)
        act.wait_ge(*free)
        act.activation(self.hi[:, p], c.raw[:, p], ACT.Copy).then_inc(self.hi_done[p], 1)

    def split_lo(self, eng, n, p):
        c = self.chunk(n)
        eng.wait_ge(self.hi_done[p], c.n + 1)
        eng.tensor_tensor(self.lo[:, p], c.raw[:, p], self.hi[:, p].bitcast(F32), ALU.subtract) \
           .then_inc(self.lo_done[p], 1)


def rows_of(w, c0):
    return [w[p * 256:(p + 1) * 256, bass.ds(c0, W)].rearrange("(k r) n -> r k n", k=2) for p in range(4)]


def halves_of(w, r0):
    return [w[bass.ds(r0 + q * 256, 256), j * W:(j + 1) * W].rearrange("(k r) n -> r k n", k=2)
            for j in range(2) for q in range(2)]


def project(pe, wts, n, banks, stat_hi, stat_lo, bank_free, group, done, tiles=NT, between=None):
    for p in range(4):
        if p == 3 and between:
            between()
        pe.wait_ge(wts.lo_done[p], n + 1)
        for kk in range(2):
            k = 2 * p + kk
            for t in range(tiles):
                if k == 0:
                    pe.wait_ge(bank_free[t], group + 1)
                s = slice(t * P, (t + 1) * P)
                last = mm3(pe, banks[t][:], stat_hi[:, k, s], stat_lo[:, k, s], wts.hi[:, p, kk], wts.lo[:, p, kk],
                           k == 0, k == KT - 1)
                if k == KT - 1:
                    last.then_inc(done, 1)
        if p < 3:
            last.then_inc(wts.used[p], 1)


def bc(ap, shape):
    return ap.broadcast_to(shape)


def rsqrt_steps(dve, links, out, var, std, tmp):
    links(dve.reciprocal(out, std))
    links.sync()
    links(dve.tensor_tensor(tmp, out, out, ALU.mult))
    links.sync()
    links(dve.tensor_tensor(tmp, tmp, var, ALU.mult))
    links.sync()
    links(dve.tensor_scalar(tmp, tmp, -0.5, 1.5, ALU.mult, ALU.add))
    links.sync()
    links(dve.tensor_tensor(out, out, tmp, ALU.mult))
    links.sync()


def phase_a(nc, io, K):
    wts = K.wts
    NCH = 12
    KEEP = 4
    with ExitStack() as ctx:
        sb = Map(nc, K.phase_base, K.sbuf_end)
        sem = lambda name: K.semaphore("a_" + name)
        x = sb("a_x", [P, NT, D_MODEL], F32)
        sq = sb("a_sq", [P, D_MODEL], F32)
        c9 = sb("a_c9", [9, D_MODEL], F32)
        c9s = sb("a_c9s", [9, D_MODEL], F32)
        cS = sb("a_cS", [P, KT, P], F32R)
        mod = sb("a_mod", [19, 6 * D_MODEL], F32)
        sel = sb("a_sel", [19, 2, P], F32)
        g = sb("a_g", [P, 2, D_MODEL], F32)
        m1 = sb("a_m1", [P, 2, 2, D_MODEL], F32)
        m2 = sb("a_m2", [P, 2, 4, D_MODEL], F32)
        st = sb("a_st", [P, 5, 8], F32)
        ps = [ctx.enter_context(nc.psum_tensor(f"a_ps{i}", [P, W], F32)) for i in range(8)]
        s_x, s_c, s_small = sem("x_in"), sem("c_in"), sem("small_in")
        silu_done, zero_done, cT_done, cT_hi, cT_split = map(sem, ("silu_done", "zero_done", "cT_done", "cT_hi", "cT_split"))
        mod_done, mod_copied, sel_done, sel_taken = map(sem, ("mod_done", "mod_copied", "sel_done", "sel_taken"))
        sumsq, var_done, std_done, h_done, hT_done, hi_done, lo_done = map(
            sem, ("sumsq", "var_done", "std_done", "h_done", "hT_done", "hT_hi_done", "hT_lo_done"))
        link, m_out = sem("dve_link"), sem("mods_out")
        block = ctx.enter_context(nc.Block())

        def kind(t):
            return 0 if t < NP_T else 1

        @block.sync
        def _(sp):
            sp.dma_start(c9[0:1], io["c_prompt"]).then_inc(s_c, 16)
            sp.dma_start(c9[1:9], io["c_sample"]).then_inc(s_c, 16)
            sp.dma_start(K.ident[:], io["ident"]).then_inc(s_small, 16)
            sp.dma_start(sel[:], io["sel"]).then_inc(s_small, 16)
            sp.dma_start(K.g16[:], io["g16"]).then_inc(s_small, 16)
            sp.dma_start(mod[18:19], io["b_ada"]).then_inc(s_small, 16)
            for i, name in enumerate(("norm1_g", "norm2_g")):
                sp.dma_start(g[:, i], io[name].broadcast_to([P, D_MODEL])) \
                  .then_inc(s_small, 16)
            for n in range(NCH):
                wts.load(sp, n, rows_of(io["w_ada"][0], n * W))
                if n == 1:
                    sp.dma_start(x[:, 0:NP_T], io["x_prompt"][0].rearrange("(t p) d -> p t d", p=P)).then_inc(s_x, 16)
                    sp.dma_start(x[:, NP_T], io["x_sample"].rearrange("b l d -> (b l) d")).then_inc(s_x, 16)
            sp.wait_ge(sel_taken, NCH * 2)
            sp.dma_start(io["mods"].rearrange("k m p d -> p k m d"), m2[:]).then_inc(m_out, 16)
            sp.wait_ge(m_out, 16)

        @block.gpsimd
        def _(pool):
            for n in range(NCH):
                for p in (1, 3):
                    wts.split_lo(pool, n, p)

        def copy_hT(q):
            act = nc.scalar
            act.wait_ge(hT_done, q + 1)
            t, half = q // 2, q % 2
            act.activation(K.hT_hi[:, 4 * half:4 * half + 4, t * P:(t + 1) * P],
                           ps[6 + q % 2][:].rearrange("p (k c) -> p k c", c=P), ACT.Copy).then_inc(hi_done, 1)

        @block.scalar
        def _(act):
            act.wait_ge(s_c, 32)
            act.activation(c9s[:], c9[:], ACT.Silu).then_inc(silu_done, 1)
            act.wait_ge(cT_done, 1)
            act.wait_ge(zero_done, 1)
            act.activation(cS[:, :, 0:9], ps[7][:, 0:72].rearrange("p (k c) -> p k c", c=9), ACT.Copy).then_inc(cT_hi, 1)

            def take_mod(n):
                act.wait_ge(mod_done, n + 1)
                act.activation(mod[0:18, n * W:(n + 1) * W], ps[n % 2][0:18], ACT.Copy).then_inc(mod_copied, 1)

            for n in range(NCH):
                wts.split_hi(act, n, 0, (wts.used[0], n))
                wts.split_hi(act, n, 1, (wts.used[1], n))
                if n:
                    take_mod(n - 1)
                wts.split_hi(act, n, 2, (wts.used[2], n))
                wts.split_hi(act, n, 3, (mod_done, n))
                if n == 3:
                    act.wait_ge(s_x, 32)
                    for t in range(NT):
                        if t:
                            act.wait_ge(sumsq, t)
                        act.activation(sq[:], x[:, t], ACT.Square, accum_out=st[:, 0, t:t + 1]).then_inc(sumsq, 1)
                if n == 4:
                    act.wait_ge(var_done, 1)
                    act.activation(st[:, 2, 0:NT], st[:, 1, 0:NT], ACT.Sqrt).then_inc(std_done, 1)
                if n >= 8:
                    for q in range(2 * (n - 8), 2 * (n - 8) + 2):
                        copy_hT(q)
            take_mod(NCH - 1)
            for q in (8, 9):
                copy_hT(q)

        @block.vector
        def _(dve):
            links = Links(dve, link)
            dve.memset(cS[:].bitcast(F32), 0.0).then_inc(zero_done, 1)

            def take_sel(n):
                seg, half = n // 2, n % 2
                cols = slice(half * W, (half + 1) * W)
                for kd in range(2):
                    dve.wait_ge(sel_done, 2 * n + kd + 1)
                    dst = m1[:, kd, seg, cols] if seg < 2 else m2[:, kd, seg - 2, cols]
                    src = ps[2 + (n % 2) * 2 + kd][:]
                    if seg in (1, 4):
                        ins = dve.scalar_tensor_tensor(dst, src, 1.0, g[:, 0 if seg == 1 else 1, cols], ALU.add, ALU.mult)
                    else:
                        ins = dve.tensor_copy(dst, src)
                    ins.then_inc(sel_taken, 1)

            def split_hT(q):
                dve.wait_ge(hi_done, q + 1)
                t, half = q // 2, q % 2
                s = (slice(None), slice(4 * half, 4 * half + 4), slice(t * P, (t + 1) * P))
                dve.tensor_tensor(K.hT_lo[s], ps[6 + q % 2][:].rearrange("p (k c) -> p k c", c=P),
                                  K.hT_hi[s].bitcast(F32), ALU.subtract).then_inc(lo_done, 1)

            def norm(t):
                if t == 0:
                    dve.wait_ge(std_done, 1)
                    rsqrt_steps(dve, links, st[:, 3, 0:NT], st[:, 1, 0:NT], st[:, 2, 0:NT], st[:, 4, 0:NT])
                    dve.wait_ge(sel_taken, 2 * KEEP)
                links(dve.scalar_tensor_tensor(x[:, t], x[:, t], st[:, 3, t:t + 1], m1[:, kind(t), 1], ALU.mult, ALU.mult))
                links.sync()
                dve.tensor_tensor(x[:, t], x[:, t], m1[:, kind(t), 0], ALU.add).then_inc(h_done, 1)

            for n in range(NCH):
                if n == 0:
                    dve.wait_ge(cT_hi, 1)
                    dve.tensor_tensor(cS[:, :, 9:18], ps[7][:, 0:72].rearrange("p (k c) -> p k c", c=9),
                                      cS[:, :, 0:9].bitcast(F32), ALU.subtract).then_inc(cT_split, 1)
                    dve.wait_ge(s_small, 6 * 16)
                wts.split_lo(dve, n, 0)
                wts.split_lo(dve, n, 2)
                if n:
                    take_sel(n - 1)
                if n == 3:
                    dve.wait_ge(sumsq, NT)
                    dve.tensor_scalar(st[:, 1, 0:NT], st[:, 0, 0:NT], 1.0 / D_MODEL, EPS, ALU.mult, ALU.add).then_inc(var_done, 1)
                if 5 <= n < 5 + NT:
                    norm(n - 5)
                if n >= 8:
                    for q in range(2 * (n - 8), 2 * (n - 8) + 2):
                        split_hT(q)
            take_sel(NCH - 1)
            for q in (8, 9):
                split_hT(q)

        @block.tensor
        def _(pe):
            pe.wait_ge(s_small, 6 * 16)
            pe.wait_ge(silu_done, 1)
            for k in range(KT):
                last = pe.transpose(ps[7][:, 9 * k:9 * k + 9], c9s[:, k * P:(k + 1) * P], K.ident[0:9, 0:9])
            last.then_inc(cT_done, 1)
            pe.wait_ge(cT_split, 1)
            def spread(m):
                pe.wait_ge(mod_copied, m + 1)
                if m >= 2:
                    pe.wait_ge(sel_taken, 2 * (m - 1))
                for kd in range(2):
                    pe.matmul(ps[2 + (m % 2) * 2 + kd][:], sel[:, kd], mod[:, m * W:(m + 1) * W],
                              start=True, stop=True).then_inc(sel_done, 1)

            for n in range(NCH + 1):
                if n < NCH:
                    for p in range(4):
                        if n and p == 2:
                            spread(n - 1)
                        pe.wait_ge(wts.lo_done[p], n + 1)
                        if p == 0 and n >= 2:
                            pe.wait_ge(mod_copied, n - 1)
                        for kk in range(2):
                            k = 2 * p + kk
                            pe.matmul(ps[n % 2][:], cS[:, k, :], wts.hi[:, p, kk], start=(k == 0), stop=False)
                            last = pe.matmul(ps[n % 2][:], cS[:, k, :], wts.lo[:, p, kk], start=False, stop=(k == KT - 1))
                        if p < 3:
                            last.then_inc(wts.used[p], 1)
                    last.then_inc(mod_done, 1)
                else:
                    spread(NCH - 1)
                if 7 <= n < 7 + NT:
                    t = n - 7
                    pe.wait_ge(h_done, t + 1)
                    for half in range(2):
                        q = 2 * t + half
                        if q >= 2:
                            pe.wait_ge(lo_done, q - 1)
                        for j in range(4):
                            k = 4 * half + j
                            last = pe.transpose(ps[6 + q % 2][:, j * P:(j + 1) * P], x[:, t, k * P:(k + 1) * P], K.ident[:])
                        last.then_inc(hT_done, 1)


def phase_r(nc, io, K):
    wts = K.wts
    N0 = 12
    G = 6
    J = 33
    J_T, J_SC, J_ST, J_UP, J_OT = 0, 5, 10, 12, 28
    UN = 2 * DEC_B
    SLOTS = 4
    NLINK = 20
    scoff = [0, 512, 896, 1152, 1280]
    with ExitStack() as ctx:
        sb = Map(nc, K.phase_base, K.sbuf_end)
        sem = lambda name: K.semaphore("r_" + name)
        K.acc_ret = sb("acc_ret", [P, NT, D_MODEL], F32)
        K.after_acc_ret = sb.at
        rope = sb("r_rope", [P, NT, 2, P], F32)
        tab = sb("r_tab", [P, T_RET], F32)
        qk = sb("r_qk", [P, NT, 2, RDK], F32)
        tmp = sb("r_tmp", [P, 2, W], F32)
        qkT = sb("r_qkT", [P, 4, NT * P], F32)
        v = sb("r_v", [P, NT, RDV], F32)
        gate = sb("r_gate", [P, NT, RDV], F32)
        scT = sb("r_scT", [P, 1280 + P], F32)
        oT_hi = sb("r_oT_hi", [P, 4, NT * P], F32R)
        oT_lo = sb("r_oT_lo", [P, 4, NT * P], F32R)
        qz = sb("r_qz", [P, DEC_B, P], F32)
        kz = sb("r_kz", [P, DEC_B, P], F32)
        S = sb("r_S", [P, SLOTS, RDV], F32)
        S_p = sb("r_S_p", [P, RDV], F32)
        S_sq = sb("r_squares", [P, RDV], F32)
        st = sb("r_st", [P, 5, 8], F32)
        pj = [ctx.enter_context(nc.psum_tensor(f"r_pj{i}", [P, W], F32)) for i in range(NT)]
        sm = [ctx.enter_context(nc.psum_tensor(f"r_sm{i}", [P, W], F32)) for i in range(3)]
        many = lambda name, n: [sem(f"{name}{i}") for i in range(n)]
        tab_in, rope_in, S_in, S_out, Sp_out = sem("tab_in"), sem("rope_in"), many("S_in", SLOTS), many("S_out", SLOTS), sem("Sp_out")
        xg_zero, acc_zero = sem("xg_zero"), sem("acc_zero")
        pj_done, pj_free, sm_done, sm_free = sem("pj_done"), many("pj_free", NT), sem("sm_done"), many("sm_free", 3)
        qk_roped, kd_done, z_done, qz_set = map(sem, ("qk_roped", "kd_done", "z_done", "qz_set"))
        sumsq, var_done, std_done, oT_hi_done, link = map(sem, ("sumsq", "var_done", "std_done", "oT_hi_done", "dve_link"))
        k_loaded = many("k_loaded", 4)
        K.start_at_one(*S_out, Sp_out, pj_done, *pj_free, qk_roped, sm_done, *sm_free, sumsq)
        block = ctx.enter_context(nc.Block())
        w_in = io["w_in"][0]

        def sm_bank(n):
            return sm[n % 3]

        def sm_taken(eng, h, job):
            eng.wait_ge(sm_free[job % 3], h * (J // 3) + job // 3 + 1 + 1)

        def pj_taken(eng, h, g, t):
            eng.wait_ge(pj_free[t], h * G + g + 1 + 1)

        @block.sync
        def _(sp):
            sp.dma_start(rope[:], io["rope_ret"]).then_inc(rope_in, 16)
            with sp.Fori(0, RH) as h:
                sp.wait_ge(sm_done, h * J + 1)
                sp.dma_start(tab[:], io["tab_ret"][bass.ds(h, 1)].rearrange("a p c -> (a p) c")).then_inc(tab_in, 16)
                q_cols, k_cols = (w_in[:, bass.ds(h * RDK + c, RDK)].rearrange("(p k r) n -> p r k n", k=2, r=P)
                                  for c in (COL_RQ, COL_RK))
                for p in range(4):
                    sp.wait_ge(wts.lo_done[p], h * 4 + N0)
                    sp.dma_start(wts.raw[:, p, :, 0:RDK], q_cols[p]).then_inc(wts.loaded[p], 16)
                    sp.dma_start(wts.raw[:, p, :, RDK:W], k_cols[p]).then_inc(k_loaded[p], 16)
                wts.load(sp, h * 4 + N0 + 1, rows_of(w_in, h * RDV + COL_RV))
                wts.load(sp, h * 4 + N0 + 2, rows_of(w_in, h * RDV + COL_RG))
                wts.load(sp, h * 4 + N0 + 3, halves_of(io["w_br_ret"][0], h * RDV))
                for u in range(UN):
                    d, b = u // DEC_B, u % DEC_B
                    sp.wait_ge(S_out[u % SLOTS], h * (UN // SLOTS * 16) + 16 * (u // SLOTS) + 1)
                    sp.dma_start(S[:, u % SLOTS], io["state_ret"][0, b, bass.ds(h, 1), d * P:(d + 1) * P, :]
                                 .rearrange("a p c -> (a p) c")).then_inc(S_in[u % SLOTS], 16)

        @block.gpsimd
        def _(pool):
            pool.memset(qz[:], 0.0).then_inc(qz_set, 1)
            pool.wait_ge(qz_set, 1)
            with pool.Fori(0, RH) as h:
                for c in range(3):
                    for p in range(4):
                        wts.split_lo(pool, h * 4 + N0 + c, p)
                pool.wait_ge(tab_in, h * 16 + 16)
                pool.wait_ge(sm_done, h * J + J_T + NT + 1)
                for t in range(NP_T):
                    pool.tensor_tensor(qk[:, t, 1], qk[:, t, 1], bc(tab[:, T_KDEC + t:T_KDEC + t + 1], [P, RDK]), ALU.mult) \
                        .then_inc(kd_done, 1)
                sm_taken(pool, h, J_T + NP_T)
                for d in range(2):
                    pool.wait_ge(sm_done, h * J + (J_UP + DEC_B) * d + 1)
                    diag = qz[:].rearrange("p b c -> p (b c)")[:, 0:DEC_B * P]
                    diag = bass.AP(tensor=diag.tensor, offset=diag.offset, ap=[list(diag.ap[0]), [P + DEC_L, DEC_B], [1, DEC_L]])
                    pool.tensor_tensor(diag, qkT[:, d, NP_T * P:NT * P].rearrange("p (b l) -> p b l", l=DEC_L),
                                       tab[:, T_QDEC:T_QDEC + P].rearrange("p (b l) -> p b l", l=DEC_L), ALU.mult).then_inc(z_done, 1)
                    last = pool.tensor_tensor(kz[:], bc(qk[:, NP_T, 1, d * P:(d + 1) * P].unsqueeze(1), [P, DEC_B, P]),
                                              bc(tab[:, T_KMASK:T_KMASK + DEC_B].unsqueeze(2), [P, DEC_B, P]), ALU.mult)
                    last.then_inc(z_done, 1)
                for p in range(4):
                    wts.split_lo(pool, h * 4 + N0 + 3, p)

        @block.scalar
        def _(act):
            act.wait_ge(acc_zero, 1)
            for e in range(N_EXP):
                act.dma_start(io["xg"][e * CAP:(e + 1) * CAP, :], K.acc_ret[:, 0]).then_inc(xg_zero, 16)
            with act.Fori(0, RH) as h:
                n = lambda c: h * 4 + N0 + c

                def hi(c, p):
                    if c == 0:
                        act.wait_ge(k_loaded[p], h * 16 + 16)
                    if p in (0, 2):
                        free = (wts.used[p], n(c))
                    elif p == 1 and c > 0:
                        free = (wts.used[1], h * 3 + N0 + c)
                    else:
                        free = (pj_done, h * (G * NT) + c * NT + 1)
                    wts.split_hi(act, n(c), p, free)

                def take(g, dst, func):
                    for t in range(NT):
                        act.wait_ge(pj_done, h * (G * NT) + g * NT + t + 1 + 1)
                        act.activation(dst(t), pj[t][:], func).then_inc(pj_free[t], 1)

                def sums(ts):
                    for t in ts:
                        act.wait_ge(pj_done, h * (G * NT) + 3 * NT + t + 1 + 1)
                        act.wait_ge(sumsq, h * NT + t + 1)
                        act.activation(S_sq[:], pj[t][:], ACT.Square, accum_out=st[:, 0, t:t + 1]).then_inc(sumsq, 1)

                def roots(a, b, i):
                    act.wait_ge(var_done, h * 2 + i + 1)
                    act.activation(st[:, 2, a:b], st[:, 1, a:b], ACT.Sqrt).then_inc(std_done, 1)

                for p in range(4):
                    hi(0, p)
                for p in range(3):
                    hi(1, p)
                take(0, lambda t: qk[:, t].rearrange("p a c -> p (a c)"), ACT.Copy)
                hi(1, 3)
                for p in range(3):
                    hi(2, p)
                take(1, lambda t: v[:, t], ACT.Copy)
                hi(2, 3)
                for p in range(3):
                    hi(3, p)
                take(2, lambda t: gate[:, t], ACT.Silu)
                hi(3, 3)
                sums(range(NP_T))
                roots(0, NP_T, 0)
                for d in range(2):
                    act.wait_ge(sm_done, h * J + J_ST + d + 1 + 1)
                    act.wait_ge(Sp_out, h * 32 + 16 * d + 1)
                    act.activation(S_p[:], sm_bank(J_ST + d)[:], ACT.Copy).then_inc(sm_free[(J_ST + d) % 3], 1)
                    sm_taken(act, h, J_ST + d)
                    act.dma_start(io["o_state_p"][0, 0, bass.ds(h, 1), d * P:(d + 1) * P, :].rearrange("a p c -> (a p) c"),
                                  S_p[:]).then_inc(Sp_out, 16)
                for u in range(UN):
                    d, b = u // DEC_B, u % DEC_B
                    sm_taken(act, h, J_UP + u)
                    act.dma_start(io["o_state_s"][0, b, bass.ds(h, 1), d * P:(d + 1) * P, :].rearrange("a p c -> (a p) c"),
                                  S[:, u % SLOTS]).then_inc(S_out[u % SLOTS], 16)
                sums([NP_T])
                roots(NP_T, NT, 1)
                for t in range(NT):
                    act.wait_ge(sm_done, h * J + J_OT + t + 1 + 1)
                    act.activation(oT_hi[:, :, t * P:(t + 1) * P], sm_bank(J_OT + t)[:].rearrange("p (k c) -> p k c", c=P),
                                   ACT.Copy).then_inc(oT_hi_done, 1)
            act.wait_ge(Sp_out, RH * 32 + 1)
            for s in range(SLOTS):
                act.wait_ge(S_out[s], RH * (UN // SLOTS) * 16 + 1)

        @block.vector
        def _(dve):
            dve.memset(K.acc_ret[:], 0.0).then_inc(acc_zero, 1)
            dve.wait_ge(rope_in, 16)
            with dve.Fori(0, RH) as h:
                links = Links(dve, link, h * NLINK)
                for t in range(NT):
                    pj_taken(dve, h, 0, t)
                    x = qk[:, t].rearrange("p a (e c) -> p (a e) c", e=2)
                    cos = bc(rope[:, t, 0].unsqueeze(1), [P, 4, P])
                    sin = bc(rope[:, t, 1].unsqueeze(1), [P, 4, P])
                    t1 = tmp[:, 0].rearrange("p (a e c) -> p a e c", a=2, e=2)
                    t2 = tmp[:, 1].rearrange("p (a e c) -> p a e c", a=2, e=2)
                    xx = qk[:, t].rearrange("p a (e c) -> p a e c", e=2)
                    dve.wait_ge(qk_roped, h * NT + t + 1)
                    links(dve.tensor_tensor(tmp[:, 0].rearrange("p (a c) -> p a c", a=4), x, cos, ALU.mult))
                    links(dve.tensor_tensor(tmp[:, 1].rearrange("p (a c) -> p a c", a=4), x, sin, ALU.mult))
                    links.sync()
                    dve.tensor_tensor(xx[:, :, 0], t1[:, :, 0], t2[:, :, 1], ALU.subtract)
                    dve.tensor_tensor(xx[:, :, 1], t1[:, :, 1], t2[:, :, 0], ALU.add).then_inc(qk_roped, 1)
                for t in range(NT):
                    dve.wait_ge(sm_done, h * J + J_T + t + 1 + 1)
                    dve.tensor_copy(qkT[:, :, t * P:(t + 1) * P], sm_bank(J_T + t)[:].rearrange("p (k c) -> p k c", c=P)) \
                       .then_inc(sm_free[(J_T + t) % 3], 1)
                dve.wait_ge(tab_in, h * 16 + 16)
                for j in range(NT):
                    n = scoff[j + 1] - scoff[j] if j < NP_T else P
                    c0 = T_DEC if j < NP_T else T_SMP
                    dve.wait_ge(sm_done, h * J + J_SC + j + 1 + 1)
                    dve.tensor_tensor(scT[:, scoff[j]:scoff[j] + n], sm_bank(J_SC + j)[:, 0:n], tab[:, c0:c0 + n], ALU.mult) \
                       .then_inc(sm_free[(J_SC + j) % 3], 1)

                def variance(a, b):
                    dve.wait_ge(sumsq, h * NT + b + 1)
                    dve.tensor_scalar(st[:, 1, a:b], st[:, 0, a:b], 1.0 / RDV, EPS, ALU.mult, ALU.add).then_inc(var_done, 1)

                def gated(ts, i):
                    dve.wait_ge(std_done, h * 2 + i + 1)
                    a, b = ts[0], ts[-1] + 1
                    rsqrt_steps(dve, links, st[:, 3, a:b], st[:, 1, a:b], st[:, 2, a:b], st[:, 4, a:b])
                    for t in ts:
                        pj_taken(dve, h, 2, t)
                        dve.scalar_tensor_tensor(gate[:, t], pj[t][:], st[:, 3, t:t + 1], gate[:, t], ALU.mult, ALU.mult) \
                           .then_inc(pj_free[t], 1)

                variance(0, NP_T)
                gated(list(range(NP_T)), 0)
                for u in range(UN):
                    dve.wait_ge(sm_done, h * J + J_UP + u + 1 + 1)
                    dve.scalar_tensor_tensor(S[:, u % SLOTS], S[:, u % SLOTS], K.g16[:, bass.ds(h, 1)], sm_bank(J_UP + u)[:],
                                             ALU.mult, ALU.add).then_inc(sm_free[(J_UP + u) % 3], 1)
                variance(NP_T, NT)
                gated([NP_T], 1)
                for t in range(NT):
                    dve.wait_ge(oT_hi_done, h * NT + t + 1)
                    s = (slice(None), slice(None), slice(t * P, (t + 1) * P))
                    dve.tensor_tensor(oT_lo[s], sm_bank(J_OT + t)[:].rearrange("p (k c) -> p k c", c=P),
                                      oT_hi[s].bitcast(F32), ALU.subtract).then_inc(sm_free[(J_OT + t) % 3], 1)
                dve.wait_ge(acc_zero, 1)
                dve.wait_ge(xg_zero, 16 * N_EXP)
                for j in range(2):
                    for t in range(NT):
                        dve.wait_ge(pj_done, h * (G * NT) + (4 + j) * NT + t + 1 + 1)
                        a = K.acc_ret[:, t, j * W:(j + 1) * W]
                        dve.tensor_tensor(a, a, pj[t][:], ALU.add).then_inc(pj_free[t], 1)
                assert links.n == NLINK, links.n

        @block.tensor
        def _(pe):
            with pe.Fori(0, RH) as h:
                n = lambda c: h * 4 + N0 + c
                group = lambda g: h * G + g

                def small(job):
                    pe.wait_ge(sm_free[job % 3], h * (J // 3) + job // 3 + 1)
                    return sm_bank(job)

                hT = (K.hT_hi, K.hT_lo)
                project(pe, wts, n(0), pj, *hT, pj_free, group(0), pj_done)
                project(pe, wts, n(1), pj, *hT, pj_free, group(1), pj_done)
                for t in range(NT):
                    pe.wait_ge(qk_roped, h * NT + t + 1 + 1)
                    out = small(J_T + t)
                    for a in range(4):
                        last = pe.transpose(out[:, a * P:(a + 1) * P], qk[:, t, a // 2, (a % 2) * P:(a % 2 + 1) * P], K.ident[:])
                    last.then_inc(sm_done, 1)
                project(pe, wts, n(2), pj, *hT, pj_free, group(2), pj_done)
                for t in (2, 3, 4):
                    sm_taken(pe, h, J_T + t)
                for j in range(NT):
                    out = small(J_SC + j)
                    ke = slice(j * P, (j + 1) * P)
                    qs = slice(j * P, SEQ) if j < NP_T else ke
                    w = qs.stop - qs.start
                    for d in range(2):
                        last = pe.matmul(out[:, 0:w], qkT[:, 2 + d, ke], qkT[:, d, qs], start=(d == 0), stop=(d == 1))
                    last.then_inc(sm_done, 1)
                for i in range(NP_T):
                    pe.wait_ge(pj_free[i], group(3) + 1)
                    for j in range(i + 1):
                        pj_taken(pe, h, 1, j)
                        sm_taken(pe, h, J_SC + j)
                        c = scoff[j] + (i - j) * P
                        last = pe.matmul(pj[i][:], scT[:, c:c + P], v[:, j], start=(j == 0), stop=(j == i))
                    last.then_inc(pj_done, 1)
                pe.wait_ge(kd_done, h * NP_T + NP_T)
                for d in range(2):
                    out = small(J_ST + d)
                    for t in range(NP_T):
                        last = pe.matmul(out[:], qk[:, t, 1, d * P:(d + 1) * P], v[:, t], start=(t == 0), stop=(t == NP_T - 1))
                    last.then_inc(sm_done, 1)
                pe.wait_ge(pj_free[NP_T], group(3) + 1)
                pj_taken(pe, h, 1, NP_T)
                sm_taken(pe, h, J_SC + NP_T)
                pe.matmul(pj[NP_T][:], scT[:, scoff[4]:scoff[4] + P], v[:, NP_T], start=True, stop=False)
                for u in range(UN):
                    d, b = u // DEC_B, u % DEC_B
                    if b == 0:
                        pe.wait_ge(z_done, h * 4 + 2 * d + 2)
                    pe.wait_ge(S_in[u % SLOTS], h * (UN // SLOTS * 16) + 16 * (u // SLOTS) + 16)
                    o = pe.matmul(pj[NP_T][:], qz[:, b], S[:, u % SLOTS], start=False, stop=(u == UN - 1))
                    if u == UN - 1:
                        o.then_inc(pj_done, 1)
                    out = small(J_UP + u)
                    last = pe.matmul(out[:], kz[:, b], v[:, NP_T], start=True, stop=True)
                    last.then_inc(sm_done, 1)
                for t in range(NT):
                    pj_taken(pe, h, 3, t)
                    out = small(J_OT + t)
                    for a in range(4):
                        last = pe.transpose(out[:, a * P:(a + 1) * P], gate[:, t, a * P:(a + 1) * P], K.ident[:])
                    last.then_inc(sm_done, 1)
                branch(pe, wts, n(3), pj, oT_hi, oT_lo, lambda t: sm_taken(pe, h, J_OT + t), pj_free, group(4), pj_done)


def branch(pe, wts, n, banks, hi, lo, stands, bank_free, group, done):
    for j in range(2):
        for p in (2 * j, 2 * j + 1):
            pe.wait_ge(wts.lo_done[p], n + 1)
            for kk in range(2):
                k = 2 * (p % 2) + kk
                for t in range(NT):
                    if k == 0:
                        pe.wait_ge(bank_free[t], group + j + 1)
                        stands(t)
                    s = slice(t * P, (t + 1) * P)
                    last = mm3(pe, banks[t][:], hi[:, k, s], lo[:, k, s], wts.hi[:, p, kk], wts.lo[:, p, kk], k == 0, k == 3)
                    if k == 3:
                        last.then_inc(done, 1)
            if k == 1:
                last.then_inc(wts.used[p], 1)


def phase_d(nc, io, K):
    wts = K.wts
    N0, USED1 = 28, 24
    G = 5
    HH = 4
    U = NP_T * HH
    NJ = 2 * NT
    SCALE = DDH ** -0.5
    KEYS = PAST + P
    NLINK = 2 * (5 + 3 * NT) + 4 * U + 3 * DEC_B + 2 * (5 + NT)
    with ExitStack() as ctx:
        sem = lambda name: K.semaphore("d_" + name)
        many = lambda name, n: [sem(f"{name}{i}") for i in range(n)]
        sb = Map(nc, K.phase_base, K.after_acc_ret)
        kc = sb("d_kc", [P, 2, 2, W], F32)
        vc = sb("d_vc", [P, 2, 2, W], F32)
        kcT = sb("d_kcT", [P, HH, PAST], F32)
        sb = Map(nc, K.after_acc_ret, K.sbuf_end)
        K.acc_diff = sb("acc_diff", [P, NT, D_MODEL], F32)
        K.after_accs = sb.at
        at_T = sb.at
        qT = sb("d_qT", [P, HH, NT * P], F32)
        kT = sb("d_kT", [P, HH, NT * P], F32)
        oT_hi = sb("d_oT_hi", [P, HH, NT * P], F32R, at=at_T)
        oT_lo = sb("d_oT_lo", [P, HH, NT * P], F32R, at=at_T + HH * NT * P * 4)
        stage = sb("d_stage", [P, NT, W], F32)
        v = sb("d_v", [P, NT, W], F32)
        at_tmp = sb.at
        tmp = sb("d_tmp", [P, 2, W], F32)
        qB = sb("d_qB", [P, 2, HH, P], F32, at=at_tmp)
        Pr = sb("d_P", [P, 4, W], F32)
        AT = sb("d_AT", [P, 2, HH, P], F32)
        Ps = sb("d_Ps", [P, 2, KEYS], F32)
        ATs = sb("d_ATs", [P, 2, 12, DEC_L], F32)
        oTs = sb("d_oTs", [P, W], F32)
        rope = sb("d_rope", [P, NT, 2, 32], F32)
        tabs = sb("d_tabs", [P, 2, NT, 2, DDH], F32)
        gains = sb("d_gains", [P, 2, DDH], F32)
        gsub = sb("d_gsub", [P, DDV], F32)
        lv = sb("d_lv", [P, 4, DDH], F32)
        lam = sb("d_lam", [P, 8], F32)
        mp = sb("d_mask_p", [P, P + CHUNK], F32)
        ms = sb("d_mask_s", [P, P + DEC_B * P], F32)
        st = sb("d_st", [P, 5, NT * 8], F32)
        sm = sb("d_sm", [P, 2, 8], F32)
        sms = sb("d_sms", [P, 2, 8], F32)
        B = [ctx.enter_context(nc.psum_tensor(f"d_B{i}", [P, W], F32)) for i in range(8)]
        pj = B[0:NT]
        const_in, spilled, kc_in, vc_in = sem("const_in"), sem("acc_ret_spilled"), many("kc_in", 2), many("vc_in", 2)
        krow_out, vrow_out, go = sem("krow_out"), sem("vrow_out"), sem("sync_goes_on")
        pj_done, pj_free = sem("pj_done"), many("pj_free", NT)
        squared, reduced, var_done, std_done, roped = map(sem, ("squared", "reduced", "var_done", "std_done", "roped"))
        qkT_done, qkT_taken = map(sem, ("qkT_done", "qkT_taken"))
        s_done, nmax_done, exp_done, A_done, at_done, at_taken, pv_done, o_taken = map(
            sem, ("s_done", "nmax_done", "exp_done", "A_done", "at_done", "at_taken", "pv_done", "o_taken"))
        kcT_done, kcT_taken, qB_zero, qB_done, ss_done, snmax_done, sexp_done, sA_done, sat_done, sat_taken, spv_done = map(
            sem, ("kcT_done", "kcT_taken", "qB_zero", "qB_done", "ss_done", "snmax_done", "sexp_done", "sA_done",
                  "sat_done", "sat_taken", "spv_done"))
        oTs_done, o4_done, osq, dn_done, ot_done, ot_hi, ot_lo, link, lam_exp, lam_sum, acc_zero = map(
            sem, ("oTs_done", "o4_done", "o_squared", "dn_done", "ot_done", "ot_hi", "ot_lo", "dve_link", "lam_exp", "lam_sum", "acc_zero"))
        K.start_at_one(at_done, kcT_done, kcT_taken, osq, pj_done, *pj_free, pv_done, reduced, roped, sat_done, spv_done, ss_done, vrow_out)
        block = ctx.enter_context(nc.Block())
        w_in = io["w_in"][0]

        def slot_wait(eng, s, i, per, u):
            eng.wait_ge(s, i * per + max(u - 1, 0) + 1)

        @block.sync
        def _(sp):
            sp.dma_start(io["acc_ret_d"], K.acc_ret[:]).then_inc(spilled, 16)
            sp.dma_start(rope[:], io["rope_diff"]).then_inc(const_in, 16)
            sp.dma_start(gains[:, 0], io["diff_qnorm_g"].broadcast_to([P, DDH])).then_inc(const_in, 16)
            sp.dma_start(gains[:, 1], io["diff_knorm_g"].broadcast_to([P, DDH])).then_inc(const_in, 16)
            sp.dma_start(gsub[:], io["diff_subln_g"].broadcast_to([P, DDV])).then_inc(const_in, 16)
            for j, name in enumerate(("q1", "k1", "q2", "k2")):
                sp.dma_start(lv[:, j], io["diff_lambda_" + name].broadcast_to([P, DDH])).then_inc(const_in, 16)
            sp.dma_start(mp[:], io["mask_p"]).then_inc(const_in, 16)
            sp.dma_start(ms[:], io["mask_s"]).then_inc(const_in, 16)
            sp.dma_start(lam[:, 5:6], io["csign"]).then_inc(const_in, 16)
            with sp.Fori(0, 2) as i:
                n = lambda c: i * 4 + N0 + c
                wts.load(sp, n(0), rows_of(w_in, i * W + COL_DQ))
                wts.load(sp, n(1), rows_of(w_in, i * W + COL_DK))
                wts.load(sp, n(2), rows_of(w_in, i * W + COL_DV))
                wts.load(sp, n(3), halves_of(io["w_br_diff"][0], i * W))
                for b in range(DEC_B):
                    s = b % 2
                    cache = lambda ap: ap[0, b].rearrange("l h d -> l (h d)")[:, bass.ds(i * W, W)].rearrange("(k p) c -> p k c", p=P)
                    sp.wait_ge(kcT_done, (i * DEC_B + max(b - 1, 0)) * 2 + 1)
                    if b == 0:
                        sp.sem_inc(go, 1)
                        sp.wait_ge(spilled, 16)
                    sp.dma_start(kc[:, s], cache(io["cache_diff_k"])).then_inc(kc_in[s], 16)
                    slot_wait(sp, spv_done, i, DEC_B, b)
                    sp.dma_start(vc[:, s], cache(io["cache_diff_v"])).then_inc(vc_in[s], 16)

        @block.gpsimd
        def _(pool):
            with pool.Fori(0, 2) as i:
                for c in range(3):
                    for p in range(4):
                        wts.split_lo(pool, i * 4 + N0 + c, p)
                for p in range(4):
                    wts.split_lo(pool, i * 4 + N0 + 3, p)

        @block.scalar
        def _(act):
            act.wait_ge(lam_sum, 1)
            act.activation(lam[:, 2:4], lam[:, 0:2], ACT.Exp).then_inc(lam_exp, 1)
            with act.Fori(0, 2) as i:
                n = lambda c: i * 4 + N0 + c

                def hi(c, p):
                    if p in (0, 2):
                        free = (wts.used[p], n(c))
                    elif p == 1 and c > 0:
                        free = (wts.used[1], i * 3 + USED1 + c)
                    else:
                        free = (pj_done, i * (G * NT) + c * NT + 1)
                    wts.split_hi(act, n(c), p, free)

                def take(g, dst, squares):
                    for t in range(NT):
                        act.wait_ge(pj_done, i * (G * NT) + g * NT + t + 1 + 1)
                        if squares:
                            act.wait_ge(reduced, i * NJ + max(g * NT + t - 3, 0) + 1)
                            act.activation(Pr[:, (g * NT + t) % 4], pj[t][:], ACT.Square).then_inc(squared, 1)
                        act.activation(dst[:, t], pj[t][:], ACT.Copy).then_inc(pj_free[t], 1)

                def root(k):
                    act.wait_ge(var_done, i * 4 + k + 1)
                    w = slice(0, NT * 8) if k < 2 else slice(0, NP_T * HH) if k == 2 else slice(NP_T * HH, NT * HH)
                    act.activation(st[:, 2, w], st[:, 1, w], ACT.Sqrt).then_inc(std_done, 1)

                def take_T(a):
                    for t in range(NT):
                        job = a * NT + t
                        act.wait_ge(qkT_done, i * NJ + job + 1)
                        act.activation((qT, kT)[a][:, :, t * P:(t + 1) * P],
                                       B[5 + job % 3][:].rearrange("p (h c) -> p h c", c=P), ACT.Copy).then_inc(qkT_taken, 1)

                def send_rows(name, rows, out):
                    flat = lambda ap: ap.rearrange("l h d -> l (h d)")[:, bass.ds(i * W, W)]
                    act.dma_start(flat(io[f"o_{name}_p"][0, 0]).rearrange("(t p) c -> p t c", p=P), rows[:, 0:NP_T]).then_inc(out, 16)
                    act.dma_start(flat(io[f"o_{name}_s"][0].rearrange("b l h d -> (b l) h d")), rows[:, NP_T]).then_inc(out, 16)

                for p in range(4):
                    hi(0, p)
                for p in range(3):
                    hi(1, p)
                take(0, stage, True)
                hi(1, 3)
                root(0)
                hi(2, 0)
                hi(2, 1)
                take_T(0)
                hi(2, 2)
                take(1, stage, True)
                hi(2, 3)
                root(1)
                hi(3, 0)
                hi(3, 1)
                take_T(1)
                send_rows("k", stage, krow_out)
                hi(3, 2)
                act.wait_ge(vrow_out, i * 32 + 1)
                take(2, v, False)
                for t in range(NT):
                    act.wait_ge(pj_free[t], i * G + 3 + 1)
                send_rows("v", v, vrow_out)
                hi(3, 3)

                def exps(u):
                    s = u % 2
                    act.wait_ge(nmax_done, i * U + u + 1)
                    slot_wait(act, at_done, i, U, u)
                    nk = (u // HH + 1) * P
                    for m in range(2):
                        last = act.activation(Pr[:, 2 * s + m, 0:nk], B[2 * s + m][:, 0:nk], ACT.Exp, scale=SCALE,
                                              bias=sm[:, s, 2 + m:3 + m], accum_out=sm[:, s, 4 + m:5 + m])
                    last.then_inc(exp_done, 1)

                def copy_AT(u):
                    s, blocks = u % 2, u // HH + 1
                    act.wait_ge(at_done, i * U + u + 1 + 1)
                    slot_wait(act, pv_done, i, U, u)
                    act.activation(AT[:, s, 0:blocks].rearrange("p b c -> p (b c)"), B[4 + s][:, 0:blocks * P], ACT.Copy).then_inc(at_taken, 1)

                def take_o(t):
                    act.wait_ge(pv_done, i * U + HH * (t + 1) + 1)
                    act.wait_ge(krow_out, i * 32 + 32)
                    act.activation(stage[:, t], B[6 + t % 2][:], ACT.Copy).then_inc(o_taken, 1)

                for u in range(U + 3):
                    if u < U:
                        exps(u)
                    if 2 <= u < U + 2:
                        copy_AT(u - 2)
                    if u >= HH + 2 and (u - 3) % HH == HH - 1:
                        take_o((u - 3) // HH)

                def sq_o(t):
                    act.wait_ge(o_taken, i * NT + t + 1)
                    act.wait_ge(osq, i * NT + t + 1)
                    act.wait_ge(A_done, i * U + U)
                    act.activation(Pr[:, t % 4], stage[:, t], ACT.Square).then_inc(osq, 1)

                for b in range(DEC_B):
                    s = b % 2
                    for k in range(2):
                        act.wait_ge(kcT_done, (i * DEC_B + b) * 2 + k + 1 + 1)
                        act.wait_ge(ss_done, i * DEC_B + b + 1)
                        act.activation(kcT[:, :, k * P:(k + 1) * P], B[k][:].rearrange("p (h c) -> p h c", c=P), ACT.Copy) \
                           .then_inc(kcT_taken, 1)
                    act.wait_ge(snmax_done, i * DEC_B + b + 1)
                    slot_wait(act, sat_done, i, DEC_B, b)
                    act.activation(Ps[:, s], B[2 + s][:, 0:KEYS], ACT.Exp, scale=SCALE, bias=sms[:, s, 1:2],
                                   accum_out=sms[:, s, 2:3]).then_inc(sexp_done, 1)
                    if b == 2:
                        for t in range(NP_T):
                            sq_o(t)
                    if b == 3:
                        root(2)
                act.wait_ge(o4_done, i + 1)
                act.activation(stage[:, NP_T], B[7][:], ACT.Copy).then_inc(o_taken, 1)
                sq_o(NP_T)
                root(3)
                for t in range(NT):
                    act.wait_ge(ot_done, i * NT + t + 1)
                    act.activation(oT_hi[:, :, t * P:(t + 1) * P], B[5 + t % 3][:].rearrange("p (h c) -> p h c", c=P),
                                   ACT.Copy).then_inc(ot_hi, 1)
            act.wait_ge(krow_out, 64)
            act.wait_ge(vrow_out, 64 + 1)

        @block.vector
        def _(dve):
            dve.memset(K.acc_diff[:], 0.0).then_inc(acc_zero, 1)
            dve.wait_ge(const_in, 11 * 16)
            first = Links(dve, link)
            for a in range(2):
                for m in range(2):
                    for e in range(2):
                        h32 = slice(e * 32, (e + 1) * 32)
                        first(dve.tensor_tensor(tabs[:, a, :, m, h32], rope[:, :, m],
                                                bc(gains[:, a, h32].unsqueeze(1), [P, NT, 32]), ALU.mult))
            first(dve.tensor_scalar(gsub[:], gsub[:], 1.0 - LAM_INIT, None, ALU.mult))
            for a in range(2):
                first(dve.tensor_tensor(lv[:, 2 * a], lv[:, 2 * a], lv[:, 2 * a + 1], ALU.mult))
            first.sync()
            for a in range(2):
                last = dve.tensor_reduce(lam[:, a:a + 1], lv[:, 2 * a], AX, ALU.add)
            last.then_inc(lam_sum, 1)
            dve.wait_ge(lam_exp, 1)
            first(dve.tensor_tensor(lam[:, 4:5], lam[:, 3:4], lam[:, 2:3], ALU.subtract))
            first.sync()
            first(dve.tensor_scalar(lam[:, 4:5], lam[:, 4:5], LAM_INIT, None, ALU.subtract))
            first.sync()
            first(dve.tensor_scalar(lam[:, 7:8], lam[:, 4:5], -1.0, 1.0, ALU.mult, ALU.add))
            first.sync()
            first(dve.tensor_tensor(lam[:, 7:8], lam[:, 7:8], lam[:, 5:6], ALU.mult))
            first.sync()
            first(dve.tensor_tensor(lam[:, 6:7], lam[:, 7:8], lam[:, 4:5], ALU.add))
            first.sync()
            with dve.Fori(0, 2) as i:
                links = Links(dve, link, i * NLINK + first.n)

                def head_norm(a):
                    for t in range(NT):
                        dve.wait_ge(squared, i * NJ + a * NT + t + 1)
                        dve.tensor_reduce(st[:, 0, t * 8:(t + 1) * 8], Pr[:, (a * NT + t) % 4].rearrange("p (g c) -> p g c", c=DDH),
                                          AX, ALU.add).then_inc(reduced, 1)
                    dve.wait_ge(reduced, i * NJ + a * NT + NT + 1)
                    dve.tensor_scalar(st[:, 1], st[:, 0], 1.0 / DDH, EPS, ALU.mult, ALU.add).then_inc(var_done, 1)
                    dve.wait_ge(std_done, i * 4 + a + 1)
                    rsqrt_steps(dve, links, st[:, 3], st[:, 1], st[:, 2], st[:, 4])
                    for t in range(NT):
                        pj_taken(dve, a, t)
                        x = stage[:, t].rearrange("p (g c) -> p g c", c=DDH)
                        xx = stage[:, t].rearrange("p (g e c) -> p g e c", e=2, c=32)
                        t1, t2 = (tmp[:, m].rearrange("p (g e c) -> p g e c", e=2, c=32) for m in range(2))
                        dve.wait_ge(roped, i * NJ + a * NT + t + 1)
                        for m in range(2):
                            links(dve.tensor_tensor(tmp[:, m].rearrange("p (g c) -> p g c", c=DDH), x,
                                                    bc(tabs[:, a, t, m].unsqueeze(1), [P, 8, DDH]), ALU.mult))
                        links.sync()
                        dve.tensor_tensor(xx[:, :, 0], t1[:, :, 0], t2[:, :, 1], ALU.subtract)
                        links(dve.tensor_tensor(xx[:, :, 1], t1[:, :, 1], t2[:, :, 0], ALU.add))
                        links.sync()
                        dve.tensor_tensor(x, x, bc(st[:, 3, t * 8:(t + 1) * 8].unsqueeze(2), [P, 8, DDH]), ALU.mult).then_inc(roped, 1)

                def pj_taken(eng, g, t):
                    eng.wait_ge(pj_free[t], i * G + g + 1 + 1)

                def block_q(b):
                    for m in range(2):
                        rows = slice(m * DDH, (m + 1) * DDH)
                        dst = qB[rows, b % 2].rearrange("p h c -> p (h c)")
                        dst = bass.AP(tensor=dst.tensor, offset=dst.offset + m * DEC_L,
                                      ap=[list(dst.ap[0]), [P + 2 * DEC_L, HH], [1, DEC_L]])
                        dve.tensor_copy(dst, qT[rows, :, SEQ + b * DEC_L:SEQ + (b + 1) * DEC_L]).then_inc(qB_done, 1)

                head_norm(0)
                head_norm(1)
                dve.wait_ge(roped, i * NJ + NJ + 1)
                dve.memset(qB[:], 0.0).then_inc(qB_zero, 1)
                dve.wait_ge(qB_zero, i + 1)
                dve.wait_ge(qkT_taken, i * NJ + NT)
                block_q(0)
                block_q(1)

                def maxima(u):
                    s, nk = u % 2, (u // HH + 1) * P
                    dve.wait_ge(s_done, i * U + u + 1)
                    for m in range(2):
                        ins = dve.tensor_reduce(sm[:, s, m:m + 1], B[2 * s + m][:, 0:nk], AX, ALU.max)
                    links(ins)
                    links.sync()
                    dve.tensor_scalar(sm[:, s, 2:4], sm[:, s, 0:2], -SCALE, None, ALU.mult).then_inc(nmax_done, 1)

                def combine(u):
                    s, nk = u % 2, (u // HH + 1) * P
                    dve.wait_ge(exp_done, i * U + u + 1)
                    links(dve.reciprocal(sm[:, s, 6:8], sm[:, s, 4:6]))
                    links.sync()
                    links(dve.tensor_tensor(sm[:, s, 7:8], sm[:, s, 7:8], lam[:, 4:5], ALU.mult))
                    a, b = Pr[:, 2 * s, 0:nk], Pr[:, 2 * s + 1, 0:nk]
                    links(dve.tensor_scalar(a, a, sm[:, s, 6:7], None, ALU.mult))
                    links.sync()
                    dve.scalar_tensor_tensor(a, b, sm[:, s, 7:8], a, ALU.mult, ALU.add).then_inc(A_done, 1)

                for u in range(U + 1):
                    if u < U:
                        maxima(u)
                    if u >= 1:
                        combine(u - 1)

                def sub_roots(ts, k):
                    for t in ts:
                        dve.wait_ge(osq, i * NT + t + 1 + 1)
                        links(dve.tensor_reduce(st[:, 0, t * HH:(t + 1) * HH], Pr[:, t % 4].rearrange("p (g c) -> p g c", c=DDV),
                                                AX, ALU.add))
                    links.sync()
                    w = slice(ts[0] * HH, (ts[-1] + 1) * HH)
                    dve.tensor_scalar(st[:, 1, w], st[:, 0, w], 1.0 / DDV, EPS, ALU.mult, ALU.add).then_inc(var_done, 1)

                def sub_norm(ts, k):
                    w = slice(ts[0] * HH, (ts[-1] + 1) * HH)
                    if ts[0] == 0 or ts[0] == NP_T:
                        w = slice(0, NP_T * HH) if ts[0] == 0 else w
                        dve.wait_ge(std_done, i * 4 + k + 1)
                        rsqrt_steps(dve, links, st[:, 3, w], st[:, 1, w], st[:, 2, w], st[:, 4, w])
                    for t in ts:
                        x = stage[:, t].rearrange("p (g c) -> p g c", c=DDV)
                        links(dve.tensor_tensor(x, x, bc(st[:, 3, t * HH:(t + 1) * HH].unsqueeze(2), [P, HH, DDV]), ALU.mult))
                        links.sync()
                        dve.tensor_tensor(x, x, bc(gsub[:].unsqueeze(1), [P, HH, DDV]), ALU.mult).then_inc(dn_done, 1)

                def s_maxima(b):
                    s = b % 2
                    dve.wait_ge(ss_done, i * DEC_B + b + 1 + 1)
                    links(dve.tensor_reduce(sms[:, s, 0:1], B[2 + s][:, 0:KEYS], AX, ALU.max))
                    links.sync()
                    dve.tensor_scalar(sms[:, s, 1:2], sms[:, s, 0:1], -SCALE, None, ALU.mult).then_inc(snmax_done, 1)

                def s_scale(b):
                    s = b % 2
                    dve.wait_ge(sexp_done, i * DEC_B + b + 1)
                    links(dve.reciprocal(sms[:, s, 3:4], sms[:, s, 2:3]))
                    links.sync()
                    links(dve.tensor_tensor(sms[:, s, 3:4], sms[:, s, 3:4], lam[:, 6:7], ALU.mult))
                    links.sync()
                    dve.tensor_scalar(Ps[:, s], Ps[:, s], sms[:, s, 3:4], None, ALU.mult).then_inc(sA_done, 1)

                def s_fold(b):
                    s = b % 2
                    dve.wait_ge(sat_done, i * DEC_B + b + 1 + 1)
                    slot_wait(dve, spv_done, i, DEC_B, b)
                    dve.tensor_reduce(ATs[:, s], B[4 + s][:, 0:3 * P].rearrange("p (g m l) -> p g l m", m=2, l=DEC_L), AX, ALU.add) \
                       .then_inc(sat_taken, 1)

                for b in range(DEC_B + 1):
                    if b < DEC_B:
                        s_maxima(b)
                        if b + 2 < DEC_B:
                            block_q(b + 2)
                    if b >= 1:
                        s_fold(b - 1)
                    if b < DEC_B:
                        s_scale(b)
                    if b == 3:
                        sub_roots(list(range(NP_T)), 2)
                    if 4 <= b < 4 + NP_T:
                        sub_norm([b - 4], 2)
                dve.wait_ge(spv_done, i * DEC_B + DEC_B + 1)
                dve.tensor_copy(oTs[:], B[6][:]).then_inc(oTs_done, 1)
                sub_roots([NP_T], 3)
                sub_norm([NP_T], 3)
                for t in range(NT):
                    dve.wait_ge(ot_hi, i * NT + t + 1)
                    sl = (slice(None), slice(None), slice(t * P, (t + 1) * P))
                    dve.tensor_tensor(oT_lo[sl], B[5 + t % 3][:].rearrange("p (h c) -> p h c", c=P),
                                      oT_hi[sl].bitcast(F32), ALU.subtract).then_inc(ot_lo, 1)
                dve.wait_ge(acc_zero, 1)
                for j in range(2):
                    for t in range(NT):
                        dve.wait_ge(pj_done, i * (G * NT) + (3 + j) * NT + t + 1 + 1)
                        a = K.acc_diff[:, t, j * W:(j + 1) * W]
                        dve.tensor_tensor(a, a, pj[t][:], ALU.add).then_inc(pj_free[t], 1)
                assert links.n == NLINK, (links.n, NLINK)

        @block.tensor
        def _(pe):
            pe.wait_ge(const_in, 11 * 16)
            with pe.Fori(0, 2) as i:
                n = lambda c: i * 4 + N0 + c
                group = lambda g: i * G + g
                hT = (K.hT_hi, K.hT_lo)

                def transpose_rows(a):
                    for t in range(NT):
                        job = a * NT + t
                        pe.wait_ge(roped, i * NJ + job + 1 + 1)
                        if job >= 3:
                            pe.wait_ge(qkT_taken, i * NJ + job - 2)
                        for h in range(HH):
                            last = pe.transpose(B[5 + job % 3][:, h * P:(h + 1) * P], stage[:, t, h * P:(h + 1) * P], K.ident[:])
                        last.then_inc(qkT_done, 1)

                project(pe, wts, n(0), pj, *hT, pj_free, group(0), pj_done)
                project(pe, wts, n(1), pj, *hT, pj_free, group(1), pj_done, between=lambda: transpose_rows(0))
                project(pe, wts, n(2), pj, *hT, pj_free, group(2), pj_done, between=lambda: transpose_rows(1))

                def scores(u):
                    s, t, h = u % 2, u // HH, u % HH
                    nk = (t + 1) * P
                    if u < 2:
                        for b in (2 * u, 2 * u + 1):
                            pe.wait_ge(pj_free[b], i * G + 3 + 1)
                    else:
                        pe.wait_ge(exp_done, i * U + u - 1)
                    for m in range(2):
                        rows = slice(m * DDH, (m + 1) * DDH)
                        pe.matmul(B[2 * s + m][:, 0:nk], qT[rows, h, t * P:(t + 1) * P], kT[rows, h, 0:nk], start=True, stop=False)
                        last = pe.matmul(B[2 * s + m][:, nk - CHUNK:nk], mp[rows, 0:P], mp[rows, P:P + CHUNK], start=False, stop=True)
                    last.then_inc(s_done, 1)

                def turn(u):
                    s, t = u % 2, u // HH
                    pe.wait_ge(A_done, i * U + u + 1)
                    if u < 2:
                        pe.wait_ge(pj_free[NP_T], i * G + 3 + 1)
                    else:
                        pe.wait_ge(at_taken, i * U + u - 1)
                    for j in range(t + 1):
                        last = pe.transpose(B[4 + s][:, j * P:(j + 1) * P], Pr[:, 2 * s, j * P:(j + 1) * P], K.ident[:])
                    last.then_inc(at_done, 1)

                def values(u):
                    s, t, h = u % 2, u // HH, u % HH
                    pe.wait_ge(at_taken, i * U + u + 1)
                    if h == 0 and t >= 2:
                        pe.wait_ge(o_taken, i * NT + t - 1)
                    for j in range(t + 1):
                        last = pe.matmul(B[6 + t % 2][:, h * P:(h + 1) * P], AT[:, s, j], v[:, j, h * P:(h + 1) * P],
                                         start=(j == 0), stop=(j == t))
                    last.then_inc(pv_done, 1)

                pe.wait_ge(qkT_taken, i * NJ + NJ)
                for u in range(U + 3):
                    if u < U:
                        scores(u)
                    if 2 <= u < U + 2:
                        turn(u - 2)
                    if u >= 3:
                        values(u - 3)

                def s_scores(b):
                    s = b % 2
                    pe.wait_ge(kc_in[s], i * (DEC_B // 2 * 16) + (b // 2 + 1) * 16)
                    if b == 0:
                        pe.wait_ge(exp_done, i * U + U)
                    pe.wait_ge(kcT_taken, (i * DEC_B + b) * 2 + 1)
                    for k in range(2):
                        for h in range(HH):
                            last = pe.transpose(B[k][:, h * P:(h + 1) * P], kc[:, s, k, h * P:(h + 1) * P], K.ident[:])
                        last.then_inc(kcT_done, 1)
                    pe.wait_ge(qB_done, (i * DEC_B + b) * 2 + 2)
                    pe.wait_ge(kcT_taken, (i * DEC_B + b) * 2 + 2 + 1)
                    if b >= 2:
                        pe.wait_ge(sexp_done, i * DEC_B + b - 1)
                    out = B[2 + s]
                    for h in range(HH):
                        pe.matmul(out[:, 0:PAST], qB[:, s, h], kcT[:, h], start=(h == 0), stop=False)
                        pe.matmul(out[:, PAST:KEYS], qB[:, s, h], kT[:, h, SEQ:SEQ + P], start=False, stop=False)
                    pe.matmul(out[:, PAST:KEYS], ms[:, 0:P], ms[:, P + b * P:P + (b + 1) * P], start=False, stop=True).then_inc(ss_done, 1)

                def s_values(b):
                    s = b % 2
                    pe.wait_ge(sA_done, i * DEC_B + b + 1)
                    if b >= 2:
                        pe.wait_ge(sat_taken, i * DEC_B + b - 1)
                    else:
                        pe.wait_ge(at_taken, i * U + U)
                    for j in range(3):
                        last = pe.transpose(B[4 + s][:, j * P:(j + 1) * P], Ps[:, s, j * P:(j + 1) * P], K.ident[:])
                    last.then_inc(sat_done, 1)
                    pe.wait_ge(vc_in[s], i * (DEC_B // 2 * 16) + (b // 2 + 1) * 16)
                    pe.wait_ge(sat_taken, i * DEC_B + b + 1)
                    if b == 0:
                        pe.wait_ge(o_taken, i * NT + NP_T)
                    for h in range(HH):
                        cols = slice(h * P + b * DEC_L, h * P + (b + 1) * DEC_L)
                        for j in range(3):
                            val = vc[:, s, j, h * P:(h + 1) * P] if j < 2 else v[:, NP_T, h * P:(h + 1) * P]
                            last = pe.matmul(B[6][:, cols], val, ATs[:, s, j * HH + h], start=(j == 0), stop=(j == 2))
                    last.then_inc(spv_done, 1)

                for b in range(DEC_B + 1):
                    if b < DEC_B:
                        s_scores(b)
                    if b >= 1:
                        s_values(b - 1)
                pe.wait_ge(oTs_done, i + 1)
                for h in range(HH):
                    last = pe.transpose(B[7][:, h * P:(h + 1) * P], oTs[:, h * P:(h + 1) * P], K.ident[:])
                last.then_inc(o4_done, 1)
                for t in range(NT):
                    pe.wait_ge(dn_done, i * NT + t + 1)
                    if t == 2:
                        pe.wait_ge(o_taken, i * NT + NT)
                    if t >= 3:
                        pe.wait_ge(ot_lo, i * NT + t - 2)
                    for h in range(HH):
                        last = pe.transpose(B[5 + t % 3][:, h * P:(h + 1) * P], stage[:, t, h * P:(h + 1) * P], K.ident[:])
                    last.then_inc(ot_done, 1)
                branch(pe, wts, n(3), pj, oT_hi, oT_lo, lambda t: pe.wait_ge(ot_lo, i * NT + t + 1), pj_free, group(3), pj_done)


def phase_g(nc, io, K):
    wts = K.wts
    N0, USED1 = 36, 30
    NE, NG, EG = N_EXP, 4, 4
    NB_T = 2 * NT
    with ExitStack() as ctx:
        sem = lambda name: K.semaphore("g_" + name)
        many = lambda name, n: [sem(f"{name}{i}") for i in range(n)]
        sb = Map(nc, K.phase_base, K.sbuf_end)
        acc_ret = sb("g_acc_ret", [P, NT, D_MODEL], F32)
        h2T = sb("g_h2T", [P, KT, NT * P], F32, at=K.phase_base)
        K.h2_at = sb.at
        K.h2 = sb("g_h2", [P, NT, D_MODEL], F32)
        K.x1 = sb("g_x1", [P, NT, D_MODEL], F32)
        K.pos = sb("g_pos", [P, 2, NT], F32)
        K.eid = sb("g_eid", [P, 2, NT], F32)
        K.wgt = sb("g_wgt", [P, 2, NT], F32)
        K.rounds = sb("g_rounds", [P, 4], I32)
        K.after_g = sb.at
        sg = sb("g_sg", [P, NT, W], F32)
        mods = sb("g_mods", [P, 2, 3, D_MODEL], F32)
        wr = sb("g_wr", [P, KT, 20], F32)
        br = sb("g_br", [P, 20], F32)
        tri = sb("g_tri", [P, 2 * P], F32)
        rk = sb("g_rk", [P, 24], F32)
        L = sb("g_L", [P, NT, 20], F32)
        s4 = sb("g_s4", [P, 8, NT, 4], F32)
        s1 = sb("g_s1", [P, 8, NT], F32)
        A = sb("g_A", [P, 4, NT, NE], F32)
        st = sb("g_st", [P, 5, 8], F32)
        B = [ctx.enter_context(nc.psum_tensor(f"g_B{i}", [P, W], F32)) for i in range(8)]
        pj = B[0:NT]
        acc_in, x_in, mods_in, small_in = map(sem, ("acc_in", "x_in", "mods_in", "small_in"))
        pj_done, pj_free, ret_gated, merged = sem("pj_done"), many("pj_free", NT), sem("ret_gated"), sem("merged")
        t_done, t_hi, t_taken, scaled, x1_done = map(sem, ("t_done", "t_hi", "t_taken", "scaled", "x1_done"))
        sumsq, var_done, std_done, h2_done, logits_done = map(sem, ("sumsq", "var_done", "std_done", "h2_done", "logits_done"))
        link, shifted, exp_done, assigned, pos_done, sg_free = map(sem, ("dve_link", "shifted", "exp_done", "assigned", "pos_done", "sg_free"))
        K.start_at_one(pj_done, *pj_free, sg_free)
        block = ctx.enter_context(nc.Block())
        w_in = io["w_in"][0]
        kind = lambda t: 0 if t < NP_T else 1
        half = lambda j: slice(j * W, (j + 1) * W)

        @block.sync
        def _(sp):
            sp.dma_start(acc_ret[:], io["acc_ret_d"]).then_inc(acc_in, 16)
            with sp.Fori(0, 2) as j:
                for c in range(2):
                    wts.load(sp, j * 2 + N0 + c, rows_of(w_in, j * W + COL_GATE + c * D_MODEL))
            sp.dma_start(K.x1[:, 0:NP_T], io["x_prompt"][0].rearrange("(t p) d -> p t d", p=P)).then_inc(x_in, 16)
            sp.dma_start(K.x1[:, NP_T], io["x_sample"].rearrange("b l d -> (b l) d")).then_inc(x_in, 16)
            for kd in range(2):
                sp.dma_start(mods[:, kd], io["mods"][kd, 0:3].rearrange("m p d -> p m d")).then_inc(mods_in, 16)
            for j in range(2):
                wts.load(sp, N0 + 4 + j, rows_of(io["w_out"][0], j * W))
            sp.dma_start(wr[:, :, 0:NG], io["w_group"][0].rearrange("(k p) n -> p k n", p=P)).then_inc(small_in, 16)
            sp.dma_start(wr[:, :, NG:20], io["w_expert_router"][0].rearrange("(k p) n -> p k n", p=P)).then_inc(small_in, 16)
            sp.dma_start(br[:, 0:NG], io["b_group"].broadcast_to([P, NG])).then_inc(small_in, 16)
            sp.dma_start(br[:, NG:20], io["b_expert"].broadcast_to([P, NE])).then_inc(small_in, 16)
            sp.dma_start(tri[:], io["tri"]).then_inc(small_in, 16)
            sp.dma_start(rk[:], io["ranks"].broadcast_to([P, 24])).then_inc(small_in, 16)

        @block.gpsimd
        def _(pool):
            with pool.Fori(0, 2) as j:
                for c in range(2):
                    for p in range(4):
                        wts.split_lo(pool, j * 2 + N0 + c, p)
            for c in range(4, 6):
                for p in range(4):
                    wts.split_lo(pool, N0 + c, p)

        @block.scalar
        def _(act):
            def hi(c, p):
                free = (pj_done, c * NT + 1) if p == 3 else (wts.used[p], c + (USED1 if p == 1 else N0))
                wts.split_hi(act, c + N0, p, free)

            with act.Fori(0, 2) as j:
                for c in range(2):
                    for p in range(4):
                        hi(j * 2 + c, p)
                    for t in range(NT):
                        act.wait_ge(pj_done, (j * 2 + c) * NT + t + 1 + 1)
                        act.wait_ge(sg_free, (j * 2 + c) * NT + 1)
                        act.activation(sg[:, t], pj[t][:], ACT.Sigmoid).then_inc(pj_free[t], 1)
            for c in range(4, 6):
                for p in range(4):
                    hi(c, p)
                if c == 4:
                    for q in range(NB_T):
                        act.wait_ge(t_done, q + 1)
                        s = (slice(None), slice(4 * (q % 2), 4 * (q % 2) + 4), slice(q // 2 * P, (q // 2 + 1) * P))
                        act.activation(K.hT_hi[s], B[5 + q % 3][:].rearrange("p (k c) -> p k c", c=P), ACT.Copy).then_inc(t_hi, 1)
            for t in range(NT):
                act.wait_ge(x1_done, 2 * NT)
                act.wait_ge(sumsq, t)
                act.activation(sg[:, 0:2].rearrange("p a c -> p (a c)"), K.x1[:, t], ACT.Square, accum_out=st[:, 0, t:t + 1]).then_inc(sumsq, 1)
            act.wait_ge(var_done, 1)
            act.activation(st[:, 2, 0:NT], st[:, 1, 0:NT], ACT.Sqrt).then_inc(std_done, 1)
            for q in range(NB_T):
                act.wait_ge(t_done, NB_T + q + 1)
                s = (slice(None), slice(4 * (q % 2), 4 * (q % 2) + 4), slice(q // 2 * P, (q // 2 + 1) * P))
                act.activation(h2T[s], B[5 + q % 3][:].rearrange("p (k c) -> p k c", c=P), ACT.Copy).then_inc(t_taken, 1)
            act.wait_ge(shifted, 1)
            act.activation(s4[:, 1], s4[:, 0], ACT.Exp).then_inc(exp_done, 1)
            act.wait_ge(shifted, 2)
            act.activation(s1[:, 5], s1[:, 4], ACT.Exp).then_inc(exp_done, 1)

        @block.vector
        def _(dve):
            links = Links(dve, link)

            def do(ins):
                links(ins)
                links.sync()

            dve.wait_ge(acc_in, 16)
            with dve.Fori(0, 2) as j:
                a_ret, a_diff = (lambda t: acc_ret[:, t, bass.ds(j * W, W)]), (lambda t: K.acc_diff[:, t, bass.ds(j * W, W)])
                for t in range(NT):
                    dve.wait_ge(pj_free[t], j * 2 + 1 + 1)
                    dve.tensor_tensor(a_ret(t), a_ret(t), sg[:, t], ALU.mult).then_inc(sg_free, 1)
                for t in range(NT):
                    dve.wait_ge(pj_free[t], j * 2 + 2 + 1)
                    dve.tensor_tensor(a_diff(t), a_diff(t), sg[:, t], ALU.mult).then_inc(sg_free, 1)
                for t in range(NT):
                    dve.wait_ge(sg_free, j * (2 * NT) + NT + t + 1 + 1)
                    dve.tensor_tensor(a_ret(t), a_ret(t), a_diff(t), ALU.add).then_inc(merged, 1)
            for q in range(NB_T):
                dve.wait_ge(t_hi, q + 1)
                s = (slice(None), slice(4 * (q % 2), 4 * (q % 2) + 4), slice(q // 2 * P, (q // 2 + 1) * P))
                dve.tensor_tensor(K.hT_lo[s], B[5 + q % 3][:].rearrange("p (k c) -> p k c", c=P), K.hT_hi[s].bitcast(F32),
                                  ALU.subtract).then_inc(t_taken, 1)
            dve.wait_ge(x_in, 32)
            dve.wait_ge(mods_in, 32)
            for j in range(2):
                for t in range(NT):
                    dve.wait_ge(pj_done, (4 + j) * NT + t + 1 + 1)
                    dve.tensor_tensor(sg[:, t], pj[t][:], mods[:, kind(t), 0, half(j)], ALU.mult).then_inc(pj_free[t], 1)
                for t in range(NT):
                    dve.wait_ge(pj_free[t], 5 + j + 1)
                    dve.tensor_tensor(K.x1[:, t, half(j)], K.x1[:, t, half(j)], sg[:, t], ALU.add).then_inc(x1_done, 1)
                if j == 0:
                    dve.wait_ge(x1_done, NT)
            dve.wait_ge(sumsq, NT)
            dve.tensor_scalar(st[:, 1, 0:NT], st[:, 0, 0:NT], 1.0 / D_MODEL, EPS, ALU.mult, ALU.add).then_inc(var_done, 1)
            dve.wait_ge(std_done, 1)
            rsqrt_steps(dve, links, st[:, 3, 0:NT], st[:, 1, 0:NT], st[:, 2, 0:NT], st[:, 4, 0:NT])
            for t in range(NT):
                links(dve.scalar_tensor_tensor(K.h2[:, t], K.x1[:, t], st[:, 3, t:t + 1], mods[:, kind(t), 2], ALU.mult, ALU.mult))
                links.sync()
                dve.tensor_tensor(K.h2[:, t], K.h2[:, t], mods[:, kind(t), 1], ALU.add).then_inc(h2_done, 1)
            dve.wait_ge(small_in, 6 * 16)
            dve.wait_ge(logits_done, 1)
            do(dve.tensor_tensor(L[:], B[0][:, 0:NT * 20].rearrange("p (t c) -> p t c", c=20), bc(br[:].unsqueeze(1), [P, NT, 20]), ALU.add))
            four = lambda x: bc(x.unsqueeze(2), [P, NT, 4])
            ranks = bc(rk[:, 0:4].unsqueeze(1), [P, NT, 4])

            def first_max(x, top, hot):
                do(dve.tensor_reduce(top, x, AX, ALU.max))
                do(dve.tensor_tensor(hot, x, four(top), ALU.is_equal))
                do(dve.tensor_tensor(hot, hot, ranks, ALU.mult))
                do(dve.tensor_reduce(s1[:, 7], hot, AX, ALU.max))
                do(dve.tensor_tensor(hot, hot, four(s1[:, 7]), ALU.is_equal))

            G4, E4, H1, H2, M4 = s4[:, 2], s4[:, 3], s4[:, 4], s4[:, 5], s4[:, 6]
            first_max(L[:, :, 0:NG], s1[:, 0], G4)
            dve.tensor_tensor(s4[:, 0], L[:, :, 0:NG], four(s1[:, 0]), ALU.subtract).then_inc(shifted, 1)
            Lg = L[:, :, NG:20].rearrange("p t (g c) -> p t g c", c=EG)
            for t in range(NT):
                links(dve.tensor_tensor(A[:, 3, t].rearrange("p (g c) -> p g c", c=EG), Lg[:, t], bc(G4[:, t].unsqueeze(2), [P, NG, EG]), ALU.mult))
            links.sync()
            do(dve.tensor_reduce(E4, A[:, 3].rearrange("p t (g c) -> p t c g", c=EG), AX, ALU.add))
            first_max(E4, s1[:, 1], H1)
            do(dve.tensor_scalar(M4, H1, NEG, None, ALU.mult))
            do(dve.tensor_tensor(M4, M4, E4, ALU.add))
            first_max(M4, s1[:, 2], H2)
            dve.tensor_tensor(s1[:, 4], s1[:, 2], s1[:, 1], ALU.subtract).then_inc(shifted, 1)
            for a, H in ((0, H1), (1, H2)):
                for t in range(NT):
                    links(dve.tensor_tensor(A[:, a, t].rearrange("p (g c) -> p g c", c=EG), bc(G4[:, t].unsqueeze(2), [P, NG, EG]),
                                            bc(H[:, t].unsqueeze(1), [P, NG, EG]), ALU.mult))
            links.sync()
            dve.tensor_tensor(A[:, 2], A[:, 0], A[:, 1], ALU.add).then_inc(assigned, 1)
            dve.wait_ge(exp_done, 2)
            do(dve.tensor_reduce(s1[:, 3], s4[:, 1], AX, ALU.add))
            do(dve.reciprocal(s1[:, 3], s1[:, 3]))
            do(dve.tensor_scalar(s1[:, 6], s1[:, 5], 1.0, None, ALU.add))
            do(dve.reciprocal(s1[:, 6], s1[:, 6]))
            do(dve.tensor_tensor(K.wgt[:, 0], s1[:, 6], s1[:, 3], ALU.mult))
            do(dve.tensor_tensor(K.wgt[:, 1], K.wgt[:, 0], s1[:, 5], ALU.mult))
            for a in range(2):
                nums = bc(rk[:, 4:20].unsqueeze(1), [P, NT, NE])
                do(dve.tensor_tensor(A[:, 3], A[:, a], nums, ALU.mult))
                do(dve.tensor_reduce(K.eid[:, a], A[:, 3], AX, ALU.add))
            dve.wait_ge(pos_done, 1)
            for a in range(2):
                do(dve.tensor_tensor(A[:, 3], A[:, a], B[1][:, 0:NT * NE].rearrange("p (t e) -> p t e", e=NE), ALU.mult))
                do(dve.tensor_reduce(K.pos[:, a], A[:, 3], AX, ALU.add))
            do(dve.tensor_reduce(s1[:, 0, 0:1], B[1][:, NT * NE:(NT + 1) * NE], AX, ALU.max))
            do(dve.tensor_tensor(s4[:, 0, 0], bc(s1[:, 0, 0:1], [P, 4]), rk[:, 20:24], ALU.is_gt))
            do(dve.tensor_reduce(s1[:, 0, 1:2], s4[:, 0, 0], AX, ALU.add))
            do(dve.tensor_scalar(K.rounds[:, 0:1], s1[:, 0, 1:2], 1.0, None, ALU.add))

        @block.tensor
        def _(pe):
            hT = (K.hT_hi, K.hT_lo)
            with pe.Fori(0, 2) as j:
                for c in range(2):
                    project(pe, wts, j * 2 + N0 + c, pj, *hT, pj_free, j * 2 + c, pj_done)

            def turn(src, ready, q0):
                for q in range(NB_T):
                    t = q // 2
                    ready(t)
                    if q0 + q >= 3:
                        pe.wait_ge(t_taken, q0 + q - 2)
                    for a in range(4):
                        k = 4 * (q % 2) + a
                        last = pe.transpose(B[5 + q % 3][:, a * P:(a + 1) * P], src[:, t, k * P:(k + 1) * P], K.ident[:])
                    last.then_inc(t_done, 1)

            turn(acc_ret, lambda t: pe.wait_ge(merged, NT + t + 1), 0)
            pe.wait_ge(t_taken, NB_T)
            for j in range(2):
                project(pe, wts, N0 + 4 + j, pj, *hT, pj_free, 4 + j, pj_done)
            turn(K.h2, lambda t: pe.wait_ge(h2_done, t + 1), NB_T)
            pe.wait_ge(t_taken, 2 * NB_T)
            pe.wait_ge(small_in, 6 * 16)
            for t in range(NT):
                pe.wait_ge(pj_free[0], 6 + 1)
                for k in range(KT):
                    last = pe.matmul(B[0][:, t * 20:(t + 1) * 20], h2T[:, k, t * P:(t + 1) * P], wr[:, k], start=(k == 0), stop=(k == KT - 1))
            last.then_inc(logits_done, 1)
            pe.wait_ge(assigned, 1)
            pe.wait_ge(pj_free[1], 6 + 1)
            for t in range(NT + 1):
                out = B[1][:, t * NE:(t + 1) * NE]
                for s in range(min(t, NT - 1) + 1):
                    last = pe.matmul(out, tri[:, 0:P] if s == t else tri[:, P:2 * P], A[:, 2, s], start=(s == 0), stop=(s == min(t, NT - 1)))
            last.then_inc(pos_done, 1)


def phase_m(nc, io, K):
    wts = K.wts
    N0, USED1 = 42, 36
    NE = N_EXP
    BIG = 1.0e6
    with ExitStack() as ctx:
        sem = lambda name: K.semaphore("m_" + name)
        sb = Map(nc, K.hT_at, K.phase_base)
        yacc = sb("m_yacc", [P, NT, D_MODEL], F32)
        xT_hi = [sb("m_xT_hi", [P, KT, P], F32R)]
        xT_lo = [sb("m_xT_lo", [P, KT, P], F32R)]
        xe = sb("m_xe", [P, D_MODEL], F32)
        yst = sb("m_yst", [P, D_MODEL], F32)
        sb = Map(nc, K.after_g, K.sbuf_end)
        xT_hi.append(sb("m_xT_hi_odd", [P, KT, P], F32R))
        xT_lo.append(sb("m_xT_lo_odd", [P, KT, P], F32R))
        gt2 = sb("m_gt2", [P, 2, D_MODEL], F32)
        gx = sb("m_gx", [P, 2, D_MODEL], F32)
        raw_odd = sb("m_raw_odd", [P, 4, 2, W], F32)
        su = sb("m_su", [P, W], F32)
        aT_hi = sb("m_aT_hi", [P, 4, P], F32R)
        aT_lo = sb("m_aT_lo", [P, 4, P], F32R)
        idf = sb("m_idf", [P, 5, 2, NT], F32)
        idx = sb("m_idx", [P, 2, 2, NT], I32)
        wv = sb("m_wv", [P, 2, NT], F32)
        B = [ctx.enter_context(nc.psum_tensor(f"m_B{i}", [P, W], F32)) for i in range(8)]
        U, V, Y, T, AT = B[0], B[1], B[2:4], B[4:6], B[6]
        gt2_in, xe_in, y_out, out_sem, scat = map(sem, ("gt2_in", "xe_in", "y_out", "rows_out", "scattered"))
        gath = [sem(f"gathered{i}") for i in range(2)]
        odd_loaded = [sem(f"odd_loaded{p}") for p in range(4)]
        idx_done, used, added, go = sem("idx_done"), sem("gathers_used"), sem("added"), sem("pool_goes_on")
        t_done, t_hi, t_lo, u_done, v_done, su_done, a_done, at_done, at_hi, at_lo, y0_done, y1_done, y_taken = map(
            sem, ("t_done", "t_hi", "t_lo", "u_done", "v_done", "su_done", "a_done", "at_done", "at_hi", "at_lo",
                  "y0_done", "y1_done", "y_taken"))
        link, y_zero, fin = sem("dve_link"), sem("y_zero"), sem("fin")
        K.start_at_one(a_done, at_done, at_lo, used, su_done, t_lo, y0_done, y1_done, y_out, y_taken)
        block = ctx.enter_context(nc.Block())
        kind = lambda t: 0 if t < NP_T else 1
        w1 = io["w1"][0].rearrange("e r n -> (e r) n")
        w3 = io["w3"][0].rearrange("e r n -> (e r) n")
        w2 = io["w2"][0].rearrange("e r n -> (e r) n")
        rounds = lambda eng: eng.value_load(K.rounds[0:1, 0:1], min_val=1, max_val=5)

        def chunk(r, pair, i):
            loads = r * (3 * NE // 2) + pair * 3 + i // 2
            n = r * (3 * NE) + pair * 6 + i + N0
            return Chunk(n, raw_odd, odd_loaded, loads, 2) if i % 2 else Chunk(n, wts.raw, wts.loaded, loads + N0, 2)

        def w1_0(r):
            return chunk(r, 0, 0)

        def w3_at(r, pair, par):
            return chunk(r, pair, par * 3 + 1)

        def w1_next(r, pair, par):
            return chunk(r, pair, par * 3 + 2)

        def w2_at(r, pair, par, last):
            return chunk(r, pair, par * 3 + (2 if last else 3))

        def w3_next(r, pair, par):
            return chunk(r, pair, par * 3 + 4)

        def experts(eng, expert):
            with eng.Fori(0, NE // 2 - 1) as g:
                expert(g * 2, g, 0, 2)
                expert(g * 2 + 1, g, 1, 2)
            expert(NE - 2, NE // 2 - 1, 0, 1)
            expert(NE - 1, NE // 2 - 1, 1, 0)

        def rows_at(w, r0):
            return [w[bass.ds(r0 + p * 256, 256), :].rearrange("(k r) n -> r k n", k=2) for p in range(4)]

        @block.sync
        def _(sp):
            R = rounds(sp)
            for kd in range(2):
                sp.dma_start(gt2[:, kd], io["mods"][kd, 3]).then_inc(gt2_in, 16)
            with sp.Fori(0, R) as r:
                def expert(e, pair, par, more):
                    wts.load(sp, w3_at(r, pair, par), rows_at(w3, e * D_MODEL))
                    if more > 1:
                        sp.wait_ge(t_done, r * (2 * NE) + e * 2 + 4)
                        sp.dma_start(xe[:], io["xg"][bass.ds(e * P + 2 * P, P), :]).then_inc(xe_in, 16)
                    if more:
                        wts.load(sp, w1_next(r, pair, par), rows_at(w1, e * D_MODEL + D_MODEL))
                    wts.load(sp, w2_at(r, pair, par, not more), halves_of(w2, e * D_EXP))

                wts.load(sp, w1_0(r), rows_at(w1, 0))
                sp.wait_ge(scat, r * (2 * NT * 16) + 2 * NT * 16)
                sp.dma_start(xe[:], io["xg"][0:P, :]).then_inc(xe_in, 16)
                sp.wait_ge(t_done, r * (2 * NE) + 2)
                sp.dma_start(xe[:], io["xg"][P:2 * P, :]).then_inc(xe_in, 16)
                experts(sp, expert)
            sp.wait_ge(fin, NT)
            sp.dma_start(io["o_y_p"][0].rearrange("(t p) d -> p t d", p=P), yacc[:, 0:NP_T]).then_inc(out_sem, 16)
            sp.dma_start(io["o_y_s"].rearrange("b l d -> (b l) d"), yacc[:, NP_T]).then_inc(out_sem, 16)
            sp.wait_ge(out_sem, 32)

        @block.gpsimd
        def _(pool):
            R = rounds(pool)
            with pool.Fori(0, R) as r:
                pool.wait_ge(idx_done, r * 4 + 4)
                pool.sem_inc(go, 1)
                for a in range(2):
                    for t in range(NT):
                        pool.indirect_dma_start(
                            out=io["xg"][:, :], out_offset=bass.IndirectOffsetOnAxis(ap=idx[:, 0, a, t:t + 1], axis=0),
                            in_=K.h2[:, t], in_offset=None, bounds_check=NE * CAP - 1, oob_is_err=False).then_inc(scat, 16)
                pool.wait_ge(y_out, r * (NE * 16) + NE * 16 + 1)
                for a in range(2):
                    for t in range(NT):
                        q = a * NT + t
                        pool.wait_ge(used, r * (2 * NT) + max(q - 1, 0) + 1)
                        pool.sem_inc(go, 1)
                        pool.indirect_dma_start(
                            out=gx[:, q % 2], out_offset=None, in_=io["yg"][:, :],
                            in_offset=bass.IndirectOffsetOnAxis(ap=idx[:, 1, a, t:t + 1], axis=0),
                            bounds_check=NE * CAP - 1, oob_is_err=False).then_inc(gath[q % 2], 16)

        @block.scalar
        def _(act):
            R = rounds(act)
            with act.Fori(0, R) as r:
                def take_x(j, par, k):
                    act.wait_ge(t_done, r * (2 * NE) + j * 2 + k + 1)
                    act.activation(xT_hi[par][:, 4 * k:4 * k + 4], T[k][:].rearrange("p (k c) -> p k c", c=P), ACT.Copy).then_inc(t_hi, 1)

                def hi(n, p, free1, free3):
                    wts.split_hi(act, n, p, (wts.used[p], n.n) if p in (0, 2) else free1 if p == 1 else free3)

                def take_y(q, j):
                    act.wait_ge((y0_done, y1_done)[j], q + 2)
                    act.wait_ge(y_out, q * 16 + 1)
                    act.activation(yst[:, j * W:(j + 1) * W], Y[j][:], ACT.Copy).then_inc(y_taken, 1)

                def send_y(q, e):
                    act.wait_ge(y_taken, q * 2 + 2 + 1)
                    act.dma_start(io["yg"][bass.ds(e * P, P), :], yst[:]).then_inc(y_out, 16)

                def expert(e, pair, par, first=False, last=False):
                    q = r * NE + e
                    used1 = q * 2 + USED1
                    act.wait_ge(u_done, q + 1)
                    act.wait_ge(at_done, q + 1)
                    act.activation(su[:], U[:], ACT.Silu).then_inc(su_done, 1)
                    for p in range(4):
                        if not last and p < 2:
                            take_x(e + 1, 1 - par, p)
                        hi(w3_at(r, pair, par), p, (wts.used[1], used1 + 1) if first else (y0_done, q + 1),
                           (u_done, q + 1) if first else (y1_done, q + 1))
                        if not first and p in (1, 3):
                            take_y(q - 1, p // 2)
                    if not first:
                        send_y(q - 1, e - 1)
                    if not last:
                        for p in range(4):
                            hi(w1_next(r, pair, par), p, (wts.used[1], used1 + 2), (v_done, q + 1))
                    for p in range(4):
                        if p == 2:
                            act.wait_ge(at_done, q + 2)
                            act.activation(aT_hi[:], AT[:].rearrange("p (k c) -> p k c", c=P), ACT.Copy).then_inc(at_hi, 1)
                        hi(w2_at(r, pair, par, last), p, (wts.used[1], used1 + (2 if last else 3)),
                           (v_done, q + 1) if last else (u_done, q + 2))

                for p in range(4):
                    hi(w1_0(r), p, (y0_done, r * NE + 1), (y1_done, r * NE + 1))
                for k in range(2):
                    take_x(0, 0, k)
                expert(0, 0, 0, first=True)
                with act.Fori(0, NE // 2 - 1) as g:
                    expert(g * 2 + 1, g, 1)
                    expert(g * 2 + 2, g + 1, 0)
                expert(NE - 1, NE // 2 - 1, 1, last=True)
                for j in range(2):
                    take_y(r * NE + NE - 1, j)
                send_y(r * NE + NE - 1, NE - 1)

        @block.vector
        def _(dve):
            R = rounds(dve)
            dve.memset(yacc[:], 0.0).then_inc(y_zero, 1)
            with dve.Fori(0, R) as r:
                NL = 7
                links = Links(dve, link, r * NL)

                def do(ins):
                    links(ins)
                    links.sync()

                ok, slot, inside, g = idf[:, 0], idf[:, 1], idf[:, 2], idf[:, 3]
                do(dve.tensor_scalar(ok, K.pos[:], 0.0, None, ALU.is_ge))
                do(dve.tensor_scalar(inside, K.pos[:], float(CAP), None, ALU.is_lt))
                do(dve.tensor_tensor(ok, ok, inside, ALU.mult))
                do(dve.scalar_tensor_tensor(slot, K.eid[:], float(CAP), K.pos[:], ALU.mult, ALU.add))
                do(dve.tensor_tensor(g, slot, ok, ALU.mult))
                do(dve.tensor_scalar(inside, ok, -BIG, BIG, ALU.mult, ALU.add))
                do(dve.tensor_tensor(inside, inside, g, ALU.add))
                dve.tensor_copy(idx[:, 0], inside).then_inc(idx_done, 1)
                dve.tensor_copy(idx[:, 1], g).then_inc(idx_done, 1)
                dve.tensor_tensor(wv[:], K.wgt[:], ok, ALU.mult).then_inc(idx_done, 1)
                dve.tensor_scalar(K.pos[:], K.pos[:], float(CAP), None, ALU.subtract).then_inc(idx_done, 1)

                def take_x(j, par, k):
                    dve.wait_ge(t_hi, r * (2 * NE) + j * 2 + k + 1)
                    s = slice(4 * k, 4 * k + 4)
                    dve.tensor_tensor(xT_lo[par][:, s], T[k][:].rearrange("p (k c) -> p k c", c=P), xT_hi[par][:, s].bitcast(F32),
                                      ALU.subtract).then_inc(t_lo, 1)

                def expert(e, pair, par, more):
                    q = r * NE + e
                    for p in range(4):
                        if p == 3:
                            dve.wait_ge(su_done, q + 2)
                            dve.wait_ge(v_done, q + 1)
                            dve.tensor_tensor(su[:], su[:], V[:], ALU.mult).then_inc(a_done, 1)
                        if more:
                            wts.split_lo(dve, w1_next(r, pair, par), p)
                    for p in range(4):
                        if p == 2:
                            dve.wait_ge(at_hi, q + 1)
                            dve.tensor_tensor(aT_lo[:], AT[:].rearrange("p (k c) -> p k c", c=P), aT_hi[:].bitcast(F32), ALU.subtract) \
                               .then_inc(at_lo, 1)
                        wts.split_lo(dve, w2_at(r, pair, par, not more), p)
                    for p in range(4):
                        if more > 1 and p < 2:
                            take_x(e + 2, par, p)
                        if more:
                            wts.split_lo(dve, w3_next(r, pair, par), p)

                for p in range(4):
                    wts.split_lo(dve, w1_0(r), p)
                for j in range(2):
                    for k in range(2):
                        take_x(j, j, k)
                for p in range(4):
                    wts.split_lo(dve, w3_at(r, 0, 0), p)
                experts(dve, expert)
                dve.wait_ge(y_zero, 1)
                for a in range(2):
                    for t in range(NT):
                        j = a * NT + t
                        dve.wait_ge(gath[j % 2], r * (NT * 16) + (j // 2 + 1) * 16)
                        dve.wait_ge(used, r * (2 * NT) + max(j - NT + 1, 0) + 1)
                        dve.scalar_tensor_tensor(yacc[:, t], gx[:, j % 2], wv[:, a, t:t + 1], yacc[:, t], ALU.mult, ALU.add).then_inc(used, 1)
                dve.wait_ge(used, r * (2 * NT) + 2 * NT + 1)
                assert links.n == NL, links.n
            dve.wait_ge(gt2_in, 32)
            for t in range(NT):
                dve.tensor_tensor(yacc[:, t], yacc[:, t], gt2[:, kind(t)], ALU.mult).then_inc(added, 1)
                dve.wait_ge(added, t + 1)
                dve.tensor_tensor(yacc[:, t], yacc[:, t], K.x1[:, t], ALU.add).then_inc(fin, 1)

        @block.tensor
        def _(pe):
            R = rounds(pe)
            with pe.Fori(0, R) as r:
                def turn_x(j):
                    pe.wait_ge(xe_in, r * (NE * 16) + j * 16 + 16)
                    pe.wait_ge(t_lo, r * (2 * NE) + j * 2 + 1)
                    for k in range(2):
                        for a in range(4):
                            c = (4 * k + a) * P
                            last = pe.transpose(T[k][:, a * P:(a + 1) * P], xe[:, c:c + P], K.ident[:])
                        last.then_inc(t_done, 1)

                def up(n, out, par, done, between=None):
                    for p in range(4):
                        if p == 2 and between:
                            between()
                        pe.wait_ge(wts.lo_done[p], n.n + 1)
                        for kk in range(2):
                            k = 2 * p + kk
                            last = mm3(pe, out[:], xT_hi[par][:, k], xT_lo[par][:, k], wts.hi[:, p, kk], wts.lo[:, p, kk], k == 0, k == KT - 1)
                        last.then_inc(done if p == 3 else wts.used[p], 1)

                def expert(e, pair, par, more):
                    q = r * NE + e

                    def turn_a():
                        pe.wait_ge(a_done, q + 2)
                        pe.wait_ge(at_lo, q + 1)
                        for a in range(4):
                            last = pe.transpose(AT[:, a * P:(a + 1) * P], su[:, a * P:(a + 1) * P], K.ident[:])
                        last.then_inc(at_done, 1)

                    pe.wait_ge(a_done, q + 1)
                    up(w3_at(r, pair, par), V, par, v_done)
                    if more:
                        pe.wait_ge(su_done, q + 2)
                        pe.wait_ge(t_lo, r * (2 * NE) + e * 2 + 4 + 1)
                        up(w1_next(r, pair, par), U, 1 - par, u_done, turn_a)
                    else:
                        turn_a()
                    if more > 1:
                        turn_x(e + 2)
                    n = w2_at(r, pair, par, not more)
                    pe.wait_ge(at_lo, q + 1 + 1)
                    pe.wait_ge(y_taken, q * 2 + 1)
                    for j in range(2):
                        for p in (2 * j, 2 * j + 1):
                            pe.wait_ge(wts.lo_done[p], n.n + 1)
                            for kk in range(2):
                                k = 2 * (p % 2) + kk
                                last = mm3(pe, Y[j][:], aT_hi[:, k], aT_lo[:, k], wts.hi[:, p, kk], wts.lo[:, p, kk], k == 0, k == 3)
                            if p % 2 == 0:
                                last.then_inc(wts.used[p], 1)
                        last.then_inc((y0_done, y1_done)[j], 1)

                turn_x(0)
                turn_x(1)
                pe.wait_ge(su_done, r * NE + 1)
                up(w1_0(r), U, 0, u_done)
                experts(pe, expert)


def constants():
    f = np.float32
    out = {"ident": np.eye(P, dtype=f)}
    sel = np.zeros((19, 2, P), f)
    for t in range(P):
        sel[0, 0, t] = sel[9, 0, t] = sel[18, 0, t] = 1
        b = t // DEC_L
        sel[1 + b, 1, t] = sel[10 + b, 1, t] = sel[18, 1, t] = 1
    out["sel"] = sel
    pos = np.concatenate([np.arange(SEQ), np.tile(PAST + np.arange(DEC_L), DEC_B)]).astype(f)
    for name, d in (("rope_ret", RDK), ("rope_diff", DDH)):
        inv = (f(10000.0) ** (-np.arange(0, d, 2, dtype=f) / f(d))).astype(f)
        ang = (pos[:, None] * inv[None, :]).astype(f)
        tab = np.stack([np.cos(ang), np.sin(ang)], 1).astype(f)
        out[name] = np.ascontiguousarray(tab.reshape(NT, P, 2, d // 2).transpose(1, 0, 2, 3))
    tab = np.zeros((RH, P, T_RET), np.float64)
    m = np.arange(P)
    for h in range(RH):
        lg = np.log1p(-np.exp2(-5.0 - h))
        c = np.arange(SEQ)
        rel = c[None, :] - m[:, None]
        tab[h, :, T_DEC:T_DEC + SEQ] = np.where(rel >= 0, np.exp(np.maximum(rel, 0) * lg), 0) / 16
        rel = m[None, :] - m[:, None]
        same = (m[None, :] // DEC_L) == (m[:, None] // DEC_L)
        tab[h, :, T_SMP:T_SMP + P] = np.where(same & (rel >= 0), np.exp(np.maximum(rel, 0) * lg), 0) / 16
        for t in range(NP_T):
            tab[h, :, T_KDEC + t] = np.exp((SEQ - 1 - t * P - m) * lg) / 16
        for b in range(DEC_B):
            tab[h, :, T_KMASK + b] = np.where(m // DEC_L == b, np.exp((DEC_L - 1 - m % DEC_L) * lg), 0) / 16
        tab[h, :, T_QDEC:T_QDEC + P] = np.exp((m % DEC_L + 1) * lg)[None, :]
    out["tab_ret"] = tab.astype(f)
    out["g16"] = np.tile(np.exp(DEC_L * np.log1p(-np.exp2(-5.0 - np.arange(RH)))).astype(f), (P, 1))
    ind = np.zeros((P, P), f)
    ind[0, 0:CHUNK] = ind[CHUNK, 0:CHUNK] = 1
    neg = np.zeros((P, CHUNK), f)
    neg[0] = neg[CHUNK] = NEG
    out["mask_p"] = np.concatenate([ind, neg], 1)
    one = np.zeros((P, P + DEC_B * P), f)
    one[0, 0:P] = 1
    for b in range(DEC_B):
        one[0, P + b * P:P + (b + 1) * P] = np.where(m // DEC_L == b, 0, NEG)
    out["mask_s"] = one
    out["csign"] = np.where((m // DEC_L) % 2 == 0, 1, 0).astype(f)[:, None]
    tri = (m[:, None] < m[None, :]).astype(f)
    out["ranks"] = np.concatenate([[4, 3, 2, 1], np.arange(N_EXP), CAP * np.arange(1, 5)]).astype(f)[None]
    out["tri"] = np.concatenate([tri, np.ones((P, P), f)], 1)
    return out


def setup(nc):
    K = type("K", (), {})()
    K.sbuf_end = nc.sbuf_usable_end if not callable(nc.sbuf_usable_end) else nc.sbuf_usable_end()
    base = nc.sbuf_base if not callable(nc.sbuf_base) else nc.sbuf_base()
    sb = Map(nc, (base + 31) // 32 * 32, K.sbuf_end)
    return K, sb


def program(nc, io, stop=None):
    with ExitStack() as ctx:
        K, sb = setup(nc)

        def semaphore(name):
            K.taken.append(nc.alloc_semaphore(name))
            return K.taken[-1]

        def start_at_one(*sems):
            for s in sems:
                nc.gpsimd.sem_inc(s, 1)
            nc.all_engine_barrier()

        K.semaphore, K.start_at_one = semaphore, start_at_one
        K.ident = sb("ident", [P, P], F32)
        K.g16 = sb("g16", [P, RH], F32)
        K.wts = Weights(nc, ctx, sb)
        K.hT_at = sb.at
        K.hT_hi = sb("hT_hi", [P, KT, NT * P], F32R)
        K.hT_lo = sb("hT_lo", [P, KT, NT * P], F32R)
        K.phase_base = sb.at
        for name, phase in (("A", phase_a), ("R", phase_r), ("D", phase_d), ("G", phase_g), ("M", phase_m)):
            K.taken = []
            phase(nc, io, K)
            if stop == name:
                break
            if name != "M":
                nc.clear_and_free_semaphores(K.taken)
        return K


INPUTS = ["x_prompt", "x_sample", "c_prompt", "c_sample", "cache_diff_k", "cache_diff_v", "state_ret", "w_ada", "b_ada",
          "norm1_g", "w_in", "diff_qnorm_g", "diff_knorm_g", "diff_lambda_q1", "diff_lambda_k1", "diff_lambda_q2",
          "diff_lambda_k2", "diff_subln_g", "w_br_ret", "w_br_diff", "w_out", "norm2_g", "w_group", "b_group",
          "w_expert_router", "b_expert", "w1", "w3", "w2"]
OUTPUTS = {"o_y_p": (1, SEQ, D_MODEL), "o_y_s": (DEC_B, DEC_L, D_MODEL), "o_k_p": (1, 1, SEQ, DH, 2 * DDH),
           "o_v_p": (1, 1, SEQ, DH, DDV), "o_state_p": (1, 1, RH, RDK, RDV), "o_k_s": (1, DEC_B, DEC_L, DH, 2 * DDH),
           "o_v_s": (1, DEC_B, DEC_L, DH, DDV), "o_state_s": (1, DEC_B, RH, RDK, RDV)}
SCRATCH = {"mods": (2, 4, P, D_MODEL), "acc_ret_d": (P, NT, D_MODEL), "xg": (N_EXP * CAP, D_MODEL),
           "yg": (N_EXP * CAP, D_MODEL)}


def kernel(**inputs):
    import concourse.bacc as bacc
    from concourse.bass_utils import run_bass_kernel_spmd

    nc = bacc.Bacc("TRN2", target_bir_lowering=False, num_devices=1)
    arrays = {name: np.ascontiguousarray(inputs[name]) for name in INPUTS}
    arrays.update(constants())
    io = {name: nc.dram_tensor(name, a.shape, mybir.dt.from_np(a.dtype), kind="ExternalInput").ap() for name, a in arrays.items()}
    io.update({name: nc.dram_tensor(name, shape, F32, kind="ExternalOutput").ap() for name, shape in OUTPUTS.items()})
    io.update({name: nc.dram_tensor(name, shape, F32).ap() for name, shape in SCRATCH.items()})
    program(nc, io)
    got = run_bass_kernel_spmd(nc, [arrays], core_ids=[0]).results[0]
    return tuple(got[name] for name in OUTPUTS)
```
